# Optimizing a Trainium2 kernel written in Bass

```python
import jax, jax.numpy as jnp
from jax import lax
import numpy as np
import math
import jax
import jax.numpy as jnp

D_MODEL = 1024
BATCH = 1
SEQ = 512
DEPTH = 1

POOL_WINDOWS = (2, 4, 8, 16)
POOL_WIDTH = D_MODEL // 2
POOL_GROUP = POOL_WIDTH // len(POOL_WINDOWS)
HEAD_DIM = 64
N_HEADS = (D_MODEL // 2) // HEAD_DIM
N_KV_HEADS = 2
ATTN_WIDTH = N_HEADS * HEAD_DIM
KV_WIDTH = N_KV_HEADS * HEAD_DIM
WINDOW = 128
BLOCK = 128
ROPE_THETA = 500000.0
ROT_DIM = HEAD_DIM // 4
MIX_WIDTH = POOL_WIDTH + ATTN_WIDTH
IN_WIDTH = POOL_WIDTH + ATTN_WIDTH + 2 * KV_WIDTH
D_FF = 2816
EPS = 1e-6
NEG_INF = -1e30


def rms_norm(x, g):
    xf = x.astype(jnp.float32)
    y = xf * lax.rsqrt(jnp.mean(xf * xf, axis=-1, keepdims=True) + EPS)
    return (y * g.astype(jnp.float32)).astype(x.dtype)

def swiglu(h, w_gu, w_down):
    gate, up = jnp.split(h @ w_gu, 2, axis=-1)
    return (jax.nn.silu(gate) * up) @ w_down

def pool_mix(u, w_pool, pool_scale):
    B, S, C = u.shape
    uf = u.astype(jnp.float32)
    cs = jnp.concatenate([jnp.zeros((B, 1, C), jnp.float32), jnp.cumsum(uf, axis=1)], axis=1)
    t = jnp.arange(S)
    outs = []
    for g, w in enumerate(POOL_WINDOWS):
        lo, hi = g * POOL_GROUP, (g + 1) * POOL_GROUP
        start = jnp.maximum(t + 1 - w, 0)
        cnt = (t + 1 - start).astype(jnp.float32)
        csg = cs[:, :, lo:hi]
        mean = (csg[:, 1:] - csg[:, start]) / cnt[None, :, None]
        outs.append(mean - uf[:, :, lo:hi])
    d = jnp.stack(outs, axis=2).astype(u.dtype)
    y = jnp.einsum('bsgc,gcd->bsgd', d, w_pool).reshape(B, S, POOL_WIDTH)
    return y * pool_scale

def apply_partial_rope(x, cos, sin):
    half = ROT_DIM // 2
    x1, x2 = x[..., :half], x[..., half:ROT_DIM]
    rot = jnp.concatenate([x1 * cos - x2 * sin, x2 * cos + x1 * sin], axis=-1)
    return jnp.concatenate([rot, x[..., ROT_DIM:]], axis=-1)

def swa_with_sinks(q, k, v, sinks):
    B, S = q.shape[0], q.shape[1]
    nb = S // BLOCK
    G = N_HEADS // N_KV_HEADS
    qb = q.reshape(B, nb, BLOCK, N_KV_HEADS, G, HEAD_DIM)
    pad = ((0, 0), (BLOCK, 0), (0, 0), (0, 0))
    kp = jnp.pad(k, pad).reshape(B, nb + 1, BLOCK, N_KV_HEADS, HEAD_DIM)
    vp = jnp.pad(v, pad).reshape(B, nb + 1, BLOCK, N_KV_HEADS, HEAD_DIM)
    kb = jnp.concatenate([kp[:, :-1], kp[:, 1:]], axis=2)
    vb = jnp.concatenate([vp[:, :-1], vp[:, 1:]], axis=2)
    s = jnp.einsum('bnqkgd,bnjkd->bnkgqj', qb, kb,
                   preferred_element_type=jnp.float32) * (HEAD_DIM ** -0.5)
    qi = jnp.arange(BLOCK)[:, None]
    kj = jnp.arange(2 * BLOCK)[None, :]
    diff = qi + BLOCK - kj
    band = (diff >= 0) & (diff < WINDOW)
    key_abs = jnp.arange(nb)[:, None] * BLOCK - BLOCK + kj
    valid = band[None] & (key_abs >= 0)[:, None, :]
    s = jnp.where(valid[None, :, None, None], s, NEG_INF)
    sink = jnp.broadcast_to(sinks.astype(jnp.float32).reshape(1, 1, N_KV_HEADS, G, 1, 1),
                            s.shape[:-1] + (1,))
    p = jax.nn.softmax(jnp.concatenate([s, sink], axis=-1), axis=-1)[..., :-1]
    o = jnp.einsum('bnkgqj,bnjkd->bnqkgd', p.astype(v.dtype), vb)
    return o.reshape(B, S, ATTN_WIDTH)

def token_mixer(h, cos, sin, w_in, w_pool, pool_scale, sinks, g_pool, g_attn, w_out):
    B, S, _ = h.shape
    z = h @ w_in
    u = z[..., :POOL_WIDTH]
    q = z[..., POOL_WIDTH:MIX_WIDTH].reshape(B, S, N_HEADS, HEAD_DIM)
    k = z[..., MIX_WIDTH:MIX_WIDTH + KV_WIDTH].reshape(B, S, N_KV_HEADS, HEAD_DIM)
    v = z[..., MIX_WIDTH + KV_WIDTH:].reshape(B, S, N_KV_HEADS, HEAD_DIM)
    pool_out = pool_mix(u, w_pool, pool_scale)
    q = apply_partial_rope(q, cos, sin)
    k = apply_partial_rope(k, cos, sin)
    attn_out = swa_with_sinks(q, k, v, sinks)
    y = jnp.concatenate([rms_norm(pool_out, g_pool), rms_norm(attn_out, g_attn)], axis=-1)
    return y @ w_out

def first_inputs(seed: int = 0) -> dict:
    key = jax.random.key(seed)
    ks = jax.random.split(key, 24)
    f32 = jnp.float32

    def w(k, shape, fan_in):
        return jax.random.normal(k, shape, f32) * fan_in ** -0.5

    def gain(k, n):
        return 1.0 + 0.05 * jax.random.normal(k, (DEPTH, n), f32)

    x = jax.random.normal(ks[0], (BATCH, SEQ, D_MODEL), f32)
    offset = jax.random.randint(ks[1], (BATCH, 1), 0, 4096, jnp.int32)
    positions = offset + jnp.arange(SEQ, dtype=jnp.int32)[None, :]
    return {
        "x": x,
        "positions": positions,
        "ffn1_pre": gain(ks[2], D_MODEL),
        "ffn1_w_gu": w(ks[3], (DEPTH, D_MODEL, 2 * D_FF), D_MODEL),
        "ffn1_w_down": w(ks[4], (DEPTH, D_FF, D_MODEL), D_FF),
        "ffn1_post": gain(ks[5], D_MODEL),
        "mix_pre": gain(ks[6], D_MODEL),
        "w_in": w(ks[7], (DEPTH, D_MODEL, IN_WIDTH), D_MODEL),
        "w_pool": w(ks[8], (DEPTH, len(POOL_WINDOWS), POOL_GROUP, POOL_GROUP), POOL_GROUP),
        "pool_scale": 0.5 + 0.05 * jax.random.normal(ks[9], (DEPTH, POOL_WIDTH), f32),
        "sinks": 0.5 * jax.random.normal(ks[10], (DEPTH, N_HEADS), f32),
        "g_pool": gain(ks[11], POOL_WIDTH),
        "g_attn": gain(ks[12], ATTN_WIDTH),
        "w_out": w(ks[13], (DEPTH, MIX_WIDTH, D_MODEL), MIX_WIDTH),
        "mix_post": gain(ks[14], D_MODEL),
        "ffn2_pre": gain(ks[15], D_MODEL),
        "ffn2_w_gu": w(ks[16], (DEPTH, D_MODEL, 2 * D_FF), D_MODEL),
        "ffn2_w_down": w(ks[17], (DEPTH, D_FF, D_MODEL), D_FF),
        "ffn2_post": gain(ks[18], D_MODEL),
    }

def first_block(x, positions, ffn1_pre, ffn1_w_gu, ffn1_w_down, ffn1_post,
              mix_pre, w_in, w_pool, pool_scale, sinks, g_pool, g_attn, w_out, mix_post,
              ffn2_pre, ffn2_w_gu, ffn2_w_down, ffn2_post):
    inv_freq = ROPE_THETA ** (-jnp.arange(0, ROT_DIM, 2, dtype=jnp.float32) / ROT_DIM)
    ang = positions.astype(jnp.float32)[..., None] * inv_freq
    cos = jnp.cos(ang)[:, :, None, :].astype(x.dtype)
    sin = jnp.sin(ang)[:, :, None, :].astype(x.dtype)
    for l in range(DEPTH):
        h = swiglu(rms_norm(x, ffn1_pre[l]), ffn1_w_gu[l], ffn1_w_down[l])
        x = x + 0.5 * rms_norm(h, ffn1_post[l])
        h = token_mixer(rms_norm(x, mix_pre[l]), cos, sin, w_in[l], w_pool[l], pool_scale[l],
                        sinks[l], g_pool[l], g_attn[l], w_out[l])
        x = x + rms_norm(h, mix_post[l])
        h = swiglu(rms_norm(x, ffn2_pre[l]), ffn2_w_gu[l], ffn2_w_down[l])
        x = x + 0.5 * rms_norm(h, ffn2_post[l])
    return x


NSA_HEADS = 8
NSA_KV_GROUPS = 2
NSA_GROUP = NSA_HEADS // NSA_KV_GROUPS
NSA_WIDTH = NSA_HEADS * HEAD_DIM
NSA_KV_WIDTH = NSA_KV_GROUPS * HEAD_DIM
CMP_BLOCK = 32
CMP_STRIDE = 16
CMP_SPAN = CMP_BLOCK // CMP_STRIDE
CMP_HIDDEN = 256
SLC_BLOCK = 64
SLC_RATIO = SLC_BLOCK // CMP_STRIDE
SLC_TOPK = 16
OVERLAP_W = (1, 2, 2, 2, 1)
WINDOW_2 = 512
WIN_QBLOCK = 128
REL_BUCKETS = 32
REL_MAX_DIST = 128
RWKV_HEADS = 8
RWKV_WIDTH = RWKV_HEADS * HEAD_DIM
LORA_W = 64
LORA_A = 64
LORA_G = 128
GN_EPS = 64e-5
CONV_WIDTH = 3
RMS_EPS = 1e-6
NEG_INF_2 = -1e30
FORCE = 1e9

RWKV_SIZES = (RWKV_WIDTH, RWKV_WIDTH, RWKV_WIDTH, LORA_W, LORA_A, LORA_G)
RWKV_IN_WIDTH = sum(RWKV_SIZES)
RWKV_SPLITS = tuple(np.cumsum(RWKV_SIZES)[:-1].tolist())
IN_SIZES = (NSA_WIDTH, NSA_KV_WIDTH, NSA_KV_WIDTH, NSA_KV_WIDTH, NSA_KV_WIDTH, NSA_KV_WIDTH, NSA_KV_WIDTH,
            NSA_HEADS * 3, RWKV_IN_WIDTH, D_MODEL, D_MODEL)
IN_WIDTH_2 = sum(IN_SIZES)
IN_SPLITS = tuple(np.cumsum(IN_SIZES)[:-1].tolist())


def rmsnorm(x, g):
    xf = x.astype(jnp.float32)
    y = xf * lax.rsqrt(jnp.mean(xf * xf, axis=-1, keepdims=True) + RMS_EPS)
    return (y * g.astype(jnp.float32)).astype(x.dtype)

def t5_bucket(dist):
    n = jnp.maximum(dist, 0)
    max_exact = REL_BUCKETS // 2
    ratio = jnp.log(jnp.maximum(n, 1).astype(jnp.float32) / max_exact) / math.log(REL_MAX_DIST / max_exact)
    large = jnp.minimum(max_exact + (ratio * (REL_BUCKETS - max_exact)).astype(jnp.int32), REL_BUCKETS - 1)
    return jnp.where(n < max_exact, n, large)

def masked_softmax(s, mask, axis):
    s = jnp.where(mask, s.astype(jnp.float32), NEG_INF_2)
    e = jnp.exp(s - jnp.max(s, axis=axis, keepdims=True)) * mask
    return e / jnp.maximum(jnp.sum(e, axis=axis, keepdims=True), 1e-30)

def compress_blocks(kv, pe, w1, w2):
    b, s, g, dh = kv.shape
    chunks = kv.reshape(b, s // CMP_STRIDE, CMP_STRIDE, g, dh)
    n_cmp = s // CMP_STRIDE - CMP_SPAN + 1
    blocks = jnp.concatenate([chunks[:, i:i + n_cmp] for i in range(CMP_SPAN)], axis=2)
    blocks = blocks + pe[None, None, :, None, :]
    flat = blocks.transpose(0, 1, 3, 2, 4).reshape(b, n_cmp, g, CMP_BLOCK * dh)
    return jax.nn.gelu(flat @ w1) @ w2

def nsa_mixer(q, k_c, v_c, k_s, v_s, k_w, v_w, gate, rel_bias, q_norm_g, k_norm_g,
              cmp_pe_k, cmp_w1_k, cmp_w2_k, cmp_pe_v, cmp_w1_v, cmp_w2_v):
    b, s, _ = q.shape
    G, R, dh = NSA_KV_GROUPS, NSA_GROUP, HEAD_DIM
    q = rmsnorm(q.reshape(b, s, G, R, dh), q_norm_g) * (dh ** -0.5)
    k_c, v_c, k_s, v_s, k_w, v_w = [t.reshape(b, s, G, dh) for t in (k_c, v_c, k_s, v_s, k_w, v_w)]
    t_pos = jnp.arange(s)
    bias_tab = rel_bias.reshape(REL_BUCKETS, G, R)

    kc = rmsnorm(compress_blocks(k_c, cmp_pe_k, cmp_w1_k, cmp_w2_k), k_norm_g)
    vc = compress_blocks(v_c, cmp_pe_v, cmp_w1_v, cmp_w2_v)
    n_cmp = kc.shape[1]
    blk_end = jnp.arange(n_cmp) * CMP_STRIDE + CMP_BLOCK - 1
    dist_c = t_pos[:, None] - blk_end[None, :]
    bias_c = bias_tab[t5_bucket(dist_c)].transpose(2, 3, 0, 1)
    s_c = jnp.einsum('bsgrd,bcgd->bgrsc', q, kc).astype(jnp.float32) + bias_c
    p_c = masked_softmax(s_c, dist_c >= 0, axis=-1)
    o_cmp = jnp.einsum('bgrsc,bcgd->bsgrd', p_c, vc)

    n_slc = s // SLC_BLOCK
    imp_c = jnp.sum(p_c, axis=2)
    imp_pad = jnp.pad(imp_c, ((0, 0), (0, 0), (0, 0), (CMP_SPAN - 1, CMP_SPAN)))
    imp = OVERLAP_W[0] * imp_pad[..., 0:SLC_RATIO * n_slc:SLC_RATIO]
    for o in range(1, SLC_RATIO + CMP_SPAN - 1):
        imp = imp + OVERLAP_W[o] * imp_pad[..., o:o + SLC_RATIO * n_slc:SLC_RATIO]
    blk = jnp.arange(n_slc)[None, :]
    cur = (t_pos // SLC_BLOCK)[:, None]
    forced = (blk == 0) | (blk == cur) | (blk == cur - 1)
    score = jnp.where(forced, FORCE, jnp.where(blk <= cur, imp, -FORCE))
    n_sel = min(SLC_TOPK, n_slc)
    _, idx = lax.top_k(score, n_sel)
    sel_valid = idx <= cur

    nq = s // SLC_BLOCK
    k_blocks = rmsnorm(k_s, k_norm_g).reshape(b, n_slc, SLC_BLOCK, G, dh).transpose(0, 3, 1, 2, 4)
    v_blocks = v_s.reshape(b, n_slc, SLC_BLOCK, G, dh).transpose(0, 3, 1, 2, 4)
    gather = jax.vmap(jax.vmap(lambda blocks, ix: blocks[ix]))
    gi = jnp.arange(G).reshape(1, G, 1, 1, 1, 1)
    ri = jnp.arange(R).reshape(1, 1, R, 1, 1, 1)

    def slc_block(args):
        q_b, idx_b, val_b, t_b = args
        k_sel = gather(k_blocks, idx_b)
        v_sel = gather(v_blocks, idx_b)
        kpos = idx_b[..., None] * SLC_BLOCK + jnp.arange(SLC_BLOCK)
        dist = t_b[:, None, None] - kpos
        mask = (val_b[..., None] & (dist >= 0))[:, :, None]
        bias = bias_tab[t5_bucket(dist)[:, :, None], gi, ri]
        sc = jnp.einsum('bcgrd,bgcnld->bgrcnl', q_b, k_sel).astype(jnp.float32) + bias
        p = masked_softmax(sc, mask, axis=(-2, -1))
        return jnp.einsum('bgrcnl,bgcnld->bcgrd', p, v_sel)

    q_ch = jnp.moveaxis(q.reshape(b, nq, SLC_BLOCK, G, R, dh), 1, 0)
    idx_ch = jnp.moveaxis(idx.reshape(b, G, nq, SLC_BLOCK, n_sel), 2, 0)
    val_ch = jnp.moveaxis(sel_valid.reshape(b, G, nq, SLC_BLOCK, n_sel), 2, 0)
    t_ch = t_pos.reshape(nq, SLC_BLOCK)
    o_slc = jnp.moveaxis(lax.map(slc_block, (q_ch, idx_ch, val_ch, t_ch)), 0, 1).reshape(b, s, G, R, dh)

    nw = s // WIN_QBLOCK
    k_pad = jnp.pad(rmsnorm(k_w, k_norm_g), ((0, 0), (WINDOW_2, 0), (0, 0), (0, 0)))
    v_pad = jnp.pad(v_w, ((0, 0), (WINDOW_2, 0), (0, 0), (0, 0)))

    def win_block(args):
        q_b, i = args
        start = i * WIN_QBLOCK
        kw = lax.dynamic_slice_in_dim(k_pad, start, WIN_QBLOCK + WINDOW_2, axis=1)
        vw = lax.dynamic_slice_in_dim(v_pad, start, WIN_QBLOCK + WINDOW_2, axis=1)
        t_b = start + jnp.arange(WIN_QBLOCK)
        s_b = start - WINDOW_2 + jnp.arange(WIN_QBLOCK + WINDOW_2)
        dist = t_b[:, None] - s_b[None, :]
        mask = (dist >= 0) & (dist < WINDOW_2) & (s_b[None, :] >= 0)
        bias = bias_tab[t5_bucket(dist)].transpose(2, 3, 0, 1)
        sc = jnp.einsum('bqgrd,bkgd->bgrqk', q_b, kw).astype(jnp.float32) + bias
        p = masked_softmax(sc, mask, axis=-1)
        return jnp.einsum('bgrqk,bkgd->bqgrd', p, vw)

    q_wch = jnp.moveaxis(q.reshape(b, nw, WIN_QBLOCK, G, R, dh), 1, 0)
    o_win = jnp.moveaxis(lax.map(win_block, (q_wch, jnp.arange(nw))), 0, 1).reshape(b, s, G, R, dh)

    gt = jax.nn.sigmoid(gate.reshape(b, s, G, R, 3).astype(jnp.float32))
    o = gt[..., 0:1] * o_cmp + gt[..., 1:2] * o_slc + gt[..., 2:3] * o_win
    return o.reshape(b, s, NSA_WIDTH)

def rwkv7_mixer(p_in, mu, w0, w2, a0, a2, g2, k_k, k_a, r_k, ln_g, ln_b):
    b, s, _ = p_in.shape
    H, N = RWKV_HEADS, HEAD_DIM
    shifted = jnp.pad(p_in, ((0, 0), (1, 0), (0, 0)))[:, :-1]
    xl = p_in + (shifted - p_in) * mu
    r, k, v, xw, xa, xg = jnp.split(xl, RWKV_SPLITS, axis=-1)
    w = -jax.nn.softplus(-(w0 + jnp.tanh(xw) @ w2)) - 0.5
    decay = jnp.exp(-jnp.exp(w.astype(jnp.float32)))
    a = jax.nn.sigmoid(a0 + xa @ a2)
    g = jax.nn.sigmoid(xg) @ g2
    heads = lambda t: t.reshape(b, s, H, N).astype(jnp.float32)
    r, k, v, a, decay = heads(r), heads(k), heads(v), heads(a), heads(decay)
    kk = k * k_k.reshape(H, N).astype(jnp.float32)
    kk = kk / jnp.maximum(jnp.sqrt(jnp.sum(kk * kk, axis=-1, keepdims=True)), 1e-12)
    k = k * (1.0 + (a - 1.0) * k_a.reshape(H, N).astype(jnp.float32))
    xs = tuple(jnp.moveaxis(t, 1, 0) for t in (r, decay, k, v, -kk, kk * a))

    def step(state, inp):
        r_t, w_t, k_t, v_t, a_t, b_t = inp
        sa = jnp.einsum('bhij,bhj->bhi', state, a_t)
        state = state * w_t[:, :, None, :] + sa[..., None] * b_t[:, :, None, :] + v_t[..., None] * k_t[:, :, None, :]
        return state, jnp.einsum('bhij,bhj->bhi', state, r_t)

    state0 = jnp.zeros((b, H, N, N), jnp.float32)
    _, y = lax.scan(step, state0, xs)
    y = jnp.moveaxis(y, 0, 1)
    mean = jnp.mean(y, axis=-1, keepdims=True)
    var = jnp.mean(jnp.square(y - mean), axis=-1, keepdims=True)
    y = (y - mean) * lax.rsqrt(var + GN_EPS) * ln_g.reshape(H, N) + ln_b.reshape(H, N)
    y = y + jnp.sum(r * k * r_k, axis=-1, keepdims=True) * v
    return y.reshape(b, s, RWKV_WIDTH) * g

def conv_ffn(h, w_up, conv_w, conv_b, w_down):
    u = h @ w_up
    s = u.shape[1]
    up = jnp.pad(u, ((0, 0), (CONV_WIDTH - 1, 0), (0, 0)))
    c = conv_b + conv_w[0] * up[:, 0:s]
    for j in range(1, CONV_WIDTH):
        c = c + conv_w[j] * up[:, j:j + s]
    val, gate = jnp.split(c, 2, axis=-1)
    return (jax.nn.silu(gate) * val) @ w_down

def second_inputs(seed: int = 0) -> dict:
    key = jax.random.key(seed)
    ks = iter(jax.random.split(key, 40))
    L, D = DEPTH, D_MODEL

    def nrm(shape, scale):
        return scale * jax.random.normal(next(ks), shape, jnp.float32)

    def unif(shape, lo, hi):
        return jax.random.uniform(next(ks), shape, jnp.float32, lo, hi)

    return {
        'x': nrm((BATCH, SEQ, D), 1.0),
        'attn_norm_g': 1.0 + nrm((L, D), 0.1),
        'w_in': nrm((L, D, IN_WIDTH_2), D ** -0.5),
        'rel_bias': nrm((REL_BUCKETS, NSA_HEADS), 0.5),
        'q_norm_g': 1.0 + nrm((L, HEAD_DIM), 0.1),
        'k_norm_g': 1.0 + nrm((L, HEAD_DIM), 0.1),
        'cmp_pe_k': nrm((L, CMP_BLOCK, HEAD_DIM), 0.1),
        'cmp_w1_k': nrm((L, CMP_BLOCK * HEAD_DIM, CMP_HIDDEN), (CMP_BLOCK * HEAD_DIM) ** -0.5),
        'cmp_w2_k': nrm((L, CMP_HIDDEN, HEAD_DIM), CMP_HIDDEN ** -0.5),
        'cmp_pe_v': nrm((L, CMP_BLOCK, HEAD_DIM), 0.1),
        'cmp_w1_v': nrm((L, CMP_BLOCK * HEAD_DIM, CMP_HIDDEN), (CMP_BLOCK * HEAD_DIM) ** -0.5),
        'cmp_w2_v': nrm((L, CMP_HIDDEN, HEAD_DIM), CMP_HIDDEN ** -0.5),
        'rwkv_mu': unif((L, RWKV_IN_WIDTH), 0.0, 1.0),
        'rwkv_w0': unif((L, RWKV_WIDTH), -6.0, -1.0),
        'rwkv_w2': nrm((L, LORA_W, RWKV_WIDTH), 0.5 * LORA_W ** -0.5),
        'rwkv_a0': nrm((L, RWKV_WIDTH), 0.1),
        'rwkv_a2': nrm((L, LORA_A, RWKV_WIDTH), 0.5 * LORA_A ** -0.5),
        'rwkv_g2': nrm((L, LORA_G, RWKV_WIDTH), LORA_G ** -0.5),
        'rwkv_k_k': 0.85 + nrm((L, RWKV_WIDTH), 0.05),
        'rwkv_k_a': 1.0 + nrm((L, RWKV_WIDTH), 0.05),
        'rwkv_r_k': nrm((L, RWKV_HEADS, HEAD_DIM), 0.1),
        'rwkv_ln_g': 1.0 + nrm((L, RWKV_WIDTH), 0.1),
        'rwkv_ln_b': nrm((L, RWKV_WIDTH), 0.01),
        'w_proj_a': nrm((L, NSA_WIDTH, D), NSA_WIDTH ** -0.5),
        'w_proj_b': nrm((L, RWKV_WIDTH, D), RWKV_WIDTH ** -0.5),
        'w_out': nrm((L, D, D), D ** -0.5),
        'ffn_norm_g': 1.0 + nrm((L, D), 0.1),
        'w_up': nrm((L, D, 2 * D_FF), D ** -0.5),
        'conv_w': nrm((L, CONV_WIDTH, 2 * D_FF), CONV_WIDTH ** -0.5),
        'conv_b': nrm((L, 2 * D_FF), 0.01),
        'w_down': nrm((L, D_FF, D), D_FF ** -0.5),
    }

def second_block(x, attn_norm_g, w_in, rel_bias, q_norm_g, k_norm_g, cmp_pe_k, cmp_w1_k, cmp_w2_k,
              cmp_pe_v, cmp_w1_v, cmp_w2_v, rwkv_mu, rwkv_w0, rwkv_w2, rwkv_a0, rwkv_a2, rwkv_g2,
              rwkv_k_k, rwkv_k_a, rwkv_r_k, rwkv_ln_g, rwkv_ln_b, w_proj_a, w_proj_b, w_out,
              ffn_norm_g, w_up, conv_w, conv_b, w_down):
    for l in range(DEPTH):
        h = rmsnorm(x, attn_norm_g[l])
        proj = h @ w_in[l]
        q, k_c, v_c, k_s, v_s, k_w, v_w, nsa_gate, rwkv_in, gate_a, gate_b = jnp.split(proj, IN_SPLITS, axis=-1)
        o_a = nsa_mixer(q, k_c, v_c, k_s, v_s, k_w, v_w, nsa_gate, rel_bias, q_norm_g[l], k_norm_g[l],
                        cmp_pe_k[l], cmp_w1_k[l], cmp_w2_k[l], cmp_pe_v[l], cmp_w1_v[l], cmp_w2_v[l])
        o_b = rwkv7_mixer(rwkv_in, rwkv_mu[l], rwkv_w0[l], rwkv_w2[l], rwkv_a0[l], rwkv_a2[l], rwkv_g2[l],
                          rwkv_k_k[l], rwkv_k_a[l], rwkv_r_k[l], rwkv_ln_g[l], rwkv_ln_b[l])
        merged = jax.nn.sigmoid(gate_a) * (o_a @ w_proj_a[l]) + jax.nn.sigmoid(gate_b) * (o_b @ w_proj_b[l])
        x = x + (merged @ w_out[l]).astype(x.dtype)
        h2 = rmsnorm(x, ffn_norm_g[l])
        x = x + conv_ffn(h2, w_up[l], conv_w[l], conv_b[l], w_down[l]).astype(x.dtype)
    return x


def setup_inputs(seed=0):
    out = dict(first_inputs(seed))
    for name, value in second_inputs(seed + 1).items():
        if name != "x":
            out[name + "_2"] = value
    return out


def reference(
    x, positions, ffn1_pre, ffn1_w_gu, ffn1_w_down, ffn1_post, mix_pre, w_in, w_pool,
    pool_scale, sinks, g_pool, g_attn, w_out, mix_post, ffn2_pre, ffn2_w_gu, ffn2_w_down,
    ffn2_post, attn_norm_g_2, w_in_2, rel_bias_2, q_norm_g_2, k_norm_g_2, cmp_pe_k_2,
    cmp_w1_k_2, cmp_w2_k_2, cmp_pe_v_2, cmp_w1_v_2, cmp_w2_v_2, rwkv_mu_2, rwkv_w0_2, rwkv_w2_2,
    rwkv_a0_2, rwkv_a2_2, rwkv_g2_2, rwkv_k_k_2, rwkv_k_a_2, rwkv_r_k_2, rwkv_ln_g_2,
    rwkv_ln_b_2, w_proj_a_2, w_proj_b_2, w_out_2, ffn_norm_g_2, w_up_2, conv_w_2, conv_b_2,
    w_down_2,
):
    x = first_block(
        x, positions, ffn1_pre, ffn1_w_gu, ffn1_w_down, ffn1_post, mix_pre, w_in, w_pool,
        pool_scale, sinks, g_pool, g_attn, w_out, mix_post, ffn2_pre, ffn2_w_gu, ffn2_w_down,
        ffn2_post,
    )
    return second_block(
        x, attn_norm_g_2, w_in_2, rel_bias_2, q_norm_g_2, k_norm_g_2, cmp_pe_k_2, cmp_w1_k_2,
        cmp_w2_k_2, cmp_pe_v_2, cmp_w1_v_2, cmp_w2_v_2, rwkv_mu_2, rwkv_w0_2, rwkv_w2_2,
        rwkv_a0_2, rwkv_a2_2, rwkv_g2_2, rwkv_k_k_2, rwkv_k_a_2, rwkv_r_k_2, rwkv_ln_g_2,
        rwkv_ln_b_2, w_proj_a_2, w_proj_b_2, w_out_2, ffn_norm_g_2, w_up_2, conv_w_2, conv_b_2,
        w_down_2,
    )


_drawn_inputs = setup_inputs


def setup_inputs(seed=0):
    import zlib

    import numpy as np

    out = dict(_drawn_inputs(seed))
    spreads = {}
    factors = {'sinks': 6.346,
     'ffn2_post': 3.291,
     'q_norm_g_2': 8.0,
     'k_norm_g_2': 8.0,
     'cmp_pe_k_2': 8.0,
     'cmp_pe_v_2': 5.617,
     'rwkv_w2_2': 7.624,
     'rwkv_a0_2': 7.147,
     'rwkv_k_k_2': 24.587,
     'rwkv_k_a_2': 4.198,
     'rwkv_ln_g_2': 3.003,
     'rwkv_ln_b_2': 52.203,
     'conv_b_2': 8.0,
     'rel_bias_2': 7.447}
    for name, (base, spread) in spreads.items():
        noise = np.random.default_rng([zlib.crc32(name.encode()), seed]).standard_normal(out[name].shape)
        drawn = base * np.exp(spread * noise) if base else spread * noise
        out[name] = jnp.asarray(drawn.astype(out[name].dtype))
    for name, factor in factors.items():
        out[name] = (out[name] * factor).astype(out[name].dtype)
    return out
```

```python
import math
from contextlib import ExitStack

import concourse.bass as bass
from concourse import mybir

F32 = mybir.dt.float32
F32R = mybir.dt.float32r
I32 = mybir.dt.int32
ACT = mybir.ActivationFunctionType
ALU = mybir.AluOpType
AX_X = mybir.AxisListType.X

P = 128
S = 512
D = 1024
KD = D // P
NT = S // P
FF = 2816
KF = FF // P
EPS = 1e-6
NH = 8
HD = 64
C = 64
NCH = S // C
KAPPA = math.exp(-0.5)
CMP_H = 256
NCMP = S // 16 - 1
ROUND = 12582912.0
PI_BELOW = 3.1415925
RING = 4
CHUNK = KD * P
DOWN_SPLIT = ((0, 8), (8, 15), (15, 22))

STREAM = (("ffn1_up", 2 * KF), ("ffn1_down", 3 * KD), ("w_in", 10), ("w_out", KD), ("ffn2_up", 2 * KF),
          ("ffn2_down", 3 * KD), ("nsa", 11), ("rwkv", 14), ("merge", 3 * KD), ("w_out_2", KD),
          ("conv_up", 2 * KF), ("conv_down", 3 * KD), ("end", 0))
FIRST = {}
_n = 0
for _stage, _count in STREAM:
    FIRST[_stage] = _n
    _n += _count

PARAMS = (("ffn1_pre", KD), ("ffn1_post", KD), ("mix_pre", KD), ("mix_post", KD), ("ffn2_pre", KD),
          ("ffn2_post", KD), ("attn_norm", KD), ("ffn_norm", KD), ("pool_scale", 4), ("g_pool", 4),
          ("g_attn", 4), ("sinks", 8), ("eps", 1), ("half_pi", 1), ("inv_freq", 1), ("rot_sign", 1), ("q_norm", 1),
          ("k_norm", 1), ("sees_block", 1), ("mu", 14), ("w0", 4), ("a0", 4), ("k_k", 4), ("k_a", 4), ("r_k", 4),
          ("ln_g", 4), ("ln_b", 4), ("gn_eps", 1), ("ln_256", 1), ("conv_b", 2 * KF), ("conv_w0", 2 * KF),
          ("conv_w1", 2 * KF), ("conv_w2", 2 * KF))
COL = {}
_n = 0
for _name, _count in PARAMS:
    COL[_name] = _n
    _n += _count
NPARAM = _n

NUNIT = 2 * NT
NORMS = (("ffn1", KD), ("mix", KD), ("pool", 4), ("attn", 4), ("ffn2", KD), ("nsa", KD), ("conv", KD))
RSQRTS = (("ffn1_in", 1), ("ffn1_post", 1), ("mix_in", 1), ("pool_in", 1), ("attn_in", 1), ("wout_post", 1),
          ("ffn2_in", 1), ("ffn2_post", 1), ("nsa_in", 1), ("head", 7), ("kk", 4), ("gn", 4), ("conv_in", 1))
UPS = (("ffn1", KF), ("ffn2", KF))
OUTS = (("ffn1", KD), ("wout", KD), ("ffn2", KD))
FAMILIES = {
    "in_sq": NORMS, "in_sq_used": NORMS, "h32": tuple((tag, 2 * n) for tag, n in NORMS),
    "h_ready": (("ffn1", KD), ("mix", KD), ("wout", KD), ("ffn2", KD), ("nsa", KD), ("conv", KD)),
    "x_ready": (("start", KD), ("ffn1", KD), ("wout", KD), ("ffn2", KD), ("conv", KD), ("end", KD)),
    "ln": RSQRTS, "rstd": RSQRTS, "post_sum": tuple((tag, 1) for tag, _ in OUTS),
    "pair_read": UPS + (("conv", KF),), "silu": UPS + (("conv", KF),), "a32": UPS + (("conv", 2 * KF),),
    "a_ready": UPS + (("conv", KF),), "sq": OUTS, "acc": OUTS, "y_read": OUTS, "scaled": OUTS,
    "acc_zero": tuple((tag, 1) for tag, _ in OUTS),
    "scores": (("swa", 2 * NUNIT), ("nsa", 10 * NUNIT)), "masked": (("swa", 4 * NUNIT), ("nsa", 10 * NUNIT)),
    "exp": (("swa", 4 * NUNIT), ("nsa", 12 * NUNIT)), "turned": (("swa", NUNIT), ("nsa", 0)),
    "out_read": (("swa", NUNIT), ("nsa", NUNIT)),
    "step": (("sinks", 1), ("angle", 10), ("sine", 1), ("rot", 12), ("win", 23), ("swa", 2 * NUNIT), ("cmp", 11),
             ("nsa_weight", 2 * NUNIT + 2), ("rw", 0)),
}
SHARED = {}
for _kind, _stages in FAMILIES.items():
    _n = 0
    for _stage, _count in _stages:
        SHARED[_stage + "_" + _kind] = (_kind, _n)
        _n += _count


def build(nc, x, positions, params, const, mix_const, w_pool, w_ffn1_gu, w_ffn1_down, w_in, w_out, w_ffn2_gu,
          w_ffn2_down, w_nsa, nsa_const, rel_bias, distance_code, cmp_pe, cmp_w1, cmp_w2,
          w_rwkv, rwkv_const, rwkv_w2a2, rwkv_g2, w_merge, w_out_2, w_conv_up, w_conv_down, out):
    with ExitStack() as ctx:
        def sb(name, shape, dt=F32):
            return ctx.enter_context(nc.sbuf_tensor(name, shape, dt))

        sems = {}

        def sem(name):
            name = SHARED.get(name, (name, 0))[0]
            if name not in sems:
                sems[name] = ctx.enter_context(nc.semaphore(name))
            return sems[name]

        def nth(name, count):
            return sem(name), count + SHARED.get(name, (name, 0))[1]

        xT = sb("xT", [P, KD, S])
        prm = sb("prm", [P, NPARAM])
        cst = sb("cst", [P, 2, P])
        ident, ones = cst[:, 0, :], cst[:, 1, :]
        w_raw = sb("w_raw", [P, RING, CHUNK])
        w_hi = sb("w_hi", [P, RING, CHUNK], F32R)
        w_lo = sb("w_lo", [P, RING, CHUNK], F32R)
        one = sb("one", [P, 1])
        sq = sb("sq", [P, 2, S])
        acc = sb("acc", [P, S])
        rstd = sb("rstd", [P, S])
        tmp = sb("tmp", [P, 2, S])
        bank = [ctx.enter_context(nc.psum_tensor(f"bank{i}", [P, S], F32)) for i in range(8)]

        with ExitStack() as scope:
            h_hi = scope.enter_context(nc.sbuf_tensor("h_hi", [P, KD, S], F32R))
            h_lo = scope.enter_context(nc.sbuf_tensor("h_lo", [P, KD, S], F32R))
        with ExitStack() as scope:
            yT = scope.enter_context(nc.sbuf_tensor("yT", [P, KD, S], F32))
        hole = ctx.enter_context(nc.sbuf_tensor("hole", [P, 2 * KD * S], F32))
        with ExitStack() as scope:
            a_hi = scope.enter_context(nc.sbuf_tensor("a_hi", [P, KF, S], F32R))
            a_lo = scope.enter_context(nc.sbuf_tensor("a_lo", [P, KF, S], F32R))
        with ExitStack() as scope:
            x_tok = scope.enter_context(nc.sbuf_tensor("x_tok", [P, NT, D], F32))

        with ExitStack() as scope:
            def in_a(name, shape, dt=F32):
                return scope.enter_context(nc.sbuf_tensor(name, shape, dt))
            z = in_a("z", [P, 10, S])
            mixed = in_a("mixed", [P, KD, S])
            mcs = in_a("mcs", [P, 5 * P + 2 * P + 64])
            rot_of, dup_of = mcs[:, 0:P], [mcs[:, P * (1 + g):P * (2 + g)] for g in range(2)]
            dup_rot_of = [mcs[:, P * (3 + g):P * (4 + g)] for g in range(2)]
            band = mcs[:, 5 * P:7 * P]
            inv_count = mcs[:, 7 * P:7 * P + 64].rearrange("p (g t) -> p g t", g=4)
            wp = in_a("wp", [P, 4, P])
            pos = in_a("pos", [P, S], I32)
            ang = in_a("ang", [P, 3, S])
            cos_t, sin_t = in_a("cos_t", [P, S]), in_a("sin_t", [P, S])
            q_rot = in_a("q_rot", [P, 4, S])
            k_rot = in_a("k_rot", [P, 2, S])
            v_tok = in_a("v_tok", [P, NT, P])
            PAD = 16
            win = in_a("win", [P, 2, PAD + S])
            dif = in_a("dif", [P, S])
            sc = in_a("sc", [P, 2, 4, 2 * P])
            pT = in_a("pT", [P, 2, 4, P])
            small = in_a("small", [P, 2, 4, 4])
        with ExitStack() as scope:
            with ExitStack() as early:
                def in_e(name, shape, dt=F32):
                    return early.enter_context(nc.sbuf_tensor(name, shape, dt))
                zn = in_e("zn", [P, 11, S])
                pair = in_e("pair", [P, 2, 2, S // 2])
                code = in_e("code", [33, 5 * P])
                rv = in_e("rv", [NH, 5 * P])
            E = in_a("E", [P, 2, 8, S])
            with ExitStack() as early:
                cw1 = early.enter_context(nc.sbuf_tensor("cw1", [P, 16, CMP_H], F32))
            toeplitz = in_a("toeplitz", [P, NH, S])
            qn = in_a("qn", [P, 4, S])
            kd = in_a("kd", [P, 4, S])
            v2_tok = in_a("v2_tok", [P, 2, NT, P])
            p2T = in_a("p2T", [P, 2, 4, P])
            oA = in_a("oA", [P, 4, S])
            ncs = in_a("ncs", [P, 4 * P])
            flip = ncs[:, 3 * P:4 * P]
            dup2 = [ncs[:, P * g:P * (g + 1)] for g in range(2)]
            head_ones = ncs[:, 2 * P:3 * P]
            rel = in_a("rel", [33, NH])
            cw2 = in_a("cw2", [P, 2, 2, 2 * HD])
            pe_in = in_a("pe_in", [P, 2, 16])
            hid = in_a("hid", [P, 2, 64])
            hid2 = in_a("hid2", [P, 2, 64])
            kcn = in_a("kcn", [P, 2 * NCMP])
            vct = in_a("vct", [NCMP, 2, HD])
            gate_tok = in_a("gate_tok", [P, NT, 24])
            Ec = in_a("Ec", [P, 2, 4, 32])
            stat = in_a("stat", [P, 2, 3, 12])

        def by_tile(x):
            return x.rearrange("p (n t) -> p n t", n=NT)

        def reverse(x):
            return by_tile(x)[:, :, ::-1]

        def param(name, k=0):
            return prm[:, COL[name] + k:COL[name] + k + 1]

        with ExitStack() as scope:
            pin = in_a("pin", [P, 14, S])
            yl = in_a("yl", [P, 4, S])
            bonus = in_a("bonus", [P, 4, S])
            AR = in_a("AR", [P, NT, 2, P])
            Bh, Kh = in_a("Bh", [P, S]), in_a("Kh", [P, S])
            At, Bt, Kt, Vt = (in_a(n, [P, NT, P]) for n in ("At", "Bt", "Kt", "Vt"))
            mats = in_a("mats", [P, 4, 4 * P])
            Dm, DT, X, OT = (in_a(n, [P, 4, P]) for n in ("Dm", "DT", "X", "OT"))
            UG = in_a("UG", [P, 4, P])
            AkV = in_a("AkV", [P, 4, HD])
            rcs = in_a("rcs", [P, 6 * P + P + HD])
            level = [rcs[:, P * i:P * (i + 1)] for i in range(6)]
            head_ones2, eye2 = rcs[:, 6 * P:7 * P], rcs[:, 7 * P:7 * P + HD]
            w2a2 = in_a("w2a2", [P, 4 * P])
            PC = in_a("PC", [P, 4, NCH])
            g2 = UG[:, :, :].rearrange("p a b -> p (a b)")
        mask4, reset = rstd, acc
        state = sq[:, :, 0:4 * HD].rearrange("p s (m i) -> p s m i", m=4)
        with ExitStack() as scope:
            with ExitStack() as early:
                oA2 = early.enter_context(nc.sbuf_tensor("oA2", [P, 4, S], F32))
            m_hi, m_lo = in_a("m_hi", [P, KD, S], F32R), in_a("m_lo", [P, KD, S], F32R)
            in_a("merge_pad", [P, 6 * S])
            o_hi, o_lo = in_a("o_hi", [P, KD, S], F32R), in_a("o_lo", [P, KD, S], F32R)
        oA_dram = nc.dram_tensor("nsa_out", (P, 4 * S), F32)
        bias_dram = nc.dram_tensor("bias_by_distance", (NH, 5 * P), F32)

        block = ctx.enter_context(nc.Block())

        @block.sync
        def _(sp):
            sp.dma_start(cst[:, :, :], const.rearrange("p (a b) -> p a b", a=2)).then_inc(sem("const_in"), 16)
            sp.dma_start(x_tok[:, :, :], x[0].rearrange("(n p) d -> p n d", p=P)).then_inc(sem("x_in"), 16)
            sp.dma_start(prm[:, :], params).then_inc(sem("params_in"), 16)

            def load(c, s, source, width=CHUNK, first=False):
                if not first:
                    sp.wait_ge(*nth("w_split", c - RING + 1))
                sp.dma_start(w_raw[:, s, 0:width], source).then_inc(sem(f"w_in{s}"), 16)

            def stream(c0, n, source, first=False):
                if first:
                    for u in range(RING):
                        load(u, u, source(u), first=True)
                with sp.Fori(1 if first else 0, n // RING) as i:
                    for u in range(RING):
                        load(i * RING + (c0 + u), (c0 + u) % RING, source(i * RING + u))
                for u in range(n - n % RING, n):
                    load(c0 + u, (c0 + u) % RING, source(u))

            def stream_down(c0, w):
                with sp.Fori(0, KD // RING) as i:
                    for u in range(RING):
                        for j, (a, b) in enumerate(DOWN_SPLIT):
                            v = c0 + 3 * u + j
                            load(i * (3 * RING) + v, v % RING, w[bass.ds(i * RING + u, 1), :, a * P:b * P]
                                 .rearrange("a p n -> (a p) n"), (b - a) * P)

            def whole(w):
                return lambda c: w[bass.ds(c, 1), :, :].rearrange("a p n -> (a p) n")

            stream(FIRST["ffn1_up"], 2 * KF, whole(w_ffn1_gu), first=True)
            stream_down(FIRST["ffn1_down"], w_ffn1_down)

            sp.wait_ge(*nth("w_used", FIRST["w_in"]))
            sp.dma_start(mcs[:, :], mix_const).then_inc(sem("mix_const_in"), 16)
            sp.dma_start(pos[:, :], positions.partition_broadcast(P)).then_inc(sem("positions_in"), 16)
            sp.dma_start(wp[:, :, :], w_pool.rearrange("g c d -> c g d")).then_inc(sem("w_pool_in"), 16)
            stream(FIRST["w_in"], 10, whole(w_in))
            stream(FIRST["w_out"], KD, whole(w_out))
            stream(FIRST["ffn2_up"], 2 * KF, whole(w_ffn2_gu))
            stream_down(FIRST["ffn2_down"], w_ffn2_down)

            sp.wait_ge(*nth("w_used", FIRST["nsa"]))
            sp.dma_start(ncs[:, :], nsa_const).then_inc(sem("nsa_small_in"), 16)
            sp.dma_start(rel[0:32, :], rel_bias).then_inc(sem("nsa_small_in"), 16)
            sp.dma_start(code[:, :], distance_code).then_inc(sem("nsa_small_in"), 16)
            sp.dma_start(pe_in[:, :, :], cmp_pe.rearrange("v p j -> p v j")).then_inc(sem("nsa_small_in"), 16)
            for v in range(2):
                for c in range(2):
                    sp.dma_start(cw2[:, v, :, c * HD:(c + 1) * HD], cmp_w2[v].rearrange("(h p) d -> p h d", p=P))\
                        .then_inc(sem("nsa_small_in"), 16)
            sp.dma_start(cw1[:, :, :], cmp_w1[0].rearrange("(j p) n -> p j n", p=P)).then_inc(sem("cw1_in"), 16)
            stream(FIRST["nsa"], 11, whole(w_nsa))
            sp.wait_ge(*nth("nsa_read", 8))
            sp.dma_start(bias_dram.ap(), rv[:, :]).then_inc(sem("bias_out"), 16)
            sp.wait_ge(*nth("nsa_job", 14))
            sp.dma_start(cw1[:, :, :], cmp_w1[1].rearrange("(j p) n -> p j n", p=P)).then_inc(sem("cw1_in"), 16)
            sp.wait_ge(*nth("nsa_job", 16))
            sp.wait_ge(*nth("bias_out", 16))
            sp.dma_start(toeplitz[:, :, :], bass.AP(bias_dram, 0, [[1, P], [5 * P, NH], [1, S]]))\
                .then_inc(sem("toeplitz_in"), 16)

            sp.wait_ge(*nth("nsa_out_read", 8))
            sp.dma_start(oA_dram.ap(), oA[:, :, :].rearrange("p a b -> p (a b)")).then_inc(sem("oA_out"), 16)
            sp.wait_ge(*nth("oA_out", 16))
            sp.dma_start(rcs[:, :], rwkv_const[:, 2 * S:]).then_inc(sem("rwkv_small_in"), 16)
            sp.dma_start(mask4[:, :], rwkv_const[:, 0:S]).then_inc(sem("rwkv_small_in"), 16)
            sp.dma_start(reset[:, :], rwkv_const[:, S:2 * S]).then_inc(sem("rwkv_small_in"), 16)
            sp.dma_start(w2a2[:, :], rwkv_w2a2).then_inc(sem("rwkv_small_in"), 16)
            stream(FIRST["rwkv"], 14, whole(w_rwkv))
            sp.wait_ge(*nth("chunk_terms", 8))
            sp.dma_start(g2, rwkv_g2).then_inc(sem("g2_in"), 16)
            sp.wait_ge(*nth("walk_read", 2 * (NCH - 1)))
            sp.dma_start(oA2[:, :, :].rearrange("p a b -> p (a b)"), oA_dram.ap()).then_inc(sem("oA_in"), 16)
            with sp.Fori(0, 2) as i:
                for u in range(3 * RING):
                    v = FIRST["merge"] + u
                    load(i * (3 * RING) + v, v % RING,
                         w_merge[bass.ds(i * (3 * RING) + u, 1), :, :].rearrange("a p n -> (a p) n"))
            stream(FIRST["w_out_2"], KD, whole(w_out_2))
            stream(FIRST["conv_up"], 2 * KF, whole(w_conv_up))
            stream_down(FIRST["conv_down"], w_conv_down)
            for n in range(NT):
                sp.wait_ge(*nth("out_copied", 2 * (n + 1)))
                sp.dma_start(out[0, n * P:(n + 1) * P, :],
                             yT[:, 2 * n:2 * n + 2, :].rearrange("p a b -> p (a b)")).then_inc(sem("out_done"), 16)
            sp.wait_ge(*nth("out_done", 16 * NT))

        @block.gpsimd
        def _(pool):
            def split(c, turn, s, width=CHUNK, first=False):
                pool.wait_ge(*nth(f"w_in{s}", (turn + 1) * 16))
                if not first:
                    pool.wait_ge(*nth("w_used", c - RING + 1))
                raw = w_raw[:, s, 0:width]
                nc.gpsimd.tensor_tensor(w_hi[:, s, 0:width], raw, one[:, 0:1].to_broadcast([P, width]), ALU.mult).then_inc(sem("w_rounded"), 1)
                pool.wait_ge(*nth("w_rounded", c + 1))
                nc.gpsimd.tensor_tensor(w_lo[:, s, 0:width], raw, w_hi[:, s, 0:width].bitcast(F32),
                                        ALU.subtract).then_inc(sem("w_split"), 1)

            def stream(c0, n, first=False):
                if first:
                    for u in range(RING):
                        split(u, 0, u, first=True)
                with pool.Fori(1 if first else 0, n // RING) as i:
                    for u in range(RING):
                        v = c0 + u
                        split(i * RING + v, i + v // RING, v % RING)
                for u in range(n - n % RING, n):
                    v = c0 + u
                    split(v, v // RING, v % RING)

            def stream_down(c0):
                with pool.Fori(0, KD // RING) as i:
                    for u in range(3 * RING):
                        a, b = DOWN_SPLIT[u % 3]
                        v = c0 + u
                        split(i * (3 * RING) + v, i * 3 + v // RING, v % RING, (b - a) * P)

            nc.gpsimd.memset(one[:, :], 1.0).then_inc(sem("one_set"), 1)
            pool.wait_ge(*nth("one_set", 1))
            stream(FIRST["ffn1_up"], 2 * KF, first=True)
            stream_down(FIRST["ffn1_down"])
            stream(FIRST["w_in"], 10)
            stream(FIRST["w_out"], KD)
            stream(FIRST["ffn2_up"], 2 * KF)
            stream_down(FIRST["ffn2_down"])
            stream(FIRST["nsa"], 11)
            stream(FIRST["rwkv"], 14)
            stream(FIRST["merge"], 3 * KD)
            stream(FIRST["w_out_2"], KD)
            stream(FIRST["conv_up"], 2 * KF)
            stream_down(FIRST["conv_down"])

        @block.tensor
        def _(pe):
            def chunk(c, s, k0, k1, rhs_hi, rhs_lo, dst, start, stop, each=None, w0=None):
                w0 = k0 if w0 is None else w0
                pe.wait_ge(*nth("w_split", c + 1))
                for k in range(k0, k1):
                    if each:
                        pe.wait_ge(*nth(each, k + 1))
                    hi = w_hi[:, s, (k - w0) * P:(k - w0 + 1) * P]
                    lo = w_lo[:, s, (k - w0) * P:(k - w0 + 1) * P]
                    nc.tensor.matmul(dst, hi, rhs_hi[:, k, :], start=start and k == k0, stop=False)
                    nc.tensor.matmul(dst, hi, rhs_lo[:, k, :], start=False, stop=False)
                    last = nc.tensor.matmul(dst, lo, rhs_hi[:, k, :], start=False, stop=stop and k == k1 - 1)
                return last

            def ffn_up(tag, c0):
                def body(i, first):
                    for u in range(2):
                        if not first:
                            pe.wait_ge(*nth(tag + "_pair_read", 2 * i + u - 1))
                        for v in range(2):
                            c = 4 * i + (c0 + 2 * u + v)
                            last = chunk(c, (c0 + 2 * u + v) % RING, 0, KD, h_hi, h_lo, bank[2 * u + v][:, :],
                                         True, True, tag + "_h_ready" if first and u == v == 0 else None)
                            last.then_inc(sem("w_used"), 1)
                body(0, True)
                with pe.Fori(1, KF // 2) as i:
                    body(i, False)

            def ffn_down(tag, c0, read):
                pe.wait_ge(*nth(tag + "_a_ready", KF))
                def body(i, first):
                    for u in range(4):
                        if not first:
                            pe.wait_ge(*nth(read, 4 * i + u - 3))
                        for j, (a, b) in enumerate(DOWN_SPLIT):
                            v = 3 * u + j
                            last = chunk(12 * i + (c0 + v), (c0 + v) % RING, a, b, a_hi, a_lo, bank[4 + u][:, :],
                                         j == 0, j == 2)
                            last.then_inc(sem("w_used"), 1)
                body(0, True)
                body(1, False)

            def sum_squares(tag, n, ready, used):
                for k in range(n):
                    pe.wait_ge(*nth(ready, k + 1))
                    nc.tensor.matmul(bank[0][:, :], ones, sq[:, k % 2, :], start=(k == 0),
                                     stop=(k == n - 1)).then_inc(sem(used), 1)

            def project(tag, c0, n, read, h_ready=True, hi=h_hi, lo=h_lo):
                def tile(c, u, first, wait=None):
                    if wait is not None:
                        pe.wait_ge(*nth(read, wait))
                    chunk(c, (c0 + u) % RING, 0, KD, hi, lo, bank[4 + u % 4][:, :], True, True,
                          tag + "_h_ready" if first else None).then_inc(sem("w_used"), 1)
                for u in range(4):
                    tile(c0 + u, u, u == 0 and h_ready)
                with pe.Fori(1, n // 4) as i:
                    for u in range(4):
                        tile(i * 4 + (c0 + u), u, False, wait=i * 4 + (u - 3))
                for m in range(n - n % 4, n):
                    tile(c0 + m, m % 4, False, wait=m - 3)

            def attend_window(n, g, unit):
                keys = slice(max(0, n - 1) * P, (n + 1) * P)
                width = keys.stop - keys.start
                if unit >= 2:
                    pe.wait_ge(*nth("swa_masked", 4 * (unit - 1)))
                for h in range(4):
                    e, i = h % 2, h // 2
                    last = nc.tensor.matmul(bank[2 * (unit % 2) + e][:, i * width:(i + 1) * width],
                                            q_rot[64 * e:64 * e + 64, 2 * g + i, n * P:(n + 1) * P],
                                            k_rot[64 * e:64 * e + 64, g, keys], start=(i == 0), stop=(i == 1),
                                            skip_group_check=True)
                    if i == 1:
                        last.then_inc(sem("swa_scores"), 1)

            def weigh_window(n, g, unit):
                tiles = [j for j in (n - 1, n) if j >= 0]
                pe.wait_ge(*nth("swa_probs", 4 * (unit + 1)))
                if unit:
                    pe.wait_ge(*nth("swa_turned_read", unit))
                for b, j in enumerate(tiles):
                    for h in range(4):
                        last = nc.tensor.transpose(bank[4 + b][:, h * P:(h + 1) * P],
                                                   sc[:, unit % 2, h, b * P:(b + 1) * P], ident)
                last.then_inc(sem("swa_turned"), 1)
                pe.wait_ge(*nth("swa_turned_read", unit + 1))
                if unit:
                    pe.wait_ge(*nth("swa_out_read", unit))
                for h in range(4):
                    e, i = h % 2, h // 2
                    for b, j in enumerate(tiles):
                        last = nc.tensor.matmul(bank[6][64 * e:64 * e + 64, i * P:(i + 1) * P],
                                                v_tok[:, j, 64 * g:64 * g + 64], pT[:, b, h, :],
                                                start=(b == 0), stop=(b == len(tiles) - 1), skip_group_check=True)
                last.then_inc(sem("swa_out"), 1)

            pe.wait_ge(*nth("const_in", 16))
            pe.wait_ge(*nth("x_in", 16))
            for k in range(KD):
                for n in range(NT):
                    last = nc.tensor.transpose(bank[k][:, n * P:(n + 1) * P], x_tok[:, n, k * P:(k + 1) * P], ident)
                last.then_inc(sem("x_turned"), 1)
            pe.wait_ge(*nth("start_x_ready", 1))
            sum_squares("ffn1", KD, "ffn1_in_sq", "ffn1_in_sq_used")
            ffn_up("ffn1", FIRST["ffn1_up"])
            ffn_down("ffn1", FIRST["ffn1_down"], "ffn1_y_read")
            pe.wait_ge(*nth("ffn1_acc", KD))
            nc.tensor.matmul(bank[0][:, :], ones, acc[:, :], start=True, stop=True).then_inc(sem("ffn1_post_sum"), 1)

            sum_squares("mix", KD, "mix_in_sq", "mix_in_sq_used")
            project("mix", FIRST["w_in"], 10, "z_read")
            pe.wait_ge(*nth("mix_const_in", 16))
            for g in range(2):
                pe.wait_ge(*nth("z_read", 1))
                if g:
                    pe.wait_ge(*nth("rot_used", 2 * g - 1))
                nc.tensor.matmul(bank[2 * g][:, :], dup_of[g], z[:, 0, :], start=True, stop=True)
                nc.tensor.matmul(bank[2 * g + 1][:, :], dup_rot_of[g], z[:, 0, :], start=True, stop=True)\
                    .then_inc(sem("rot_done"), 1)
            for i in range(4):
                pe.wait_ge(*nth("z_read", 3 + i))
                pe.wait_ge(*nth("rot_used", 1 + i // 2 if i < 2 else 1 + i))
                nc.tensor.matmul(bank[i % 2 if i < 2 else i][:, :], rot_of, z[:, 2 + i, :], start=True, stop=True)\
                    .then_inc(sem("rot_done"), 1)
            pe.wait_ge(*nth("z_read", 10))
            for n in range(NT):
                last = nc.tensor.transpose(bank[4][:, n * P:(n + 1) * P], z[:, 1, n * P:(n + 1) * P], ident)
            last.then_inc(sem("v_turned"), 1)
            for g in range(4):
                pe.wait_ge(*nth("w_pool_in", 16))
                pe.wait_ge(*nth("pool_diff", g + 1))
                if g:
                    pe.wait_ge(*nth("pooled", g))
                nc.tensor.matmul(bank[7][:, :], wp[:, g, :], dif[:, :], start=True, stop=True)\
                    .then_inc(sem("pool_product"), 1)
            pe.wait_ge(*nth("rot_used", 6))
            pe.wait_ge(*nth("v_read", 1))
            units = [(n, g) for n in range(NT) for g in range(2)]
            attend_window(*units[0], 0)
            for u, (n, g) in enumerate(units):
                if u + 1 < len(units):
                    attend_window(*units[u + 1], u + 1)
                weigh_window(n, g, u)
            pe.wait_ge(*nth("swa_masked", 4 * len(units)))
            sum_squares("pool", 4, "pool_in_sq", "pool_in_sq_used")
            pe.wait_ge(*nth("pool_in_rstd", 1))
            sum_squares("attn", 4, "attn_in_sq", "attn_in_sq_used")
            project("wout", FIRST["w_out"], KD, "wout_y_read")
            pe.wait_ge(*nth("wout_acc", KD))
            nc.tensor.matmul(bank[0][:, :], ones, acc[:, :], start=True, stop=True).then_inc(sem("wout_post_sum"), 1)

            sum_squares("ffn2", KD, "ffn2_in_sq", "ffn2_in_sq_used")
            ffn_up("ffn2", FIRST["ffn2_up"])
            ffn_down("ffn2", FIRST["ffn2_down"], "ffn2_y_read")
            pe.wait_ge(*nth("ffn2_acc", KD))
            nc.tensor.matmul(bank[0][:, :], ones, acc[:, :], start=True, stop=True).then_inc(sem("ffn2_post_sum"), 1)

            sum_squares("nsa", KD, "nsa_in_sq", "nsa_in_sq_used")
            project("nsa", FIRST["nsa"], 11, "zn_read")
            pe.wait_ge(*nth("nsa_small_in", 8 * 16))
            job = [0]

            def job_bank():
                if job[0] >= 2:
                    pe.wait_ge(*nth("nsa_read", job[0] - 1))
                job[0] += 1
                return bank[2 + (job[0] - 1) % 2]

            pe.wait_ge(*nth("zn_read", 11))
            for v in range(2):
                b = job_bank()
                for n in range(NT):
                    last = nc.tensor.transpose(b[:, n * P:(n + 1) * P], zn[:, 2 + v, n * P:(n + 1) * P], ident)
                last.then_inc(sem("nsa_job"), 1)
            for v in range(2):
                for g in range(2):
                    nc.tensor.matmul(job_bank()[:, :], dup2[g], zn[:, 4 + v, :], start=True, stop=True)\
                        .then_inc(sem("nsa_job"), 1)
            pe.wait_ge(*nth("rel_one", 1))
            for a, b in ((0, S), (S, 5 * P)):
                nc.tensor.matmul(job_bank()[0:NH, 0:b - a], rel[:, :], code[:, a:b], start=True, stop=True)\
                    .then_inc(sem("nsa_job"), 1)
            pe.wait_ge(*nth("gates", 1))
            b = job_bank()
            for n in range(NT):
                last = nc.tensor.transpose(b[:, n * 24:(n + 1) * 24], oA[0:24, 0, n * P:(n + 1) * P],
                                           ident[0:24, 0:24])
            last.then_inc(sem("nsa_job"), 1)
            for i in range(6):
                pe.wait_ge(*nth("head_sq", i + 1))
                nc.tensor.matmul(bank[i % 2][:, :], head_ones, sq[:, i % 2, :], start=True, stop=True)\
                    .then_inc(sem("head_sum"), 1)
            for v in range(2):
                pe.wait_ge(*nth("head_rstd_used", v + 1))
                for g in range(2):
                    nc.tensor.matmul(job_bank()[:, :], dup2[g], zn[:, v, :], start=True, stop=True)\
                        .then_inc(sem("nsa_job"), 1)
            for v in range(2):
                pe.wait_ge(*nth("cw1_in", 16 * (v + 1)))
                pe.wait_ge(*nth("nsa_read", 4 + 2 * v))
                b = job_bank()
                for h in range(2):
                    for j in range(16):
                        nc.tensor.matmul(b[:, h * 64:h * 64 + 2 * NCMP], cw1[:, j, h * P:(h + 1) * P],
                                         pair[:, v, :, j:j + 8 * NCMP - 7:8], start=(j == 0), stop=(j == 15),
                                         skip_group_check=True)
                    for j in range(16):
                        last = nc.tensor.matmul(b[:, h * 64 + 2 * NCMP:h * 64 + 2 * NCMP + 1],
                                                cw1[:, j, h * P:(h + 1) * P], pe_in[:, v, j:j + 1], start=(j == 0),
                                                stop=(j == 15), skip_group_check=True)
                last.then_inc(sem("nsa_job"), 1)
                pe.wait_ge(*nth("gelu", v + 1))
                b = job_bank()
                if v == 0:
                    for h in range(2):
                        last = nc.tensor.matmul(b[:, 0:2 * NCMP], cw2[:, 0, h, :], hid[:, h, 0:2 * NCMP],
                                                start=(h == 0), stop=(h == 1))
                    last.then_inc(sem("nsa_job"), 1)
                    pe.wait_ge(*nth("head_sq", 7))
                    nc.tensor.matmul(bank[0][:, 0:2 * NCMP], head_ones, sq[:, 0, 0:2 * NCMP], start=True, stop=True)\
                        .then_inc(sem("head_sum"), 1)
                else:
                    for g in range(2):
                        for h in range(2):
                            last = nc.tensor.matmul(b[0:NCMP, g * HD:(g + 1) * HD], hid[:, h, g * NCMP:(g + 1) * NCMP],
                                                    cw2[:, 1, h, 0:HD], start=(h == 0), stop=(h == 1),
                                                    skip_group_check=True)
                    last.then_inc(sem("nsa_job"), 1)
            pe.wait_ge(*nth("nsa_read", 17))
            pe.wait_ge(*nth("kc_normed", 1))

            def nsa_scores(n, g, unit):
                for i in range(10):
                    b = bank[i % 4] if unit % 2 == 0 else bank[(i + 2) % 4]
                    if 10 * unit + i >= 4:
                        pe.wait_ge(*nth("nsa_masked", 10 * unit + i - 3))
                    if i < 8:
                        h, e = i % 4, i % 2
                        last = nc.tensor.matmul(b[:, 0:(n + 1) * P],
                                                qn[64 * e:64 * e + 64, 2 * g + h // 2, n * P:(n + 1) * P],
                                                kd[64 * e:64 * e + 64, 2 * (i // 4) + g, 0:(n + 1) * P],
                                                start=True, stop=True)
                    else:
                        e = i - 8
                        for h in range(2):
                            last = nc.tensor.matmul(b[:, h * 32:h * 32 + 8 * n + 7],
                                                    qn[64 * e:64 * e + 64, 2 * g + h, n * P:(n + 1) * P],
                                                    kcn[64 * e:64 * e + 64, g * NCMP:g * NCMP + 8 * n + 7],
                                                    start=(h == 0), stop=(h == 1), skip_group_check=True)
                    last.then_inc(sem("nsa_scores"), 1)

            turn = [0]

            def nsa_weigh(n, g, unit):
                dst = bank[6 + unit % 2]
                if unit >= 2:
                    pe.wait_ge(*nth("nsa_out_read", unit - 1))
                items = [(v, j) for v in range(2) for j in range(n + 1)] + [(2, 0)]
                pe.wait_ge(*nth("nsa_weighed", unit + 1))

                def turn_item(x):
                    v, j = items[x]
                    k = turn[0] + x
                    if k >= 2:
                        pe.wait_ge(*nth("p2T_ready", k - 1))
                    for h in range(4):
                        src = Ec[:, unit % 2, h, 0:8 * n + 7] if v == 2 else E[:, unit % 2, 4 * v + h, j * P:(j + 1) * P]
                        rows = 8 * n + 7 if v == 2 else P
                        last = nc.tensor.transpose(bank[4 + k % 2][0:rows, h * P:(h + 1) * P], src, flip)
                    last.then_inc(sem("nsa_turned"), 1)

                def sum_item(x):
                    v, j = items[x]
                    k = turn[0] + x
                    pe.wait_ge(*nth("p2T_ready", k + 1))
                    for h in range(4):
                        e, i = h % 2, h // 2
                        if v == 2:
                            lhs, rhs = vct[0:8 * n + 7, g, :], p2T[0:8 * n + 7, k % 2, h, :]
                        else:
                            lhs, rhs = v2_tok[:, v, j, 64 * g:64 * g + 64], p2T[:, k % 2, h, :]
                        last = nc.tensor.matmul(dst[64 * e:64 * e + 64, i * P:(i + 1) * P], lhs, rhs,
                                                start=(x == 0 and i == 0), stop=(v == 2), skip_group_check=True)
                    last.then_inc(sem("p2T_used"), 1)
                    return last

                turn_item(0)
                for x in range(len(items)):
                    if x + 1 < len(items):
                        turn_item(x + 1)
                    last = sum_item(x)
                turn[0] += len(items)

            units = [(n, g) for n in range(NT) for g in range(2)]
            nsa_scores(*units[0], 0)
            for u, (n, g) in enumerate(units):
                if u + 1 < len(units):
                    nsa_scores(*units[u + 1], u + 1)
                nsa_weigh(n, g, u)

            pe.wait_ge(*nth("oA_out", 16))
            project("rwkv", FIRST["rwkv"], 14, "pin_read", h_ready=False)
            pe.wait_ge(*nth("rwkv_small_in", 4 * 16))
            pe.wait_ge(*nth("pin_read", 14))
            for m in range(4):
                cols = slice(m * P, (m + 1) * P)
                if m == 0:
                    pe.wait_ge(*nth("lora_in", 1))
                else:
                    pe.wait_ge(*nth("chunk_terms_read", 2 * m))
                nc.tensor.matmul(bank[0][:, :], w2a2[0:64, cols], pin[0:64, 12, :], start=True, stop=True)
                nc.tensor.matmul(bank[1][:, :], w2a2[64:128, cols], pin[64:128, 12, :], start=True, stop=True)\
                    .then_inc(sem("lora"), 1)
                for i in range(2):
                    pe.wait_ge(*nth("rw_square", 1 + m)) if i == 0 else pe.wait_ge(*nth("rk_product", 1 + m))
                    nc.tensor.matmul(bank[2 + i][:, :], head_ones2, sq[:, i, :], start=True, stop=True)\
                        .then_inc(sem("rw_head_sum"), 1)
                pe.wait_ge(*nth("hats", 3 * (m + 1)))
                for b, src in enumerate((AR[:, :, 0, :], Bh[:, :].rearrange("p (n t) -> p n t", n=NT),
                                         Kh[:, :].rearrange("p (n t) -> p n t", n=NT),
                                         pin[:, 8 + m, :].rearrange("p (n t) -> p n t", n=NT))):
                    for n in range(NT):
                        last = nc.tensor.transpose(bank[4 + b][:, n * P:(n + 1) * P], src[:, n, :], ident)
                    last.then_inc(sem("rw_turned"), 1)
                for half in range(2):
                    r = 2 * m + half
                    units = [(2 * half + i, e) for i in range(2) for e in range(2)]
                    if half == 0:
                        pe.wait_ge(*nth("bonus_done", m + 1))
                    else:
                        pe.wait_ge(*nth("chunk_terms_read", r))
                    for u, (n, e) in enumerate(units):
                        rows = slice(64 * e, 64 * e + 64)
                        rhs = AR[rows, n, :, :].rearrange("p a t -> p (a t)")
                        nc.tensor.matmul(bank[u][:, 0:2 * P], Bh[rows, n * P:(n + 1) * P], rhs, start=True, stop=True,
                                         skip_group_check=True)
                        nc.tensor.matmul(bank[u][:, 2 * P:], Kh[rows, n * P:(n + 1) * P], rhs, start=True, stop=True,
                                         skip_group_check=True).then_inc(sem("rw_scores"), 1)
                    pe.wait_ge(*nth("rw_tok", 4 * (m + 1)))
                    pe.wait_ge(*nth("level_mask", 6 * r + 1))
                    for u in range(4):
                        last = nc.tensor.transpose(bank[4][:, u * P:(u + 1) * P], OT[:, u, :], ident)
                    last.then_inc(sem("level_turned"), 1)
                    for k in range(1, 6):
                        pe.wait_ge(*nth("level_mask", 6 * r + k + 1))
                        pe.wait_ge(*nth("inverse", 6 * r + k))
                        for u in range(4):
                            last = nc.tensor.matmul(bank[5][:, u * P:(u + 1) * P], OT[:, u, :], Dm[:, u, :],
                                                    start=True, stop=True, skip_group_check=True)
                        last.then_inc(sem("level_x"), 1)
                        pe.wait_ge(*nth("level_x_read", 5 * r + k))
                        for u in range(4):
                            if k < 5:
                                nc.tensor.matmul(bank[6][:, u * P:(u + 1) * P], DT[:, u, :], X[:, u, :],
                                                 start=True, stop=True, skip_group_check=True)
                            last = nc.tensor.matmul(bank[7][:, u * P:(u + 1) * P], X[:, u, :], DT[:, u, :],
                                                    start=True, stop=True, skip_group_check=True)
                        last.then_inc(sem("level_added"), 1)
                    for u, (n, e) in enumerate(units):
                        last = nc.tensor.matmul(bank[0][:, u * HD:(u + 1) * HD], mats[:, u, 2 * P:3 * P],
                                                Vt[:, n, 64 * e:64 * e + 64], start=True, stop=True,
                                                skip_group_check=True)
                    last.then_inc(sem("akv"), 1)
                    pe.wait_ge(*nth("akv_read", r + 1))
                    pe.wait_ge(*nth("inverse", 6 * r + 6))
                    for u, (n, e) in enumerate(units):
                        nc.tensor.matmul(bank[1][:, u * P:u * P + HD], DT[:, u, :], AkV[:, u, :],
                                         start=True, stop=True, skip_group_check=True)
                        last = nc.tensor.matmul(bank[1][:, u * P + HD:(u + 1) * P], DT[:, u, :],
                                                At[:, n, 64 * e:64 * e + 64], start=True, stop=True,
                                                skip_group_check=True)
                    last.then_inc(sem("ug"), 1)
                    pe.wait_ge(*nth("ug_read", r + 1))
                    for u, (n, e) in enumerate(units):
                        rows, at = slice(64 * e, 64 * e + 64), slice((u // 2) * P, (u // 2 + 1) * P)
                        U, G = UG[:, u, 0:HD], UG[:, u, HD:]
                        V = Vt[:, n, 64 * e:64 * e + 64]
                        nc.tensor.matmul(bank[2][rows, at], G, mats[:, u, P:2 * P], start=True, stop=True,
                                         skip_group_check=True)
                        nc.tensor.matmul(bank[3][rows, at], U, mats[:, u, P:2 * P], start=True, stop=False,
                                         skip_group_check=True)
                        nc.tensor.matmul(bank[3][rows, at], V, mats[:, u, 3 * P:], start=False, stop=True,
                                         skip_group_check=True)
                        at = slice((u // 2) * HD, (u // 2 + 1) * HD)
                        for c in range(2):
                            tok = slice(64 * c, 64 * c + 64)
                            B, K, V = (x[tok, n, 64 * e:64 * e + 64] for x in (Bt, Kt, Vt))
                            nc.tensor.matmul(bank[4 + c][rows, at], UG[tok, u, HD:], B, start=True, stop=True,
                                             skip_group_check=True)
                            nc.tensor.matmul(bank[6 + c][rows, at], B, UG[tok, u, 0:HD], start=True, stop=False,
                                             skip_group_check=True)
                            last = nc.tensor.matmul(bank[6 + c][rows, at], K, V, start=False, stop=True,
                                                    skip_group_check=True)
                    last.then_inc(sem("chunk_terms"), 1)
            pe.wait_ge(*nth("chunk_terms_read", 8))
            for c in range(1, NCH):
                pe.wait_ge(*nth("state", 2 * c))
                if c > 1:
                    pe.wait_ge(*nth("walk_read", 2 * (c - 1)))
                at = slice(c * C, (c + 1) * C)
                for e in range(2):
                    rows = slice(64 * e, 64 * e + 64)
                    if c < NCH - 1:
                        for m in range(4):
                            last = nc.tensor.matmul(bank[2 + e][rows, m * HD:(m + 1) * HD], pin[rows, 4 + m, at],
                                                    state[rows, c % 2, m, :], start=True, stop=True,
                                                    skip_group_check=True)
                        last.then_inc(sem("state_product"), 1)
                for e in range(2):
                    rows = slice(64 * e, 64 * e + 64)
                    for m in range(4):
                        last = nc.tensor.matmul(bank[e][rows, m * HD:(m + 1) * HD], state[rows, c % 2, m, :],
                                                pin[rows, m, at], start=True, stop=True, skip_group_check=True)
                    last.then_inc(sem("walk_y"), 1)
            pe.wait_ge(*nth("walk_read", 2 * (NCH - 1)))
            pe.wait_ge(*nth("g2_in", 16))
            for m in range(4):
                if m:
                    pe.wait_ge(*nth("gn_out", m))
                nc.tensor.matmul(bank[4][:, :], head_ones2, yl[:, m, :], start=True, stop=True)\
                    .then_inc(sem("gn_sum"), 1)
                nc.tensor.matmul(bank[6][:, :], g2[:, m * P:(m + 1) * P], pin[:, 13, :], start=True, stop=True)\
                    .then_inc(sem("gn_gate"), 1)
                pe.wait_ge(*nth("gn_sq", m + 1))
                nc.tensor.matmul(bank[5][:, :], head_ones2, sq[:, 1, :], start=True, stop=True)\
                    .then_inc(sem("gn_var"), 1)

            pe.wait_ge(*nth("gn_out", 4))
            pe.wait_ge(*nth("o_ready", KD))

            def merge(i, first):
                for u in range(4):
                    if not (first and u < 2):
                        pe.wait_ge(*nth("m_ready", 4 * i + u - 1))
                    for j in range(3):
                        v = FIRST["merge"] + 3 * u + j
                        b = 4 * (u % 2) + j
                        if j < 2:
                            last = chunk(12 * i + v, v % RING, 0, KD, h_hi, h_lo, bank[b][:, :], True, True)
                        else:
                            chunk(12 * i + v, v % RING, 0, 4, o_hi, o_lo, bank[b][:, :], True, True)
                            last = chunk(12 * i + v, v % RING, 4, 8, o_hi, o_lo, bank[b + 1][:, :], True, True, w0=0)
                        last.then_inc(sem("w_used"), 1)
            merge(0, True)
            merge(1, False)
            pe.wait_ge(*nth("m_ready", KD))
            project("w_out_2", FIRST["w_out_2"], KD, "conv_x_ready", h_ready=False, hi=m_hi, lo=m_lo)

            sum_squares("conv", KD, "conv_in_sq", "conv_in_sq_used")
            ffn_up("conv", FIRST["conv_up"])
            ffn_down("conv", FIRST["conv_down"], "end_x_ready")
            pe.wait_ge(*nth("end_x_ready", KD))
            for n in range(NT):
                for h in range(2):
                    for k in range(4):
                        last = nc.tensor.transpose(bank[2 * n + h][:, k * P:(k + 1) * P],
                                                   xT[:, 4 * h + k, n * P:(n + 1) * P], ident)
                    last.then_inc(sem("out_turned"), 1)

        @block.scalar
        def _(act):
            def inv_rms(tag, ready, count, n=D):
                act.wait_ge(*nth(ready, count))
                nc.scalar.activation(rstd[:, :], bank[0][:, :], ACT.Ln, bias=param("eps"), scale=1.0 / n)\
                    .then_inc(sem(tag + "_ln"), 1)
                act.wait_ge(*nth(tag + "_ln", 1))
                nc.scalar.activation(rstd[:, :], rstd[:, :], ACT.Exp, scale=-0.5).then_inc(sem(tag + "_rstd"), 1)

            def pre_norm(tag, x_ready, count=None, src=xT, k0=0, n=KD):
                for k in range(n):
                    act.wait_ge(*nth(x_ready, k + 1 if count is None else count))
                    if k >= 2:
                        act.wait_ge(*nth(tag + "_in_sq_used", k - 1))
                    nc.scalar.activation(sq[:, k % 2, :], src[:, k0 + k, :], ACT.Square)\
                        .then_inc(sem(tag + "_in_sq"), 1)
                inv_rms(tag + "_in", tag + "_in_sq_used", n, n * P)

            def ffn_up(tag):
                def body(i, first):
                    for u in range(2):
                        act.wait_ge(*nth("w_used", FIRST[tag + "_up"] + 4 * i + 2 * u + 1))
                        if not first:
                            act.wait_ge(*nth(tag + "_pair_read", 2 * i + u - 1))
                        nc.scalar.activation(tmp[:, u, :], bank[2 * u][:, :], ACT.Silu).then_inc(sem(tag + "_silu"), 1)
                body(0, True)
                with act.Fori(1, KF // 2) as i:
                    body(i, False)

            def copy_out(tag, c0, per, y):
                for m in range(KD):
                    act.wait_ge(*nth("w_used", c0 + per * (m + 1)))
                    if m >= 2:
                        act.wait_ge(*nth(tag + "_acc", m - 1))
                    nc.scalar.activation(sq[:, m % 2, :], bank[4 + m % 4][:, :], ACT.Square).then_inc(sem(tag + "_sq"), 1)
                    nc.scalar.activation(y[:, m, :], bank[4 + m % 4][:, :], ACT.Copy).then_inc(sem(tag + "_y_read"), 1)

            act.wait_ge(*nth("params_in", 16))
            pre_norm("ffn1", "start_x_ready")
            ffn_up("ffn1")
            copy_out("ffn1", FIRST["ffn1_down"], 3, yT)
            inv_rms("ffn1_post", "ffn1_post_sum", 1)

            pre_norm("mix", "ffn1_x_ready")
            act.wait_ge(*nth("angle_step", 10))
            nc.scalar.activation(sin_t[:, :], ang[:, 0, :], ACT.Sin).then_inc(sem("sine"), 1)
            nc.scalar.activation(cos_t[:, :], ang[:, 2, :], ACT.Sin, bias=param("half_pi"), scale=-1.0)\
                .then_inc(sem("sine"), 1)
            for m in range(10):
                act.wait_ge(*nth("w_used", FIRST["w_in"] + m + 1))
                nc.scalar.activation(z[:, m, :], bank[4 + m % 4][:, :], ACT.Copy).then_inc(sem("z_read"), 1)
            act.wait_ge(*nth("v_turned", 1))
            nc.scalar.activation(v_tok[:, :, :].rearrange("p n c -> p (n c)"), bank[4][:, :], ACT.Copy)\
                .then_inc(sem("v_read"), 1)
            units = [(n, g) for n in range(NT) for g in range(2)]

            def exps(n, g, unit):
                width = (2 if n else 1) * P
                act.wait_ge(*nth("swa_masked", 4 * (unit + 1)))
                for h in range(4):
                    s = sc[:, unit % 2, h, 0:width]
                    nc.scalar.activation(s, s, ACT.Exp, bias=small[:, unit % 2, 0, h:h + 1], scale=-1.0,
                                         accum_out=small[:, unit % 2, 1, h:h + 1]).then_inc(sem("swa_exp"), 1)
                act.wait_ge(*nth("swa_sink_arg", unit + 1))
                nc.scalar.activation(small[:, unit % 2, 2, :], small[:, unit % 2, 2, :], ACT.Exp)\
                    .then_inc(sem("swa_sink_exp"), 1)

            def copies(n, g, unit):
                act.wait_ge(*nth("swa_turned", unit + 1))
                if unit:
                    act.wait_ge(*nth("swa_out", unit))
                for b in range(2 if n else 1):
                    last = nc.scalar.activation(pT[:, b, :, :].rearrange("p h t -> p (h t)"), bank[4 + b][:, :],
                                                ACT.Copy)
                last.then_inc(sem("swa_turned_read"), 1)

            def store_out(n, g, unit):
                act.wait_ge(*nth("swa_out", unit + 1))
                nc.scalar.activation(mixed[:, 4 + 2 * g:6 + 2 * g, n * P:(n + 1) * P],
                                     bank[6][:, 0:2 * P].rearrange("p (i t) -> p i t", i=2), ACT.Copy)\
                    .then_inc(sem("swa_out_read"), 1)

            exps(*units[0], 0)
            for u, (n, g) in enumerate(units):
                copies(n, g, u)
                if u + 1 < len(units):
                    exps(*units[u + 1], u + 1)
                store_out(n, g, u)
            pre_norm("pool", "pooled", 4, src=mixed, n=4)
            act.wait_ge(*nth("pool_h32", 8))
            pre_norm("attn", "swa_out_read", len(units), src=mixed, k0=4, n=4)
            copy_out("wout", FIRST["w_out"], 1, mixed)
            inv_rms("wout_post", "wout_post_sum", 1)

            pre_norm("ffn2", "wout_x_ready")
            ffn_up("ffn2")
            copy_out("ffn2", FIRST["ffn2_down"], 3, yT)
            inv_rms("ffn2_post", "ffn2_post_sum", 1)

            pre_norm("nsa", "ffn2_x_ready")
            for m in range(11):
                act.wait_ge(*nth("w_used", FIRST["nsa"] + m + 1))
                nc.scalar.activation(zn[:, m, :], bank[4 + m % 4][:, :], ACT.Copy).then_inc(sem("zn_read"), 1)
            act.wait_ge(*nth("zn_read", 11))
            nc.scalar.activation(reverse(oA[0:24, 0, :]), by_tile(zn[0:24, 10, :]), ACT.Sigmoid)\
                .then_inc(sem("gates"), 1)
            def head_rms(i, width=S):
                act.wait_ge(*nth("head_sum", i + 1))
                if i >= 2:
                    act.wait_ge(*nth("head_rstd_used", i - 1))
                nc.scalar.activation(tmp[:, i % 2, 0:width], bank[i % 2][:, 0:width], ACT.Ln, bias=param("eps"),
                                     scale=1.0 / HD).then_inc(sem("head_ln"), 1)
                act.wait_ge(*nth("head_ln", i + 1))
                nc.scalar.activation(tmp[:, i % 2, 0:width], tmp[:, i % 2, 0:width], ACT.Exp, scale=-0.5)\
                    .then_inc(sem("head_rstd"), 1)

            for i in range(6):
                nc.scalar.activation(sq[:, i % 2, :], zn[:, i if i < 2 else i + 4, :], ACT.Square)\
                    .then_inc(sem("head_sq"), 1)
                if i:
                    head_rms(i - 1)
            head_rms(5)
            for v in range(2):
                act.wait_ge(*nth("gelu_arg", v + 1))
                nc.scalar.activation(hid2[:, :, 0:2 * NCMP], hid2[:, :, 0:2 * NCMP], ACT.Tanh, scale=math.sqrt(2.0 / math.pi))\
                    .then_inc(sem("gelu_tanh"), 1)
                if v == 0:
                    act.wait_ge(*nth("nsa_read", 15))
                    nc.scalar.activation(sq[:, 0, 0:2 * NCMP], kcn[:, :], ACT.Square).then_inc(sem("head_sq"), 1)
                    head_rms(6, 2 * NCMP)

            def nsa_exps(n, g, unit):
                for i in range(10):
                    act.wait_ge(*nth("nsa_masked", 10 * unit + i + 1))
                    if i < 8:
                        s, c = E[:, unit % 2, i, 0:(n + 1) * P], 4 + i
                        nc.scalar.activation(s, s, ACT.Exp, bias=stat[:, unit % 2, 0, c:c + 1], scale=-1.0,
                                             accum_out=stat[:, unit % 2, 1, c:c + 1]).then_inc(sem("nsa_exp"), 1)
                    else:
                        for k in range(2):
                            c = 2 * k + i - 8
                            s = Ec[:, unit % 2, c, 0:8 * n + 7]
                            nc.scalar.activation(s, s, ACT.Exp, bias=stat[:, unit % 2, 0, c:c + 1], scale=-1.0,
                                                 accum_out=stat[:, unit % 2, 1, c:c + 1])\
                                .then_inc(sem("nsa_exp"), 1)

            turn = [0]

            def nsa_copies(n, g, unit):
                items = 2 * (n + 1) + 1
                for x in range(items):
                    k = turn[0] + x
                    act.wait_ge(*nth("nsa_turned", k + 1))
                    if k >= 2:
                        act.wait_ge(*nth("p2T_used", k - 1))
                    rows = 8 * n + 7 if x == items - 1 else P
                    nc.scalar.activation(p2T[0:rows, k % 2, :, :].rearrange("p h t -> p (h t)"),
                                         bank[4 + k % 2][0:rows, :], ACT.Copy).then_inc(sem("p2T_ready"), 1)
                turn[0] += items
                act.wait_ge(*nth("p2T_used", turn[0]))
                nc.scalar.activation(oA[:, 2 * g:2 * g + 2, n * P:(n + 1) * P],
                                     bank[6 + unit % 2][:, 0:2 * P].rearrange("p (i t) -> p i t", i=2), ACT.Copy)\
                    .then_inc(sem("nsa_out_read"), 1)

            nsa_exps(*units[0], 0)
            for u, (n, g) in enumerate(units):
                if u + 1 < len(units):
                    nsa_exps(*units[u + 1], u + 1)
                nsa_copies(n, g, u)

            act.wait_ge(*nth("oA_out", 16))
            for m in range(14):
                act.wait_ge(*nth("w_used", FIRST["rwkv"] + m + 1))
                nc.scalar.activation(pin[:, m, :], bank[4 + m % 4][:, :], ACT.Copy).then_inc(sem("pin_read"), 1)
            act.wait_ge(*nth("mixed_in", 2))
            nc.scalar.activation(pin[:, 13, :], pin[:, 13, :], ACT.Sigmoid).then_inc(sem("gate_in"), 1)
            nc.scalar.activation(pin[0:64, 12, :], pin[0:64, 12, :], ACT.Tanh).then_inc(sem("lora_in"), 1)
            T = [mats[:, i, :] for i in range(4)] + [x[:, :, :].rearrange("p a b -> p (a b)") for x in (Dm, DT, X, OT)]
            for m in range(4):
                act.wait_ge(*nth("lora", m + 1))
                for b in range(2):
                    last = nc.scalar.activation(T[b], bank[b][:, :], ACT.Sigmoid, bias=param("a0" if b else "w0", m))
                last.then_inc(sem("lora_read"), 1)
                act.wait_ge(*nth("kk", m + 1))
                if m:
                    act.wait_ge(*nth("rw_head_sum", 2 * m))
                nc.scalar.activation(sq[:, 0, :], T[4], ACT.Square).then_inc(sem("rw_square"), 1)
                act.wait_ge(*nth("cumulative", m + 1))
                nc.scalar.activation(T[5], T[2], ACT.Exp, scale=-KAPPA).then_inc(sem("decays"), 1)
                nc.scalar.activation(T[6], T[2], ACT.Exp, scale=KAPPA).then_inc(sem("decays"), 1)
                nc.scalar.activation(T[3], T[3], ACT.Exp, scale=-KAPPA).then_inc(sem("decays"), 1)
                act.wait_ge(*nth("kk_sum", m + 1))
                nc.scalar.activation(tmp[:, 0, :], tmp[:, 0, :], ACT.Ln, scale=65536.0).then_inc(sem("kk_ln"), 1)
                act.wait_ge(*nth("kk_ln", m + 1))
                nc.scalar.activation(tmp[:, 0, :], tmp[:, 0, :], ACT.Exp, bias=param("ln_256"), scale=-0.5)\
                    .then_inc(sem("kk_rstd"), 1)
                for b, to in enumerate((At, Bt, Kt, Vt)):
                    act.wait_ge(*nth("rw_turned", 4 * m + b + 1))
                    nc.scalar.activation(to[:, :, :].rearrange("p a b -> p (a b)"), bank[4 + b][:, :], ACT.Copy)\
                        .then_inc(sem("rw_tok"), 1)
                for half in range(2):
                    r = 2 * m + half
                    for k in range(1, 6):
                        act.wait_ge(*nth("level_x", 5 * r + k))
                        nc.scalar.activation(X[:, :, :].rearrange("p a b -> p (a b)"), bank[5][:, :], ACT.Copy)\
                            .then_inc(sem("level_x_read"), 1)
                    act.wait_ge(*nth("akv", r + 1))
                    nc.scalar.activation(AkV[:, :, :].rearrange("p a b -> p (a b)"), bank[0][:, 0:4 * HD], ACT.Copy)\
                        .then_inc(sem("akv_read"), 1)
                    act.wait_ge(*nth("ug", r + 1))
                    nc.scalar.activation(UG[:, :, :].rearrange("p a b -> p (a b)"), bank[1][:, :], ACT.Copy)\
                        .then_inc(sem("ug_read"), 1)
            for m in range(4):
                act.wait_ge(*nth("gn_centred", m + 1))
                nc.scalar.activation(sq[:, 1, :], yl[:, m, :], ACT.Square).then_inc(sem("gn_sq"), 1)
                act.wait_ge(*nth("gn_var", m + 1))
                nc.scalar.activation(tmp[:, 0, :], bank[5][:, :], ACT.Ln, bias=param("gn_eps"), scale=1.0 / HD)\
                    .then_inc(sem("gn_ln"), 1)
                act.wait_ge(*nth("gn_ln", m + 1))
                nc.scalar.activation(tmp[:, 0, :], tmp[:, 0, :], ACT.Exp, scale=-0.5).then_inc(sem("gn_rstd"), 1)

            for m in range(KD):
                c = FIRST["merge"] + 3 * m
                if m:
                    act.wait_ge(*nth("gates_used", m))
                for j in range(2):
                    act.wait_ge(*nth("w_used", c + j + 1))
                    nc.scalar.activation(tmp[:, j, :], bank[4 * (m % 2) + j][:, :], ACT.Sigmoid)\
                        .then_inc(sem("merge_gate"), 1)

            pre_norm("conv", "conv_x_ready")
            with act.Fori(0, KF) as p:
                act.wait_ge(*nth("conv_pair_read", p + 1))
                nc.scalar.activation(sq[:, 0, :], tmp[:, 1, :], ACT.Silu).then_inc(sem("conv_silu"), 1)

        @block.vector
        def _(dve):
            def pre_norm(tag, gain, ready, src=xT, k0=0, n=KD, done=0):
                dve.wait_ge(*nth(tag + "_in_rstd", 1))
                for k in range(n):
                    at = k0 + k
                    for to, name in ((h_hi[:, at, :], "_h32"), (tmp[:, k % 2, :], "_h32")):
                        nc.vector.scalar_tensor_tensor(to, src[:, at, :], param(gain, k), rstd[:, :], ALU.mult,
                                                       ALU.mult).then_inc(sem(tag + name), 1)
                    dve.wait_ge(*nth(tag + "_h32", 2 * k + 2))
                    nc.vector.tensor_tensor(h_lo[:, at, :], tmp[:, k % 2, :], h_hi[:, at, :].bitcast(F32),
                                            ALU.subtract).then_inc(sem(ready), 1)

            def ffn_up(tag):
                def body(i, first):
                    for u in range(2):
                        p = 2 * i + u
                        dve.wait_ge(*nth(tag + "_silu", p + 1))
                        dve.wait_ge(*nth("w_used", FIRST[tag + "_up"] + 4 * i + 2 * u + 2))
                        hi, lo = (a[:, bass.ds(p, 1), :].rearrange("q a t -> q (a t)") for a in (a_hi, a_lo))
                        nc.vector.tensor_tensor(hi, tmp[:, u, :], bank[2 * u + 1][:, :], ALU.mult)\
                            .then_inc(sem(tag + "_a32"), 1)
                        nc.vector.tensor_tensor(sq[:, u, :], tmp[:, u, :], bank[2 * u + 1][:, :], ALU.mult)\
                            .then_inc(sem(tag + "_pair_read"), 1)
                        dve.wait_ge(*nth(tag + "_a32", p + 1))
                        dve.wait_ge(*nth(tag + "_pair_read", p + 1))
                        nc.vector.tensor_tensor(lo, sq[:, u, :], hi.bitcast(F32), ALU.subtract)\
                            .then_inc(sem(tag + "_a_ready"), 1)
                with dve.Fori(0, KF // 2) as i:
                    body(i, False)

            def sum_out(tag):
                nc.vector.memset(acc[:, :], 0.0).then_inc(sem(tag + "_acc_zero"), 1)
                dve.wait_ge(*nth(tag + "_acc_zero", 1))
                for m in range(KD):
                    dve.wait_ge(*nth(tag + "_sq", m + 1))
                    if m:
                        dve.wait_ge(*nth(tag + "_acc", m))
                    nc.vector.tensor_tensor(acc[:, :], acc[:, :], sq[:, m % 2, :], ALU.add).then_inc(sem(tag + "_acc"), 1)

            def post_norm(tag, gain, factor, y):
                dve.wait_ge(*nth(tag + "_post_rstd", 1))
                dve.wait_ge(*nth(tag + "_y_read", KD))
                for k in range(KD):
                    nc.vector.scalar_tensor_tensor(tmp[:, k % 2, :], y[:, k, :], param(gain, k), rstd[:, :],
                                                   ALU.mult, ALU.mult).then_inc(sem(tag + "_scaled"), 1)
                    dve.wait_ge(*nth(tag + "_scaled", k + 1))
                    nc.vector.scalar_tensor_tensor(xT[:, k, :], tmp[:, k % 2, :], factor, xT[:, k, :],
                                                   ALU.mult, ALU.add).then_inc(sem(tag + "_x_ready"), 1)

            for k in range(KD):
                dve.wait_ge(*nth("x_turned", k + 1))
                nc.vector.tensor_copy(xT[:, k, :], bank[k][:, :]).then_inc(sem("start_x_ready"), 1)
            dve.wait_ge(*nth("params_in", 16))
            sinks = prm[:, COL["sinks"]:COL["sinks"] + NH]
            nc.vector.tensor_scalar(sinks, sinks, -1.0, None, ALU.mult).then_inc(sem("sinks_step"), 1)
            dve.wait_ge(*nth("sinks_step", 1))
            pre_norm("ffn1", "ffn1_pre", "ffn1_h_ready")
            ffn_up("ffn1")
            sum_out("ffn1")
            post_norm("ffn1", "ffn1_post", 0.5, yT)

            pre_norm("mix", "mix_pre", "mix_h_ready")
            TURN = (6.28125, 0.0019350051879882812, 3.0199159819e-7)
            step = [0]

            def link(ins):
                step[0] += 1
                ins.then_inc(sem("angle_step"), 1)
                dve.wait_ge(*nth("angle_step", step[0]))

            a0, a1, a2 = (ang[:, i, :] for i in range(3))
            dve.wait_ge(*nth("positions_in", 16))
            link(nc.vector.tensor_copy(a0, pos[:, :]))
            link(nc.vector.tensor_scalar(a0, a0, param("inv_freq"), None, ALU.mult))
            link(nc.vector.tensor_scalar(a1, a0, 1.0 / (2.0 * math.pi), ROUND, ALU.mult, ALU.add))
            link(nc.vector.tensor_scalar(a1, a1, -ROUND, None, ALU.add))
            for part in TURN:
                link(nc.vector.scalar_tensor_tensor(a0, a1, -part, a0, ALU.mult, ALU.add))
            link(nc.vector.tensor_scalar(a0, a0, PI_BELOW, -PI_BELOW, ALU.min, ALU.max))
            link(nc.vector.tensor_scalar(a2, a0, -1.0, None, ALU.mult))
            link(nc.vector.tensor_tensor(a2, a2, a0, ALU.max))
            dve.wait_ge(*nth("sine", 2))
            nc.vector.tensor_scalar(sin_t[:, :], sin_t[:, :], param("rot_sign"), None, ALU.mult)\
                .then_inc(sem("sine_step"), 1)
            dve.wait_ge(*nth("sine_step", 1))
            for i in range(6):
                dve.wait_ge(*nth("rot_done", i + 1))
                if i < 2:
                    b, r, to, factor = bank[2 * i][:, :], bank[2 * i + 1][:, :], k_rot[:, i, :], 1.0
                else:
                    b, to, factor = z[:, i, :], q_rot[:, i - 2, :], -0.125
                    r = bank[(i - 2) % 2 if i < 4 else i - 2][:, :]
                if i:
                    dve.wait_ge(*nth("rot_used", i))
                nc.vector.scalar_tensor_tensor(tmp[:, 0, :], b, factor, cos_t[:, :], ALU.mult, ALU.mult)\
                    .then_inc(sem("rot_step"), 1)
                nc.vector.scalar_tensor_tensor(tmp[:, 1, :], r, factor, sin_t[:, :], ALU.mult, ALU.mult)\
                    .then_inc(sem("rot_step"), 1)
                dve.wait_ge(*nth("rot_step", 2 * i + 2))
                nc.vector.tensor_tensor(to, tmp[:, 0, :], tmp[:, 1, :], ALU.add).then_inc(sem("rot_used"), 1)

            nc.vector.memset(win[:, :, 0:PAD], 0.0).then_inc(sem("win_step"), 1)
            dve.wait_ge(*nth("win_step", 1))
            dve.wait_ge(*nth("z_read", 10))
            dve.wait_ge(*nth("mix_const_in", 16))
            adds = 1
            for g in range(4):
                if g:
                    dve.wait_ge(*nth("pool_product", g))
                nc.vector.tensor_copy(win[:, 0, PAD:], z[:, 6 + g, :]).then_inc(sem("win_step"), 1)
                adds += 1
                dve.wait_ge(*nth("win_step", adds))
                src = 0
                for j in range(g + 1):
                    k = 1 << j
                    nc.vector.tensor_tensor(win[:, 1 - src, PAD:], win[:, src, PAD:], win[:, src, PAD - k:PAD + S - k],
                                            ALU.add).then_inc(sem("win_step"), 1)
                    src = 1 - src
                    adds += 1
                    dve.wait_ge(*nth("win_step", adds))
                u = z[:, 6 + g, :]
                nc.vector.tensor_tensor(win[:, 1 - src, PAD:2 * PAD], win[:, src, PAD:2 * PAD], inv_count[:, g, :],
                                        ALU.mult).then_inc(sem("win_step"), 1)
                adds += 1
                dve.wait_ge(*nth("win_step", adds))
                nc.vector.tensor_tensor(dif[:, 0:PAD], win[:, 1 - src, PAD:2 * PAD], u[:, 0:PAD], ALU.subtract)\
                    .then_inc(sem("win_step"), 1)
                adds += 1
                nc.vector.scalar_tensor_tensor(dif[:, PAD:], win[:, src, 2 * PAD:], 1.0 / (2 << g), u[:, PAD:],
                                               ALU.mult, ALU.subtract).then_inc(sem("pool_diff"), 1)
                dve.wait_ge(*nth("pool_product", g + 1))
                nc.vector.tensor_scalar(mixed[:, g, :], bank[7][:, :], param("pool_scale", g), None, ALU.mult)\
                    .then_inc(sem("pooled"), 1)

            units = [(n, g) for n in range(NT) for g in range(2)]

            def mask(n, g, unit):
                width = (2 if n else 1) * P
                dve.wait_ge(*nth("swa_scores", 2 * (unit + 1)))
                if unit >= 2:
                    dve.wait_ge(*nth("swa_turned", unit - 1))
                for h in range(4):
                    e, i = h % 2, h // 2
                    nc.vector.tensor_tensor_reduce(sc[:, unit % 2, h, 0:width],
                                                   bank[2 * (unit % 2) + e][:, i * width:(i + 1) * width],
                                                   band[:, 2 * P - width:], 1.0, param("sinks", 4 * g + h),
                                                   ALU.add, ALU.min, small[:, unit % 2, 0, h:h + 1])\
                        .then_inc(sem("swa_masked"), 1)
                dve.wait_ge(*nth("swa_masked", 4 * (unit + 1)))
                c = COL["sinks"] + 4 * g
                nc.vector.tensor_tensor(small[:, unit % 2, 2, :], small[:, unit % 2, 0, :], prm[:, c:c + 4],
                                        ALU.subtract).then_inc(sem("swa_sink_arg"), 1)

            def normalise(n, g, unit):
                width = (2 if n else 1) * P
                sm = small[:, unit % 2, :, :]
                dve.wait_ge(*nth("swa_sink_exp", unit + 1))
                dve.wait_ge(*nth("swa_exp", 4 * (unit + 1)))
                nc.vector.tensor_tensor(sm[:, 3, :], sm[:, 1, :], sm[:, 2, :], ALU.add).then_inc(sem("swa_step"), 1)
                dve.wait_ge(*nth("swa_step", 2 * unit + 1))
                nc.vector.reciprocal(sm[:, 3, :], sm[:, 3, :]).then_inc(sem("swa_step"), 1)
                dve.wait_ge(*nth("swa_step", 2 * unit + 2))
                for h in range(4):
                    nc.vector.tensor_scalar(sc[:, unit % 2, h, 0:width], sc[:, unit % 2, h, 0:width],
                                            sm[:, 3, h:h + 1], None, ALU.mult).then_inc(sem("swa_probs"), 1)

            mask(*units[0], 0)
            for u, (n, g) in enumerate(units):
                if u + 1 < len(units):
                    mask(*units[u + 1], u + 1)
                normalise(n, g, u)
            pre_norm("pool", "g_pool", "wout_h_ready", src=mixed, n=4)
            pre_norm("attn", "g_attn", "wout_h_ready", src=mixed, k0=4, n=4)
            sum_out("wout")
            post_norm("wout", "mix_post", 1.0, mixed)

            pre_norm("ffn2", "ffn2_pre", "ffn2_h_ready")
            ffn_up("ffn2")
            sum_out("ffn2")
            post_norm("ffn2", "ffn2_post", 0.5, yT)

            pre_norm("nsa", "attn_norm", "nsa_h_ready")
            dve.wait_ge(*nth("nsa_small_in", 8 * 16))
            nc.vector.memset(rel[32:33, :], 1.0).then_inc(sem("rel_one"), 1)
            job = [0]

            def job_bank():
                job[0] += 1
                dve.wait_ge(*nth("nsa_job", job[0]))
                return bank[2 + (job[0] - 1) % 2]

            for v in range(2):
                nc.vector.tensor_copy(v2_tok[:, v, :, :].rearrange("p n c -> p (n c)"), job_bank()[:, :])\
                    .then_inc(sem("nsa_read"), 1)
            for v in range(2):
                for g in range(2):
                    b = job_bank()[:, :].rearrange("p (t o) -> p o t", o=2)
                    for o in range(2):
                        last = nc.vector.tensor_copy(pair[64 * o:64 * o + 64, v, g, :], b[64 * o:64 * o + 64, o, :])
                    last.then_inc(sem("nsa_read"), 1)
            for a, b in ((0, S), (S, 5 * P)):
                nc.vector.tensor_copy(rv[:, a:b], job_bank()[0:NH, 0:b - a]).then_inc(sem("nsa_read"), 1)
            nc.vector.tensor_copy(gate_tok[:, :, :].rearrange("p n c -> p (n c)"), job_bank()[:, 0:NT * 24])\
                .then_inc(sem("nsa_read"), 1)
            for i in range(2):
                dve.wait_ge(*nth("head_rstd", i + 1))
                nc.vector.tensor_tensor(zn[:, i, :], zn[:, i, :], tmp[:, i, :], ALU.mult)\
                    .then_inc(sem("head_rstd_used"), 1)
            for i in range(2, 6):
                dve.wait_ge(*nth("head_rstd", i + 1))
                nc.vector.scalar_tensor_tensor(reverse(qn[:, i - 2, :]), by_tile(zn[:, i + 4, :]), param("q_norm"),
                                               by_tile(tmp[:, i % 2, :]),
                                               ALU.mult, ALU.mult).then_inc(sem("head_rstd_used"), 1)
            for c in range(4):
                nc.vector.tensor_scalar(kd[:, c, :], job_bank()[:, :], param("k_norm"), -HD ** -0.5, ALU.mult,
                                        ALU.mult).then_inc(sem("nsa_read"), 1)
            chain = [0]

            def link(ins):
                chain[0] += 1
                ins.then_inc(sem("cmp_step"), 1)
                dve.wait_ge(*nth("cmp_step", chain[0]))

            for v in range(2):
                w = 2 * NCMP
                b = job_bank()[:, 0:2 * 64].rearrange("p (h c) -> p h c", h=2)
                nc.vector.tensor_copy(hid2[:, :, 0:w + 1], b[:, :, 0:w + 1]).then_inc(sem("nsa_read"), 1)
                dve.wait_ge(*nth("nsa_read", job[0]))
                for h in range(2):
                    link(nc.vector.tensor_scalar(hid[:, h, 0:w], hid2[:, h, 0:w], hid2[:, h, w:w + 1], None, ALU.add))
                x, t = hid[:, :, 0:w], hid2[:, :, 0:w]
                link(nc.vector.tensor_tensor(t, x, x, ALU.mult))
                link(nc.vector.scalar_tensor_tensor(t, t, 0.044715, x, ALU.mult, ALU.mult))
                nc.vector.tensor_tensor(t, t, x, ALU.add).then_inc(sem("gelu_arg"), 1)
                dve.wait_ge(*nth("gelu_tanh", v + 1))
                link(nc.vector.scalar_tensor_tensor(t, t, 1.0, x, ALU.add, ALU.mult))
                nc.vector.tensor_scalar(x, t, 0.5, None, ALU.mult).then_inc(sem("gelu"), 1)
                dve.wait_ge(*nth("gelu", v + 1))
                if v == 0:
                    nc.vector.tensor_copy(kcn[:, :], job_bank()[:, 0:w]).then_inc(sem("nsa_read"), 1)
                    dve.wait_ge(*nth("head_rstd", 7))
                    link(nc.vector.tensor_tensor(kcn[:, :], kcn[:, :], tmp[:, 0, 0:w], ALU.mult))
                    nc.vector.tensor_scalar(kcn[:, :], kcn[:, :], param("k_norm"), -HD ** -0.5, ALU.mult, ALU.mult)\
                        .then_inc(sem("kc_normed"), 1)
                else:
                    nc.vector.tensor_copy(vct[:, :, :].rearrange("n g d -> n (g d)"), job_bank()[0:NCMP, 0:2 * HD])\
                        .then_inc(sem("nsa_read"), 1)
            dve.wait_ge(*nth("toeplitz_in", 16))

            def nsa_mask(n, g, unit):
                if unit >= 2:
                    dve.wait_ge(*nth("nsa_out_read", unit - 1))
                for i in range(10):
                    b = bank[i % 4] if unit % 2 == 0 else bank[(i + 2) % 4]
                    dve.wait_ge(*nth("nsa_scores", 10 * unit + i + 1))
                    if i < 8:
                        nc.vector.tensor_tensor_reduce(E[:, unit % 2, i, 0:(n + 1) * P], b[:, 0:(n + 1) * P],
                                                       toeplitz[:, 4 * g + i % 4, (3 - n) * P:], 1.0, 3.0e38,
                                                       ALU.add, ALU.min, stat[:, unit % 2, 0, 4 + i:5 + i])\
                            .then_inc(sem("nsa_masked"), 1)
                    else:
                        c0 = 31 + (3 - n) * P
                        for k in range(2):
                            h = 2 * k + i - 8
                            last = nc.vector.tensor_tensor_reduce(
                                Ec[:, unit % 2, h, 0:8 * n + 7], b[:, k * 32:k * 32 + 8 * n + 7],
                                toeplitz[:, 4 * g + h, c0:c0 + 16 * (8 * n + 6) + 1:16], 1.0, 3.0e38,
                                ALU.add, ALU.min, stat[:, unit % 2, 0, h:h + 1])
                        last.then_inc(sem("nsa_masked"), 1)

            wstep = [0]

            def nsa_weights(n, g, unit):
                def link(ins):
                    wstep[0] += 1
                    ins.then_inc(sem("nsa_weight_step"), 1)
                    dve.wait_ge(*nth("nsa_weight_step", wstep[0]))
                st = stat[:, unit % 2, :, :]
                dve.wait_ge(*nth("nsa_exp", 12 * (unit + 1)))
                link(nc.vector.reciprocal(st[:, 2, :], st[:, 1, :]))
                gates = gate_tok[:, n, 12 * g:12 * g + 12].rearrange("p (h b) -> p b h", b=3)
                link(nc.vector.tensor_tensor(st[:, 2, :].rearrange("p (b h) -> p b h", b=3),
                                             st[:, 2, :].rearrange("p (b h) -> p b h", b=3), gates, ALU.mult))
                if n == 0:
                    link(nc.vector.tensor_scalar(st[:, 2, 0:4], st[:, 2, 0:4], param("sees_block"), None, ALU.mult))
                for h in range(4):
                    s = Ec[:, unit % 2, h, 0:8 * n + 7]
                    nc.vector.tensor_scalar(s, s, st[:, 2, h:h + 1], None, ALU.mult)
                for i in range(8):
                    s = E[:, unit % 2, i, 0:(n + 1) * P]
                    last = nc.vector.tensor_scalar(s, s, st[:, 2, 4 + i:5 + i], None, ALU.mult)
                last.then_inc(sem("nsa_weighed"), 1)

            nsa_mask(*units[0], 0)
            for u, (n, g) in enumerate(units):
                if u + 1 < len(units):
                    nsa_mask(*units[u + 1], u + 1)
                nsa_weights(n, g, u)

            dve.wait_ge(*nth("rwkv_small_in", 4 * 16))
            steps = [0]

            def link(ins):
                steps[0] += 1
                ins.then_inc(sem("rw_step"), 1)
                dve.wait_ge(*nth("rw_step", steps[0]))

            for i, c in enumerate((12, 13, *range(12))):
                dve.wait_ge(*nth("pin_read", c + 1))
                if i:
                    dve.wait_ge(*nth("mixed_in", i))
                x, d = pin[:, c, :], tmp[:, i % 2, :]
                link(nc.vector.tensor_tensor(d[:, 1:], x[:, 0:S - 1], x[:, 1:], ALU.subtract))
                link(nc.vector.tensor_scalar(d[:, 0:1], x[:, 0:1], -1.0, None, ALU.mult))
                nc.vector.scalar_tensor_tensor(x, d, param("mu", c), x, ALU.mult, ALU.add)\
                    .then_inc(sem("mixed_in"), 1)
            T = [mats[:, i, :] for i in range(4)] + [x[:, :, :].rearrange("p a b -> p (a b)") for x in (Dm, DT, X, OT)]
            SG, RATE, CUM, PREV, KK, UPTO, INV, MOD = T
            wide = lambda x: x.rearrange("p (n t) -> p n t", n=NT)
            for m in range(4):
                dve.wait_ge(*nth("mixed_in", 14))
                r_, k_, v_ = pin[:, m, :], pin[:, 4 + m, :], pin[:, 8 + m, :]
                if m:
                    dve.wait_ge(*nth("chunk_terms_read", 2 * m))
                nc.vector.tensor_scalar(KK, k_, param("k_k", m), None, ALU.mult).then_inc(sem("kk"), 1)
                dve.wait_ge(*nth("lora_read", m + 1))
                link(nc.vector.tensor_tensor_scan(CUM, reset[:, :], SG, 0.0, ALU.mult, ALU.add))
                nc.vector.tensor_tensor(PREV, CUM, SG, ALU.subtract).then_inc(sem("cumulative"), 1)
                dve.wait_ge(*nth("rw_head_sum", 2 * m + 1))
                nc.vector.tensor_scalar(tmp[:, 0, :], bank[2][:, :], 1e-24, None, ALU.max).then_inc(sem("kk_sum"), 1)
                link(nc.vector.tensor_scalar(MOD, RATE, 1.0, param("k_a", m), ALU.subtract, ALU.mult))
                link(nc.vector.scalar_tensor_tensor(MOD, MOD, 1.0, k_, ALU.add, ALU.mult))
                nc.vector.scalar_tensor_tensor(sq[:, 1, :], r_, param("r_k", m), MOD, ALU.mult, ALU.mult)\
                    .then_inc(sem("rk_product"), 1)
                dve.wait_ge(*nth("decays", 3 * (m + 1)))
                dve.wait_ge(*nth("kk_rstd", m + 1))
                link(nc.vector.tensor_tensor(KK, KK, tmp[:, 0, :], ALU.mult))
                nc.vector.scalar_tensor_tensor(AR[:, :, 0, :], wide(KK), -1.0, wide(PREV), ALU.mult, ALU.mult)\
                    .then_inc(sem("hats"), 1)
                link(nc.vector.tensor_tensor(KK, KK, RATE, ALU.mult))
                nc.vector.tensor_tensor(Bh[:, :], KK, INV, ALU.mult).then_inc(sem("hats"), 1)
                nc.vector.tensor_tensor(Kh[:, :], MOD, INV, ALU.mult).then_inc(sem("hats"), 1)
                link(nc.vector.tensor_tensor(AR[:, :, 1, :], wide(r_), wide(UPTO), ALU.mult))
                link(nc.vector.tensor_copy(PC[:, m, :], UPTO[:, C - 1::C]))
                dve.wait_ge(*nth("rw_head_sum", 2 * m + 2))
                nc.vector.tensor_tensor(bonus[:, m, :], bank[3][:, :], v_, ALU.mult).then_inc(sem("bonus_done"), 1)
                dve.wait_ge(*nth("bonus_done", m + 1))
                for half in range(2):
                    r = 2 * m + half
                    if half == 0:
                        dve.wait_ge(*nth("hats", 3 * (m + 1)))
                    for u in range(4):
                        dve.wait_ge(*nth("rw_scores", 4 * r + u + 1))
                        link(nc.vector.tensor_tensor(mats[:, u, :], bank[u][:, :], mask4[:, :], ALU.mult))
                    eye = ident.unsqueeze(1).to_broadcast([P, 4, P])
                    for k in range(6):
                        if k > 1:
                            dve.wait_ge(*nth("level_x", 5 * r + k - 1))
                        elif k == 1:
                            dve.wait_ge(*nth("inverse", 6 * r + 1))
                        nc.vector.tensor_tensor(OT[:, :, :], mats[:, :, 0:P],
                                                level[k].unsqueeze(1).to_broadcast([P, 4, P]), ALU.mult)\
                            .then_inc(sem("level_mask"), 1)
                        if k == 0:
                            dve.wait_ge(*nth("level_mask", 6 * r + 1))
                            link(nc.vector.tensor_tensor(DT[:, :, :], OT[:, :, :], eye, ALU.add))
                            dve.wait_ge(*nth("level_turned", r + 1))
                            nc.vector.tensor_tensor(Dm[:, :, :], bank[4][:, :].rearrange("p (u t) -> p u t", u=4), eye,
                                                    ALU.add).then_inc(sem("inverse"), 1)
                        else:
                            dve.wait_ge(*nth("level_added", 5 * r + k))
                            if k < 5:
                                link(nc.vector.tensor_tensor(Dm[:, :, :], Dm[:, :, :],
                                                             bank[6][:, :].rearrange("p (u t) -> p u t", u=4), ALU.add))
                            nc.vector.tensor_tensor(DT[:, :, :], DT[:, :, :],
                                                    bank[7][:, :].rearrange("p (u t) -> p u t", u=4), ALU.add)\
                                .then_inc(sem("inverse"), 1)
                            dve.wait_ge(*nth("inverse", 6 * r + k + 1))
                    dve.wait_ge(*nth("chunk_terms", r + 1))
                    at = slice(half * 2 * P, (half + 1) * 2 * P)
                    link(nc.vector.tensor_tensor(pin[:, m, at].rearrange("p (n t) -> p n t", n=2),
                                                 bank[2][:, 0:2 * P].rearrange("p (n t) -> p n t", n=2),
                                                 AR[:, 2 * half:2 * half + 2, 1, :], ALU.add))
                    link(nc.vector.tensor_copy(yl[:, m, at], bank[3][:, 0:2 * P]))
                    for c in range(2):
                        to = pin[:, 4 + m, at].rearrange("p (n c t) -> p c n t", n=2, c=2)[:, c, :, :]
                        link(nc.vector.tensor_tensor(to, bank[4 + c][:, 0:2 * HD].rearrange("p (n t) -> p n t", n=2),
                                                     eye2.unsqueeze(1).to_broadcast([P, 2, HD]), ALU.add))
                        to = pin[:, 8 + m, at].rearrange("p (n c t) -> p c n t", n=2, c=2)[:, c, :, :]
                        last = nc.vector.tensor_copy(to, bank[6 + c][:, 0:2 * HD].rearrange("p (n t) -> p n t", n=2))
                        if c == 0:
                            link(last)
                    last.then_inc(sem("chunk_terms_read"), 1)
                    dve.wait_ge(*nth("chunk_terms_read", r + 1))
            dve.wait_ge(*nth("rw_head_sum", 8))
            for c in range(NCH):
                at = slice(c * C, (c + 1) * C)
                if c < NCH - 1:
                    for e in range(2):
                        rows = slice(64 * e, 64 * e + 64)
                        to, n_ = state[rows, (c + 1) % 2, :, :], pin[rows, 8:12, at]
                        if c:
                            dve.wait_ge(*nth("state_product", 2 * (c - 1) + e + 1))
                            if c > 1:
                                dve.wait_ge(*nth("walk_y", 2 * (c - 1)))
                            link(nc.vector.tensor_tensor(to, bank[2 + e][rows, 0:4 * HD]
                                                         .rearrange("p (m i) -> p m i", m=4), n_, ALU.add))
                            n_ = to
                        nc.vector.tensor_tensor(to, n_, PC[rows, :, c:c + 1].to_broadcast([64, 4, HD]), ALU.mult)\
                            .then_inc(sem("state"), 1)
                if c:
                    for e in range(2):
                        rows = slice(64 * e, 64 * e + 64)
                        dve.wait_ge(*nth("walk_y", 2 * (c - 1) + e + 1))
                        y = yl[rows, :, at]
                        nc.vector.tensor_tensor(y, y, bank[e][rows, 0:4 * HD].rearrange("p (m i) -> p m i", m=4),
                                                ALU.add).then_inc(sem("walk_read"), 1)
            dve.wait_ge(*nth("walk_read", 2 * (NCH - 1)))
            for m in range(4):
                dve.wait_ge(*nth("gn_sum", m + 1))
                y = yl[:, m, :]
                nc.vector.scalar_tensor_tensor(y, bank[4][:, :], -1.0 / HD, y, ALU.mult, ALU.add)\
                    .then_inc(sem("gn_centred"), 1)
                dve.wait_ge(*nth("gn_rstd", m + 1))
                link(nc.vector.scalar_tensor_tensor(y, y, param("ln_g", m), tmp[:, 0, :], ALU.mult, ALU.mult))
                link(nc.vector.scalar_tensor_tensor(y, y, param("ln_b", m), bonus[:, m, :], ALU.add, ALU.add))
                dve.wait_ge(*nth("gn_gate", m + 1))
                link(nc.vector.tensor_tensor(o_hi[:, 4 + m, :], y, bank[6][:, :], ALU.mult))
                nc.vector.tensor_tensor(y, y, bank[6][:, :], ALU.mult).then_inc(sem("gn_out"), 1)
                dve.wait_ge(*nth("gn_out", m + 1))
                nc.vector.tensor_tensor(o_lo[:, 4 + m, :], y, o_hi[:, 4 + m, :].bitcast(F32), ALU.subtract)\
                    .then_inc(sem("o_ready"), 1)
            dve.wait_ge(*nth("oA_in", 16))
            for m in range(4):
                link(nc.vector.tensor_copy(o_hi[:, m, :], oA2[:, m, :]))
                nc.vector.tensor_tensor(o_lo[:, m, :], oA2[:, m, :], o_hi[:, m, :].bitcast(F32), ALU.subtract)\
                    .then_inc(sem("o_ready"), 1)

            for m in range(KD):
                dve.wait_ge(*nth("merge_gate", 2 * (m + 1)))
                dve.wait_ge(*nth("w_used", FIRST["merge"] + 3 * (m + 1)))
                b = 4 * (m % 2)
                if m:
                    dve.wait_ge(*nth("m_ready", m))
                for j in range(2):
                    link(nc.vector.tensor_tensor(sq[:, j, :], tmp[:, j, :], bank[b + 2 + j][:, :], ALU.mult))
                nc.vector.tensor_tensor(m_hi[:, m, :], sq[:, 0, :], sq[:, 1, :], ALU.add).then_inc(sem("gates_used"), 1)
                dve.wait_ge(*nth("gates_used", m + 1))
                link(nc.vector.tensor_tensor(sq[:, 0, :], sq[:, 0, :], sq[:, 1, :], ALU.add))
                nc.vector.tensor_tensor(m_lo[:, m, :], sq[:, 0, :], m_hi[:, m, :].bitcast(F32), ALU.subtract)\
                    .then_inc(sem("m_ready"), 1)
            for m in range(KD):
                dve.wait_ge(*nth("w_used", FIRST["w_out_2"] + m + 1))
                nc.vector.tensor_tensor(xT[:, m, :], xT[:, m, :], bank[4 + m % 4][:, :], ALU.add)\
                    .then_inc(sem("conv_x_ready"), 1)

            pre_norm("conv", "ffn_norm", "conv_h_ready")

            def conv_pair(i, first):
                for u in range(2):
                    p = 2 * i + u
                    for v in range(2):
                        dve.wait_ge(*nth("w_used", FIRST["conv_up"] + 4 * i + 2 * u + v + 1))
                        b, c = bank[2 * u + v], tmp[:, v, :]
                        if v == 1 and not (first and u == 0):
                            dve.wait_ge(*nth("conv_silu", p))
                        w = [prm[:, bass.ds(p + (COL[f"conv_{x}"] + KF * v), 1)] for x in ("w0", "w1", "w2", "b")]
                        nc.vector.tensor_scalar(c, b[:, :], w[2], w[3], ALU.mult, ALU.add)\
                            .then_inc(sem("conv_step"), 1)
                        dve.wait_ge(*nth("conv_step", 4 * p + 2 * v + 1))
                        nc.vector.scalar_tensor_tensor(c[:, 1:], b[:, 0:S - 1], w[1], c[:, 1:], ALU.mult, ALU.add)\
                            .then_inc(sem("conv_step"), 1)
                        dve.wait_ge(*nth("conv_step", 4 * p + 2 * v + 2))
                        last = nc.vector.scalar_tensor_tensor(c[:, 2:], b[:, 0:S - 2], w[0], c[:, 2:], ALU.mult,
                                                              ALU.add)
                        last.then_inc(sem("conv_pair_read" if v else "conv_value"), 1)
                    hi, lo = (a[:, bass.ds(p, 1), :].rearrange("q a t -> q (a t)") for a in (a_hi, a_lo))
                    dve.wait_ge(*nth("conv_value", p + 1))
                    dve.wait_ge(*nth("conv_silu", p + 1))
                    nc.vector.tensor_tensor(hi, tmp[:, 0, :], sq[:, 0, :], ALU.mult).then_inc(sem("conv_a32"), 1)
                    nc.vector.tensor_tensor(sq[:, 1, :], tmp[:, 0, :], sq[:, 0, :], ALU.mult)\
                        .then_inc(sem("conv_a32"), 1)
                    dve.wait_ge(*nth("conv_a32", 2 * p + 2))
                    nc.vector.tensor_tensor(lo, sq[:, 1, :], hi.bitcast(F32), ALU.subtract)\
                        .then_inc(sem("conv_a_ready"), 1)
            conv_pair(0, True)
            with dve.Fori(1, KF // 2) as i:
                conv_pair(i, False)
            for m in range(KD):
                dve.wait_ge(*nth("w_used", FIRST["conv_down"] + 3 * (m + 1)))
                nc.vector.tensor_tensor(xT[:, m, :], xT[:, m, :], bank[4 + m % 4][:, :], ALU.add)\
                    .then_inc(sem("end_x_ready"), 1)
            for i in range(2 * NT):
                dve.wait_ge(*nth("out_turned", i + 1))
                nc.vector.tensor_copy(yT[:, i, :], bank[i][:, :]).then_inc(sem("out_copied"), 1)


def _layouts(inputs):
    import numpy as np
    f32 = np.float32

    def blocks(w):
        k, n = w.shape
        return w.reshape(k // P, P, n // P, P).transpose(2, 1, 0, 3).reshape(n // P, P, k)

    def pairs(w):
        b = blocks(w)
        return np.stack([b[:KF], b[KF:]], 1).reshape(2 * KF, P, D)

    def columns(v):
        return v.reshape(-1, P).T

    one = {name: (a[0] if a.shape[0] == 1 and name not in ("x", "positions") else a) for name, a in inputs.items()}
    cols = lambda name: columns(one[name].reshape(-1))
    conv_w = one["conv_w_2"]
    ch = np.arange(P)
    rope_of = ch % HD
    freq = 500000.0 ** (-(np.arange(0, 16, 2, dtype=f32)) / f32(16))
    values = {
        "ffn1_pre": cols("ffn1_pre"), "ffn1_post": cols("ffn1_post"), "mix_pre": cols("mix_pre"),
        "mix_post": cols("mix_post"), "ffn2_pre": cols("ffn2_pre"), "ffn2_post": cols("ffn2_post"),
        "attn_norm": cols("attn_norm_g_2"), "ffn_norm": cols("ffn_norm_g_2"), "pool_scale": cols("pool_scale"),
        "g_pool": cols("g_pool"), "g_attn": cols("g_attn"), "sinks": np.tile(one["sinks"], (P, 1)),
        "eps": np.full((P, 1), EPS), "half_pi": np.full((P, 1), math.pi / 2),
        "inv_freq": np.where(rope_of < 16, freq.astype(f32)[rope_of % 8], 0)[:, None],
        "rot_sign": np.where(rope_of < 8, -1, 1)[:, None],
        "q_norm": np.tile(one["q_norm_g_2"], 2)[:, None], "k_norm": np.tile(one["k_norm_g_2"], 2)[:, None],
        "sees_block": (P - 1 - ch >= 31)[:, None], "mu": cols("rwkv_mu_2"), "w0": cols("rwkv_w0_2"), "a0": cols("rwkv_a0_2"),
        "k_k": cols("rwkv_k_k_2"), "k_a": cols("rwkv_k_a_2"), "r_k": cols("rwkv_r_k_2"), "ln_g": cols("rwkv_ln_g_2"),
        "ln_b": cols("rwkv_ln_b_2"), "gn_eps": np.full((P, 1), 64e-5), "ln_256": np.full((P, 1), 8 * math.log(2)),
        "conv_b": cols("conv_b_2"), "conv_w0": columns(conv_w[0]), "conv_w1": columns(conv_w[1]),
        "conv_w2": columns(conv_w[2])}
    params = np.concatenate([values[name].astype(f32) for name, _ in PARAMS], 1)

    def takes(from_of):
        a = np.zeros((P, P), f32)
        a[from_of(ch), ch] = 1
        return a

    def rotated(c):
        d = c % HD
        return np.where(d < 8, c + 8, np.where(d < 16, c - 8, c))
    dup = [takes(lambda c, g=g: HD * g + c % HD) for g in range(2)]
    dup_rot = [takes(lambda c, g=g: HD * g + rotated(c % HD)) for g in range(2)]
    diff = ch[:, None] + P - np.arange(2 * P)[None]
    band = np.where((diff >= 0) & (diff < P), 0, 1e30).astype(f32)
    first = np.arange(16) + 1
    inv_count = np.stack([1 / np.minimum(first, w) for w in (2, 4, 8, 16)]).astype(f32).reshape(1, 64).repeat(P, 0)
    mix_const = np.concatenate([takes(rotated)] + dup + dup_rot + [band, inv_count], 1)

    dist = S - 1 - np.arange(5 * P)
    n = np.maximum(dist, 0)
    ratio = np.log(np.maximum(n, 1).astype(f32) / f32(16)) / f32(math.log(128 / 16))
    bucket = np.where(n < 16, n, np.minimum(16 + (ratio * f32(16)).astype(np.int32), 31))
    code = np.zeros((33, 5 * P), f32)
    code[bucket, np.arange(5 * P)] = -1
    code[:, dist < 0] = 0
    code[32, dist < 0] = 1e30
    head_ones = np.kron(np.eye(2), np.ones((HD, HD))).astype(f32)

    s, t = ch[:, None], ch[None]
    before, upto = (s // C == t // C) & (s < t), (s // C == t // C) & (s <= t)
    levels = [(s >> (k + 1) == t >> (k + 1)) & ((s >> k) % 2 == 0) & ((t >> k) % 2 == 1) for k in range(6)]
    reset = np.tile(np.arange(S) % C != 0, (P, 1))
    rwkv_const = np.concatenate([before, upto, before, upto, reset] + levels
                                + [head_ones, np.tile(np.eye(HD), (2, 1))], 1).astype(f32)

    w2 = one["w_in_2"]
    part = lambda a, b: blocks(w2[:, a:b])
    merge = np.stack([part(3096, 4120), part(4120, 5144),
                      np.concatenate([blocks(one["w_proj_a_2"]), blocks(one["w_proj_b_2"])], 2)], 1)
    pe = [one[n].reshape(16, P).T for n in ("cmp_pe_k_2", "cmp_pe_v_2")]
    return dict(
        x=inputs["x"], positions=inputs["positions"], params=params,
        const=np.concatenate([np.eye(P), np.ones((P, P))], 1).astype(f32), mix_const=mix_const,
        w_pool=one["w_pool"], w_ffn1_gu=pairs(one["ffn1_w_gu"]), w_ffn1_down=blocks(one["ffn1_w_down"]),
        w_in=blocks(one["w_in"])[[8, 9, 4, 5, 6, 7, 0, 1, 2, 3]], w_out=blocks(one["w_out"]),
        w_ffn2_gu=pairs(one["ffn2_w_gu"]), w_ffn2_down=blocks(one["ffn2_w_down"]),
        w_nsa=np.concatenate([part(768, 896), part(1024, 1152), part(896, 1024), part(1152, 1280), part(512, 640),
                              part(640, 768), part(0, 512), part(1280, 1408)]),
        nsa_const=np.concatenate(dup + [head_ones, np.eye(P)[::-1]], 1).astype(f32), rel_bias=inputs["rel_bias_2"], distance_code=code,
        cmp_pe=np.stack(pe), cmp_w1=np.stack([one["cmp_w1_k_2"], one["cmp_w1_v_2"]]),
        cmp_w2=np.stack([one["cmp_w2_k_2"], one["cmp_w2_v_2"]]), w_rwkv=part(1304, 3096), rwkv_const=rwkv_const,
        rwkv_w2a2=np.concatenate([one["rwkv_w2_2"], one["rwkv_a2_2"]]), rwkv_g2=one["rwkv_g2_2"],
        w_merge=merge.reshape(3 * KD, P, D), w_out_2=blocks(one["w_out_2"]), w_conv_up=pairs(one["w_up_2"]),
        w_conv_down=blocks(one["w_down_2"]))


def kernel(**inputs):
    import numpy as _np
    import concourse.bacc as _bacc
    from concourse import mybir as _mybir
    from concourse.bass_utils import run_bass_kernel_spmd as _run

    nc = _bacc.Bacc("TRN2", target_bir_lowering=False, num_devices=1)
    laid_out = _layouts({name: _np.asarray(a) for name, a in inputs.items()})
    arrays, args = {}, {}
    for name, a in laid_out.items():
        a = _np.ascontiguousarray(a)
        arrays[f"{name}_dram"] = a
        args[name] = nc.dram_tensor(f"{name}_dram", a.shape, _mybir.dt.from_np(a.dtype), kind="ExternalInput").ap()
    out = nc.dram_tensor("out_dram", (1, S, D), F32, kind="ExternalOutput").ap()
    build(nc, out=out, **args)
    r = _run(nc, [arrays], core_ids=[0])
    return r.results[0]["out_dram"]
```

```python
import math
from contextlib import ExitStack

import concourse.bass as bass
from concourse import mybir

F32 = mybir.dt.float32
F32R = mybir.dt.float32r
I32 = mybir.dt.int32
ACT = mybir.ActivationFunctionType
ALU = mybir.AluOpType
AX_X = mybir.AxisListType.X

P = 128
S = 512
D = 1024
KD = D // P
NT = S // P
FF = 2816
KF = FF // P
EPS = 1e-6
NH = 8
HD = 64
C = 64
NCH = S // C
KAPPA = math.exp(-0.5)
CMP_H = 256
NCMP = S // 16 - 1
ROUND = 12582912.0
PI_BELOW = 3.1415925
RING = 4
CHUNK = KD * P
DOWN_SPLIT = ((0, 8), (8, 15), (15, 22))

STREAM = (("ffn1_up", 2 * KF), ("ffn1_down", 3 * KD), ("w_in", 10), ("w_out", KD), ("ffn2_up", 2 * KF),
          ("ffn2_down", 3 * KD), ("nsa", 11), ("rwkv", 14), ("gates", 2 * KD), ("merge", KD), ("w_out_2", KD),
          ("conv_up", 2 * KF), ("conv_down", 3 * KD), ("end", 0))
FIRST = {}
_n = 0
for _stage, _count in STREAM:
    FIRST[_stage] = _n
    _n += _count

PARAMS = (("ffn1_pre", KD), ("ffn1_post", KD), ("mix_pre", KD), ("mix_post", KD), ("ffn2_pre", KD),
          ("ffn2_post", KD), ("attn_norm", KD), ("ffn_norm", KD), ("pool_scale", 4), ("g_pool", 4),
          ("g_attn", 4), ("sinks", 8), ("eps", 1), ("half_pi", 1), ("inv_freq", 1), ("rot_sign", 1), ("q_norm", 1),
          ("k_norm", 1), ("sees_block", 1), ("mu", 14), ("w0", 4), ("a0", 4), ("k_k", 4), ("k_a", 4), ("r_k", 4),
          ("ln_g", 4), ("ln_b", 4), ("gn_eps", 1), ("ln_256", 1), ("conv_b", 2 * KF), ("conv_w0", 2 * KF),
          ("conv_w1", 2 * KF), ("conv_w2", 2 * KF))
COL = {}
_n = 0
for _name, _count in PARAMS:
    COL[_name] = _n
    _n += _count
NPARAM = _n

RW_ORDER = (12, 13, 0, 4, 8, 1, 5, 9, 2, 6, 10, 3, 7, 11)
RW_GROUPS = ((0, 2), (2, 5), (5, 8), (8, 11), (11, 14))
PREPARE_AT = {4: 1, 5: 2, 7: 4, 10: 6}
NFILL, LATE = 14 + 2 * KD, 7
NUNIT = 2 * NT
NORMS = (("ffn1", KD), ("mix", KD), ("pool", 4), ("attn", 4), ("ffn2", KD), ("nsa", KD), ("conv", KD))
RSQRTS = (("ffn1_in", 1), ("ffn1_post", 1), ("mix_in", 1), ("pool_in", 1), ("attn_in", 1), ("wout_post", 1),
          ("ffn2_in", 1), ("ffn2_post", 1), ("nsa_in", 1), ("head", 7), ("kk", 4), ("gn", 4), ("conv_in", 1))
UPS = (("ffn1", KF), ("ffn2", KF))
OUTS = (("ffn1", KD), ("wout", KD), ("ffn2", KD))
FAMILIES = {
    "in_sq": NORMS, "in_sq_used": NORMS, "h32": tuple((tag, 2 * n) for tag, n in NORMS),
    "h_ready": (("ffn1", KD), ("mix", KD), ("wout", KD), ("ffn2", KD), ("nsa", KD), ("conv", KD)),
    "x_ready": (("start", KD), ("ffn1", KD), ("wout", KD), ("ffn2", KD), ("conv", KD), ("end", KD)),
    "ln": RSQRTS, "rstd": RSQRTS, "post_sum": tuple((tag, 1) for tag, _ in OUTS),
    "pair_read": UPS + (("conv", KF),), "silu": UPS + (("conv", KF),), "a32": UPS + (("conv", 2 * KF),),
    "a_ready": UPS + (("conv", KF),), "sq": OUTS, "acc": OUTS, "y_read": OUTS, "scaled": OUTS,
    "acc_zero": tuple((tag, 1) for tag, _ in OUTS),
    "scores": (("swa", 2 * NUNIT), ("nsa", 10 * NUNIT)), "masked": (("swa", 4 * NUNIT), ("nsa", 10 * NUNIT)),
    "exp": (("swa", 4 * NUNIT), ("nsa", 12 * NUNIT)), "turned": (("swa", NUNIT), ("nsa", 0)),
    "out_read": (("swa", NUNIT), ("nsa", NUNIT)),
    "step": (("sinks", 1), ("angle", 10), ("sine", 1), ("rot", 12), ("win", 23), ("swa", 2 * NUNIT), ("cmp", 7),
             ("nsa_weight", 2 * NUNIT + 2), ("rw", 0)),
}
SHARED = {}
for _kind, _stages in FAMILIES.items():
    _n = 0
    for _stage, _count in _stages:
        SHARED[_stage + "_" + _kind] = (_kind, _n)
        _n += _count


def build(nc, x, positions, params, const, mix_const, w_pool, w_ffn1_gu, w_ffn1_down, w_in, w_out, w_ffn2_gu,
          w_ffn2_down, w_nsa, nsa_const, rel_bias, distance_code, cmp_pe, cmp_w1, cmp_w2,
          w_rwkv, rwkv_const, rwkv_w2a2, rwkv_g2, w_gates, w_merge, w_out_2, w_conv_up, w_conv_down, out):
    with ExitStack() as ctx:
        def sb(name, shape, dt=F32):
            return ctx.enter_context(nc.sbuf_tensor(name, shape, dt))

        sems = {}

        def sem(name):
            name = SHARED.get(name, (name, 0))[0]
            if name not in sems:
                sems[name] = ctx.enter_context(nc.semaphore(name))
            return sems[name]

        def nth(name, count):
            return sem(name), count + SHARED.get(name, (name, 0))[1]

        with ExitStack() as scope:
            xT = scope.enter_context(nc.sbuf_tensor("xT", [P, KD, S], F32))
        with ExitStack() as scope:
            KK0, MOD0, SG, RATE, CUM, UPTO = (scope.enter_context(nc.sbuf_tensor(n, [P, S], F32))
                                            for n in ("KK0", "MOD0", "SG", "RATE", "CUM", "UPTO"))
            UG = scope.enter_context(nc.sbuf_tensor("UG", [P, 2, 4, P], F32))
        with ExitStack() as scope:
            stage = scope.enter_context(nc.sbuf_tensor("stage", [P, 8, S], F32))
        x_place = ctx.enter_context(nc.sbuf_tensor("x_place", [P, KD * S], F32))
        prm = sb("prm", [P, NPARAM])
        cst = sb("cst", [P, 2, P])
        ident, ones = cst[:, 0, :], cst[:, 1, :]
        w_raw = sb("w_raw", [P, RING, CHUNK])
        w_hi = sb("w_hi", [P, RING, CHUNK], F32R)
        w_lo = sb("w_lo", [P, RING, CHUNK], F32R)
        one = sb("one", [P, 1])
        sq = sb("sq", [P, 2, S])
        acc = sb("acc", [P, S])
        rstd = sb("rstd", [P, S])
        tmp = sb("tmp", [P, 2, S])
        AkV = sb("AkV", [P, 2, 4, HD])
        rcs = sb("rcs", [P, 6 * P + P + HD])
        level = [rcs[:, P * i:P * (i + 1)] for i in range(6)]
        head_ones2, eye2 = rcs[:, 6 * P:7 * P], rcs[:, 7 * P:7 * P + HD]
        w2a2 = sb("w2a2", [P, 4 * P])
        PC = sb("PC", [P, 4, NCH])
        bank = [ctx.enter_context(nc.psum_tensor(f"bank{i}", [P, S], F32)) for i in range(8)]

        with ExitStack() as scope:
            h_hi = scope.enter_context(nc.sbuf_tensor("h_hi", [P, KD, S], F32R))
            h_lo = scope.enter_context(nc.sbuf_tensor("h_lo", [P, KD, S], F32R))
        with ExitStack() as scope:
            yT = scope.enter_context(nc.sbuf_tensor("yT", [P, KD, S], F32))
        def rw_pair_set(place, name, KK, MOD):
            return [KK, MOD, place("AR" + name, [P, NT, 2, P])] + [place(n + name, [P, NT, P])
                                                                   for n in ("At", "Bt", "Kt", "Vt")]
        with ExitStack() as scope:
            in_h = lambda name, shape: scope.enter_context(nc.sbuf_tensor(name, shape, F32))
            odd_set = rw_pair_set(in_h, "1", in_h("KK1", [P, S]), in_h("MOD1", [P, S]))
        with ExitStack() as scope:
            gates = scope.enter_context(nc.sbuf_tensor("gates", [P, 2 * KD, S], F32))
        hole = ctx.enter_context(nc.sbuf_tensor("hole", [P, 2 * KD * S], F32))
        with ExitStack() as scope:
            a_hi = scope.enter_context(nc.sbuf_tensor("a_hi", [P, KF, S], F32R))
            a_lo = scope.enter_context(nc.sbuf_tensor("a_lo", [P, KF, S], F32R))
        with ExitStack() as scope:
            x_tok = scope.enter_context(nc.sbuf_tensor("x_tok", [P, NT, D], F32))

        with ExitStack() as scope:
            def in_a(name, shape, dt=F32):
                return scope.enter_context(nc.sbuf_tensor(name, shape, dt))
            z = in_a("z", [P, 10, S])
            mixed = in_a("mixed", [P, KD, S])
            mcs = in_a("mcs", [P, 5 * P + 2 * P + 64])
            rot_of, dup_of = mcs[:, 0:P], [mcs[:, P * (1 + g):P * (2 + g)] for g in range(2)]
            dup_rot_of = [mcs[:, P * (3 + g):P * (4 + g)] for g in range(2)]
            band = mcs[:, 5 * P:7 * P]
            inv_count = mcs[:, 7 * P:7 * P + 64].rearrange("p (g t) -> p g t", g=4)
            wp = in_a("wp", [P, 4, P])
            pos = in_a("pos", [P, S], I32)
            ang = in_a("ang", [P, 3, S])
            cos_t, sin_t = in_a("cos_t", [P, S]), in_a("sin_t", [P, S])
            q_rot = in_a("q_rot", [P, 4, S])
            k_rot = in_a("k_rot", [P, 2, S])
            v_tok = in_a("v_tok", [P, NT, P])
            PAD = 16
            win = in_a("win", [P, 2, PAD + S])
            dif = in_a("dif", [P, S])
            sc = in_a("sc", [P, 2, 4, 2 * P])
            pT = in_a("pT", [P, 2, 4, P])
            small = in_a("small", [P, 2, 4, 4])
        with ExitStack() as scope:
            with ExitStack() as early:
                def in_e(name, shape, dt=F32):
                    return early.enter_context(nc.sbuf_tensor(name, shape, dt))
                zn = in_e("zn", [P, 11, S])
                pair = in_e("pair", [P, 2, 2, S // 2])
                code = in_e("code", [33, 5 * P])
                rv = in_e("rv", [NH, 5 * P])
            cmp_blocks = [zn[:, a:a + 2, :].rearrange("p a b -> p (a b)")[:, 0:32 * NCMP]
                          .rearrange("p (j g b) -> p j g b", j=16, g=2) for a in (4, 2)]
            E = in_a("E", [P, 2, 8, S])
            with ExitStack() as early:
                cw1 = early.enter_context(nc.sbuf_tensor("cw1", [P, 16, CMP_H], F32))
            toeplitz = in_a("toeplitz", [P, NH, S])
            qn = in_a("qn", [P, 4, S])
            kd = in_a("kd", [P, 4, S])
            v2_tok = in_a("v2_tok", [P, 2, NT, P])
            p2T = in_a("p2T", [P, 2, 4, P])
            oA = in_a("oA", [P, 4, S])
            ncs = in_a("ncs", [P, 4 * P])
            flip = ncs[:, 3 * P:4 * P]
            dup2 = [ncs[:, P * g:P * (g + 1)] for g in range(2)]
            head_ones = ncs[:, 2 * P:3 * P]
            rel = in_a("rel", [33, NH])
            cw2 = in_a("cw2", [P, 2, 2, 2 * HD])
            pe_in = in_a("pe_in", [P, 2, 16])
            hid = in_a("hid", [P, 2, 64])
            hid2 = in_a("hid2", [P, 2, 64])
            kcn = in_a("kcn", [P, 2 * NCMP])
            vct = in_a("vct", [NCMP, 2, HD])
            gate_tok = in_a("gate_tok", [P, NT, 24])
            Ec = in_a("Ec", [P, 2, 4, 32])
            stat = in_a("stat", [P, 2, 3, 12])

        def fill_bank(f):
            return 4 + f % 4 if f < 14 else 7 if f < NFILL - LATE else (0, 1, 2, 4, 5, 6, 0)[f - NFILL + LATE]

        def by_tile(x):
            return x.rearrange("p (n t) -> p n t", n=NT)

        def reverse(x):
            return by_tile(x)[:, :, ::-1]

        def param(name, k=0):
            return prm[:, COL[name] + k:COL[name] + k + 1]

        with ExitStack() as scope:
            pin = in_a("pin", [P, 14, S])
            yl = in_a("yl", [P, 4, S])
            bonus = in_a("bonus", [P, 4, S])
            pair_sets = [rw_pair_set(in_a, "0", KK0, MOD0), odd_set]
            with ExitStack() as early:
                late_stage = early.enter_context(nc.sbuf_tensor("late_stage", [P, LATE, S], F32))
            mats = in_a("mats", [P, 2, 4, 4 * P])
            Dm, DT, X, OT = (in_a(n, [P, 2, 4, P]) for n in ("Dm", "DT", "X", "OT"))
        g2 = UG[:, 0, :, :].rearrange("p a b -> p (a b)")
        PREV, INV = SG, CUM
        gn_work = [sq[:, 0, :], sq[:, 1, :], tmp[:, 0, :], tmp[:, 1, :]]
        mask4, reset = rstd, acc
        state = sq[:, :, 0:4 * HD].rearrange("p s (m i) -> p s m i", m=4)
        with ExitStack() as scope:
            with ExitStack() as early:
                oA2 = early.enter_context(nc.sbuf_tensor("oA2", [P, 4, S], F32))
            m_hi, m_lo = in_a("m_hi", [P, KD, S], F32R), in_a("m_lo", [P, KD, S], F32R)
            in_a("merge_pad", [P, 6 * S])
            o_hi, o_lo = in_a("o_hi", [P, KD, S], F32R), in_a("o_lo", [P, KD, S], F32R)
        oA_dram = nc.dram_tensor("nsa_out", (P, 4 * S), F32)
        fill_dram = nc.dram_tensor("rwkv_and_gates", (P, NFILL * S), F32)
        x_dram = nc.dram_tensor("x_between", (P, KD * S), F32)
        bias_dram = nc.dram_tensor("bias_by_distance", (NH, 5 * P), F32)

        block = ctx.enter_context(nc.Block())

        @block.sync
        def _(sp):
            sp.dma_start(cst[:, :, :], const.rearrange("p (a b) -> p a b", a=2)).then_inc(sem("const_in"), 16)
            sp.dma_start(x_tok[:, :, :], x[0].rearrange("(n p) d -> p n d", p=P)).then_inc(sem("x_in"), 16)
            sp.dma_start(prm[:, :], params).then_inc(sem("params_in"), 16)

            def load(c, s, source, width=CHUNK, first=False):
                if not first:
                    sp.wait_ge(*nth("w_split", c - RING + 1))
                sp.dma_start(w_raw[:, s, 0:width], source).then_inc(sem(f"w_in{s}"), 16)

            def stream(c0, n, source, first=False):
                if first:
                    for u in range(RING):
                        load(u, u, source(u), first=True)
                with sp.Fori(1 if first else 0, n // RING) as i:
                    for u in range(RING):
                        load(i * RING + (c0 + u), (c0 + u) % RING, source(i * RING + u))
                for u in range(n - n % RING, n):
                    load(c0 + u, (c0 + u) % RING, source(u))

            def stream_down(c0, w):
                with sp.Fori(0, KD // RING) as i:
                    for u in range(RING):
                        for j, (a, b) in enumerate(DOWN_SPLIT):
                            v = c0 + 3 * u + j
                            load(i * (3 * RING) + v, v % RING, w[bass.ds(i * RING + u, 1), :, a * P:b * P]
                                 .rearrange("a p n -> (a p) n"), (b - a) * P)

            def whole(w):
                return lambda c: w[bass.ds(c, 1), :, :].rearrange("a p n -> (a p) n")

            stream(FIRST["ffn1_up"], 2 * KF, whole(w_ffn1_gu), first=True)
            stream_down(FIRST["ffn1_down"], w_ffn1_down)

            sp.wait_ge(*nth("w_used", FIRST["w_in"]))
            sp.dma_start(mcs[:, :], mix_const).then_inc(sem("mix_const_in"), 16)
            sp.dma_start(pos[:, :], positions.partition_broadcast(P)).then_inc(sem("positions_in"), 16)
            sp.dma_start(wp[:, :, :], w_pool.rearrange("g c d -> c g d")).then_inc(sem("w_pool_in"), 16)
            stream(FIRST["w_in"], 10, whole(w_in))
            stream(FIRST["w_out"], KD, whole(w_out))
            stream(FIRST["ffn2_up"], 2 * KF, whole(w_ffn2_gu))
            stream_down(FIRST["ffn2_down"], w_ffn2_down)

            sp.wait_ge(*nth("w_used", FIRST["nsa"]))
            sp.dma_start(ncs[:, :], nsa_const).then_inc(sem("nsa_small_in"), 16)
            sp.dma_start(rel[0:32, :], rel_bias).then_inc(sem("nsa_small_in"), 16)
            sp.dma_start(code[:, :], distance_code).then_inc(sem("nsa_small_in"), 16)
            sp.dma_start(pe_in[:, :, :], cmp_pe.rearrange("v p j -> p v j")).then_inc(sem("nsa_small_in"), 16)
            for v in range(2):
                for c in range(2):
                    sp.dma_start(cw2[:, v, :, c * HD:(c + 1) * HD], cmp_w2[v].rearrange("(h p) d -> p h d", p=P))\
                        .then_inc(sem("nsa_small_in"), 16)
            sp.dma_start(cw1[:, :, :], cmp_w1[0].rearrange("(j p) n -> p j n", p=P)).then_inc(sem("cw1_in"), 16)
            stream(FIRST["nsa"], 11, whole(w_nsa))
            sp.wait_ge(*nth("nsa_h_ready", KD))
            sp.dma_start(x_dram.ap(), xT[:, :, :].rearrange("p a b -> p (a b)")).then_inc(sem("x_out"), 16)
            sp.dma_start(rcs[:, :], rwkv_const[:, 2 * S:]).then_inc(sem("rwkv_small_in"), 16)
            sp.dma_start(mask4[:, :], rwkv_const[:, 0:S]).then_inc(sem("rwkv_small_in"), 16)
            sp.dma_start(reset[:, :], rwkv_const[:, S:2 * S]).then_inc(sem("rwkv_small_in"), 16)
            sp.dma_start(w2a2[:, :], rwkv_w2a2).then_inc(sem("rwkv_small_in"), 16)
            stream(FIRST["rwkv"], 14, whole(w_rwkv))
            stream(FIRST["gates"], 2 * KD, whole(w_gates))

            sp.wait_ge(*nth("oA_out", 16 * NT))
            for group in range(2):
                sp.wait_ge(*nth(f"fill_out{group}", 16 * sum(f // 4 % 2 == group for f in range(NFILL - LATE))))
            for i, (a, b) in enumerate(RW_GROUPS):
                c = RW_ORDER[a]
                to = pin[:, 12:14, :] if i == 0 else pin[:, c:12:4, :]
                sp.dma_start(to, fill_dram.ap()[:, a * S:b * S].rearrange("p (a b) -> p a b", b=S))\
                    .then_inc(sem(f"pin_in{i}"), 16)
            stream(FIRST["merge"], RING, whole(w_merge))
            sp.wait_ge(*nth("chunk_terms", 8))
            sp.dma_start(g2, rwkv_g2).then_inc(sem("g2_in"), 16)
            sp.wait_ge(*nth("chunk_terms_read", 8))
            sp.wait_ge(*nth("fill_late", 16 * LATE))
            sp.dma_start(gates[:, :, :].rearrange("p a b -> p (a b)"), fill_dram.ap()[:, 14 * S:])\
                .then_inc(sem("gates_in"), 16)
            sp.wait_ge(*nth("walk_read", 2 * (NCH - 1)))
            sp.dma_start(oA2[:, :, :].rearrange("p a b -> p (a b)"), oA_dram.ap()).then_inc(sem("oA_in"), 16)
            sp.wait_ge(*nth("x_out", 16))
            sp.wait_ge(*nth("gn_gate", 4))
            sp.dma_start(xT[:, :, :].rearrange("p a b -> p (a b)"), x_dram.ap()).then_inc(sem("x_back"), 16)
            stream(FIRST["merge"] + RING, KD - RING, lambda c: whole(w_merge)(c + RING))
            stream(FIRST["w_out_2"], KD, whole(w_out_2))
            stream(FIRST["conv_up"], 2 * KF, whole(w_conv_up))
            stream_down(FIRST["conv_down"], w_conv_down)
            for n in range(NT):
                sp.wait_ge(*nth("out_copied", 2 * (n + 1)))
                sp.dma_start(out[0, n * P:(n + 1) * P, :],
                             yT[:, 2 * n:2 * n + 2, :].rearrange("p a b -> p (a b)")).then_inc(sem("out_done"), 16)
            sp.wait_ge(*nth("out_done", 16 * NT))

        @block.gpsimd
        def _(pool):
            def split(c, turn, s, width=CHUNK, first=False):
                pool.wait_ge(*nth(f"w_in{s}", (turn + 1) * 16))
                if not first:
                    pool.wait_ge(*nth("w_used", c - RING + 1))
                raw = w_raw[:, s, 0:width]
                nc.gpsimd.tensor_tensor(w_hi[:, s, 0:width], raw, one[:, 0:1].to_broadcast([P, width]), ALU.mult).then_inc(sem("w_rounded"), 1)
                pool.wait_ge(*nth("w_rounded", c + 1))
                nc.gpsimd.tensor_tensor(w_lo[:, s, 0:width], raw, w_hi[:, s, 0:width].bitcast(F32),
                                        ALU.subtract).then_inc(sem("w_split"), 1)

            def stream(c0, n, first=False):
                if first:
                    for u in range(RING):
                        split(u, 0, u, first=True)
                with pool.Fori(1 if first else 0, n // RING) as i:
                    for u in range(RING):
                        v = c0 + u
                        split(i * RING + v, i + v // RING, v % RING)
                for u in range(n - n % RING, n):
                    v = c0 + u
                    split(v, v // RING, v % RING)

            def stream_down(c0):
                with pool.Fori(0, KD // RING) as i:
                    for u in range(3 * RING):
                        a, b = DOWN_SPLIT[u % 3]
                        v = c0 + u
                        split(i * (3 * RING) + v, i * 3 + v // RING, v % RING, (b - a) * P)

            nc.gpsimd.memset(one[:, :], 1.0).then_inc(sem("one_set"), 1)
            pool.wait_ge(*nth("one_set", 1))
            stream(FIRST["ffn1_up"], 2 * KF, first=True)
            stream_down(FIRST["ffn1_down"])
            stream(FIRST["w_in"], 10)
            stream(FIRST["w_out"], KD)
            stream(FIRST["ffn2_up"], 2 * KF)
            stream_down(FIRST["ffn2_down"])
            stream(FIRST["nsa"], 11)
            stream(FIRST["rwkv"], 14)
            stream(FIRST["gates"], 2 * KD)
            stream(FIRST["merge"], RING)
            for m in range(4):
                for k in range(1, 6):
                    for half in range(2):
                        if k == 1:
                            pool.wait_ge(*nth("d_ready", 10 * m + half + 1))
                        else:
                            pool.wait_ge(*nth("level_x", 10 * m + 2 * (k - 2) + half + 1))
                        nc.gpsimd.tensor_tensor(OT[:, half, :, :], mats[:, half, :, 0:P],
                                                level[k].unsqueeze(1).to_broadcast([P, 4, P]), ALU.mult)\
                            .then_inc(sem("level_mask"), 1)
            stream(FIRST["merge"] + RING, KD - RING)
            stream(FIRST["w_out_2"], KD)
            stream(FIRST["conv_up"], 2 * KF)
            stream_down(FIRST["conv_down"])

        @block.tensor
        def _(pe):
            def chunk(c, s, k0, k1, rhs_hi, rhs_lo, dst, start, stop, each=None, w0=None):
                w0 = k0 if w0 is None else w0
                pe.wait_ge(*nth("w_split", c + 1))
                for k in range(k0, k1):
                    if each:
                        pe.wait_ge(*nth(each, k + 1))
                    hi = w_hi[:, s, (k - w0) * P:(k - w0 + 1) * P]
                    lo = w_lo[:, s, (k - w0) * P:(k - w0 + 1) * P]
                    nc.tensor.matmul(dst, hi, rhs_hi[:, k, :], start=start and k == k0, stop=False)
                    nc.tensor.matmul(dst, hi, rhs_lo[:, k, :], start=False, stop=False)
                    last = nc.tensor.matmul(dst, lo, rhs_hi[:, k, :], start=False, stop=stop and k == k1 - 1)
                return last

            def ffn_up(tag, c0):
                def body(i, first):
                    for u in range(2):
                        if not first:
                            pe.wait_ge(*nth(tag + "_pair_read", 2 * i + u - 1))
                        for v in range(2):
                            c = 4 * i + (c0 + 2 * u + v)
                            last = chunk(c, (c0 + 2 * u + v) % RING, 0, KD, h_hi, h_lo, bank[2 * u + v][:, :],
                                         True, True, tag + "_h_ready" if first and u == v == 0 else None)
                            last.then_inc(sem("w_used"), 1)
                body(0, True)
                with pe.Fori(1, KF // 2) as i:
                    body(i, False)

            def ffn_down(tag, c0, read):
                pe.wait_ge(*nth(tag + "_a_ready", KF))
                def body(i, first):
                    for u in range(4):
                        if not first:
                            pe.wait_ge(*nth(read, 4 * i + u - 3))
                        for j, (a, b) in enumerate(DOWN_SPLIT):
                            v = 3 * u + j
                            last = chunk(12 * i + (c0 + v), (c0 + v) % RING, a, b, a_hi, a_lo, bank[4 + u][:, :],
                                         j == 0, j == 2)
                            last.then_inc(sem("w_used"), 1)
                body(0, True)
                body(1, False)

            def sum_squares(tag, n, ready, used):
                for k in range(n):
                    pe.wait_ge(*nth(ready, k + 1))
                    nc.tensor.matmul(bank[0][:, :], ones, sq[:, k % 2, :], start=(k == 0),
                                     stop=(k == n - 1)).then_inc(sem(used), 1)

            def project(tag, c0, n, read, h_ready=True, hi=h_hi, lo=h_lo):
                def tile(c, u, first, wait=None):
                    if wait is not None:
                        pe.wait_ge(*nth(read, wait))
                    chunk(c, (c0 + u) % RING, 0, KD, hi, lo, bank[4 + u % 4][:, :], True, True,
                          tag + "_h_ready" if first else None).then_inc(sem("w_used"), 1)
                for u in range(4):
                    tile(c0 + u, u, u == 0 and h_ready)
                with pe.Fori(1, n // 4) as i:
                    for u in range(4):
                        tile(i * 4 + (c0 + u), u, False, wait=i * 4 + (u - 3))
                for m in range(n - n % 4, n):
                    tile(c0 + m, m % 4, False, wait=m - 3)

            def attend_window(n, g, unit):
                keys = slice(max(0, n - 1) * P, (n + 1) * P)
                width = keys.stop - keys.start
                if unit >= 2:
                    pe.wait_ge(*nth("swa_masked", 4 * (unit - 1)))
                for h in range(4):
                    e, i = h % 2, h // 2
                    last = nc.tensor.matmul(bank[2 * (unit % 2) + e][:, i * width:(i + 1) * width],
                                            q_rot[64 * e:64 * e + 64, 2 * g + i, n * P:(n + 1) * P],
                                            k_rot[64 * e:64 * e + 64, g, keys], start=(i == 0), stop=(i == 1),
                                            skip_group_check=True)
                    if i == 1:
                        last.then_inc(sem("swa_scores"), 1)

            def weigh_window(n, g, unit):
                tiles = [j for j in (n - 1, n) if j >= 0]
                pe.wait_ge(*nth("swa_probs", 4 * (unit + 1)))
                if unit:
                    pe.wait_ge(*nth("swa_turned_read", unit))
                for b, j in enumerate(tiles):
                    for h in range(4):
                        last = nc.tensor.transpose(bank[4 + b][:, h * P:(h + 1) * P],
                                                   sc[:, unit % 2, h, b * P:(b + 1) * P], ident)
                last.then_inc(sem("swa_turned"), 1)
                pe.wait_ge(*nth("swa_turned_read", unit + 1))
                if unit:
                    pe.wait_ge(*nth("swa_out_read", unit))
                for h in range(4):
                    e, i = h % 2, h // 2
                    for b, j in enumerate(tiles):
                        last = nc.tensor.matmul(bank[6][64 * e:64 * e + 64, i * P:(i + 1) * P],
                                                v_tok[:, j, 64 * g:64 * g + 64], pT[:, b, h, :],
                                                start=(b == 0), stop=(b == len(tiles) - 1), skip_group_check=True)
                last.then_inc(sem("swa_out"), 1)

            pe.wait_ge(*nth("const_in", 16))
            pe.wait_ge(*nth("x_in", 16))
            for k in range(KD):
                for n in range(NT):
                    last = nc.tensor.transpose(bank[k][:, n * P:(n + 1) * P], x_tok[:, n, k * P:(k + 1) * P], ident)
                last.then_inc(sem("x_turned"), 1)
            pe.wait_ge(*nth("start_x_ready", 1))
            sum_squares("ffn1", KD, "ffn1_in_sq", "ffn1_in_sq_used")
            ffn_up("ffn1", FIRST["ffn1_up"])
            ffn_down("ffn1", FIRST["ffn1_down"], "ffn1_y_read")
            pe.wait_ge(*nth("ffn1_acc", KD))
            nc.tensor.matmul(bank[0][:, :], ones, acc[:, :], start=True, stop=True).then_inc(sem("ffn1_post_sum"), 1)

            sum_squares("mix", KD, "mix_in_sq", "mix_in_sq_used")
            project("mix", FIRST["w_in"], 10, "z_read")
            pe.wait_ge(*nth("mix_const_in", 16))
            for g in range(2):
                pe.wait_ge(*nth("z_read", 1))
                if g:
                    pe.wait_ge(*nth("rot_used", 2 * g - 1))
                nc.tensor.matmul(bank[2 * g][:, :], dup_of[g], z[:, 0, :], start=True, stop=True)
                nc.tensor.matmul(bank[2 * g + 1][:, :], dup_rot_of[g], z[:, 0, :], start=True, stop=True)\
                    .then_inc(sem("rot_done"), 1)
            for i in range(4):
                pe.wait_ge(*nth("z_read", 3 + i))
                pe.wait_ge(*nth("rot_used", 1 + i // 2 if i < 2 else 1 + i))
                nc.tensor.matmul(bank[i % 2 if i < 2 else i][:, :], rot_of, z[:, 2 + i, :], start=True, stop=True)\
                    .then_inc(sem("rot_done"), 1)
            pe.wait_ge(*nth("z_read", 10))
            for n in range(NT):
                last = nc.tensor.transpose(bank[4][:, n * P:(n + 1) * P], z[:, 1, n * P:(n + 1) * P], ident)
            last.then_inc(sem("v_turned"), 1)
            for g in range(4):
                pe.wait_ge(*nth("w_pool_in", 16))
                pe.wait_ge(*nth("pool_diff", g + 1))
                if g:
                    pe.wait_ge(*nth("pooled", g))
                nc.tensor.matmul(bank[7][:, :], wp[:, g, :], dif[:, :], start=True, stop=True)\
                    .then_inc(sem("pool_product"), 1)
            pe.wait_ge(*nth("rot_used", 6))
            pe.wait_ge(*nth("v_read", 1))
            units = [(n, g) for n in range(NT) for g in range(2)]
            attend_window(*units[0], 0)
            for u, (n, g) in enumerate(units):
                if u + 1 < len(units):
                    attend_window(*units[u + 1], u + 1)
                weigh_window(n, g, u)
            pe.wait_ge(*nth("swa_masked", 4 * len(units)))
            sum_squares("pool", 4, "pool_in_sq", "pool_in_sq_used")
            pe.wait_ge(*nth("pool_in_rstd", 1))
            sum_squares("attn", 4, "attn_in_sq", "attn_in_sq_used")
            project("wout", FIRST["w_out"], KD, "wout_y_read")
            pe.wait_ge(*nth("wout_acc", KD))
            nc.tensor.matmul(bank[0][:, :], ones, acc[:, :], start=True, stop=True).then_inc(sem("wout_post_sum"), 1)

            sum_squares("ffn2", KD, "ffn2_in_sq", "ffn2_in_sq_used")
            ffn_up("ffn2", FIRST["ffn2_up"])
            ffn_down("ffn2", FIRST["ffn2_down"], "ffn2_y_read")
            pe.wait_ge(*nth("ffn2_acc", KD))
            nc.tensor.matmul(bank[0][:, :], ones, acc[:, :], start=True, stop=True).then_inc(sem("ffn2_post_sum"), 1)

            sum_squares("nsa", KD, "nsa_in_sq", "nsa_in_sq_used")
            project("nsa", FIRST["nsa"], 11, "zn_read")
            pe.wait_ge(*nth("nsa_small_in", 8 * 16))
            job = [0]

            def job_bank():
                if job[0] >= 2:
                    pe.wait_ge(*nth("nsa_read", job[0] - 1))
                job[0] += 1
                return bank[2 + (job[0] - 1) % 2]

            filled = [0]

            def fill(n=1):
                for f in range(filled[0], filled[0] + n):
                    if f == NFILL - 1:
                        pe.wait_ge(*nth("fill_read", NFILL - LATE + 1))
                    elif 4 <= f <= NFILL - LATE:
                        pe.wait_ge(*nth("fill_read", f - 3 if f < 14 else f))
                    chunk(FIRST["rwkv"] + f, (FIRST["rwkv"] + f) % RING, 0, KD, h_hi, h_lo,
                          bank[fill_bank(f)][:, :], True, True).then_inc(sem("w_used"), 1)
                filled[0] += n

            pe.wait_ge(*nth("zn_read", 11))
            for v in range(2):
                b = job_bank()
                for n in range(NT):
                    last = nc.tensor.transpose(b[:, n * P:(n + 1) * P], zn[:, 2 + v, n * P:(n + 1) * P], ident)
                last.then_inc(sem("nsa_job"), 1)
            fill()
            for v in range(2):
                for g in range(2):
                    nc.tensor.matmul(job_bank()[:, :], dup2[g], zn[:, 4 + v, :], start=True, stop=True)\
                        .then_inc(sem("nsa_job"), 1)
            fill()
            pe.wait_ge(*nth("rel_one", 1))
            for a, b in ((0, S), (S, 5 * P)):
                nc.tensor.matmul(job_bank()[0:NH, 0:b - a], rel[:, :], code[:, a:b], start=True, stop=True)\
                    .then_inc(sem("nsa_job"), 1)
            pe.wait_ge(*nth("gates", 1))
            b = job_bank()
            for n in range(NT):
                last = nc.tensor.transpose(b[:, n * 24:(n + 1) * 24], oA[0:24, 0, n * P:(n + 1) * P],
                                           ident[0:24, 0:24])
            last.then_inc(sem("nsa_job"), 1)
            for i in range(6):
                pe.wait_ge(*nth("head_sq", i + 1))
                nc.tensor.matmul(bank[i % 2][:, :], head_ones, sq[:, i % 2, :], start=True, stop=True)\
                    .then_inc(sem("head_sum"), 1)
                fill()
            for v in range(2):
                pe.wait_ge(*nth("head_rstd_used", v + 1))
                for g in range(2):
                    nc.tensor.matmul(job_bank()[:, :], dup2[g], zn[:, v, :], start=True, stop=True)\
                        .then_inc(sem("nsa_job"), 1)
                fill()
            for v in range(2):
                pe.wait_ge(*nth("cw1_in", 16 * (v + 1)))
                pe.wait_ge(*nth("blocks_ready", 2 * v + 2))
                b = job_bank()
                for h in range(2):
                    for j in range(16):
                        last = nc.tensor.matmul(b[:, h * 64:h * 64 + 2 * NCMP], cw1[:, j, h * P:(h + 1) * P],
                                                cmp_blocks[v][:, j, :, :], start=(j == 0), stop=(j == 15),
                                                skip_group_check=True)
                last.then_inc(sem("nsa_job"), 1)
                fill()
                pe.wait_ge(*nth("gelu", v + 1))
                b = job_bank()
                if v == 0:
                    for h in range(2):
                        last = nc.tensor.matmul(b[:, 0:2 * NCMP], cw2[:, 0, h, :], hid[:, h, 0:2 * NCMP],
                                                start=(h == 0), stop=(h == 1))
                    last.then_inc(sem("nsa_job"), 1)
                    fill()
                    pe.wait_ge(*nth("head_sq", 7))
                    nc.tensor.matmul(bank[0][:, 0:2 * NCMP], head_ones, sq[:, 0, 0:2 * NCMP], start=True, stop=True)\
                        .then_inc(sem("head_sum"), 1)
                else:
                    for g in range(2):
                        for h in range(2):
                            last = nc.tensor.matmul(b[0:NCMP, g * HD:(g + 1) * HD], hid[:, h, g * NCMP:(g + 1) * NCMP],
                                                    cw2[:, 1, h, 0:HD], start=(h == 0), stop=(h == 1),
                                                    skip_group_check=True)
                    last.then_inc(sem("nsa_job"), 1)
            fill()
            pe.wait_ge(*nth("nsa_read", 17))
            pe.wait_ge(*nth("kc_normed", 1))

            def nsa_scores(n, g, unit):
                for i in range(10):
                    b = bank[i % 4] if unit % 2 == 0 else bank[(i + 2) % 4]
                    if 10 * unit + i >= 4:
                        pe.wait_ge(*nth("nsa_masked", 10 * unit + i - 3))
                    if i < 8:
                        h, e = i % 4, i % 2
                        last = nc.tensor.matmul(b[:, 0:(n + 1) * P],
                                                qn[64 * e:64 * e + 64, 2 * g + h // 2, n * P:(n + 1) * P],
                                                kd[64 * e:64 * e + 64, 2 * (i // 4) + g, 0:(n + 1) * P],
                                                start=True, stop=True)
                    else:
                        e = i - 8
                        for h in range(2):
                            last = nc.tensor.matmul(b[:, h * 32:h * 32 + 8 * n + 7],
                                                    qn[64 * e:64 * e + 64, 2 * g + h, n * P:(n + 1) * P],
                                                    kcn[64 * e:64 * e + 64, g * NCMP:g * NCMP + 8 * n + 7],
                                                    start=(h == 0), stop=(h == 1), skip_group_check=True)
                    last.then_inc(sem("nsa_scores"), 1)

            turn = [0]

            def nsa_weigh(n, g, unit):
                c0 = 2 * P * (unit % 2)
                dst = bank[6][:, c0:c0 + 2 * P]
                if unit >= 2:
                    pe.wait_ge(*nth("nsa_out_read", unit - 1))
                items = [(v, j) for v in range(2) for j in range(n + 1)] + [(2, 0)]
                pe.wait_ge(*nth("nsa_weighed", unit + 1))

                def turn_item(x):
                    v, j = items[x]
                    k = turn[0] + x
                    if k >= 2:
                        pe.wait_ge(*nth("p2T_ready", k - 1))
                    for h in range(4):
                        src = Ec[:, unit % 2, h, 0:8 * n + 7] if v == 2 else E[:, unit % 2, 4 * v + h, j * P:(j + 1) * P]
                        rows = 8 * n + 7 if v == 2 else P
                        last = nc.tensor.transpose(bank[4 + k % 2][0:rows, h * P:(h + 1) * P], src, flip)
                    last.then_inc(sem("nsa_turned"), 1)

                def sum_item(x):
                    v, j = items[x]
                    k = turn[0] + x
                    pe.wait_ge(*nth("p2T_ready", k + 1))
                    for h in range(4):
                        e, i = h % 2, h // 2
                        if v == 2:
                            lhs, rhs = vct[0:8 * n + 7, g, :], p2T[0:8 * n + 7, k % 2, h, :]
                        else:
                            lhs, rhs = v2_tok[:, v, j, 64 * g:64 * g + 64], p2T[:, k % 2, h, :]
                        last = nc.tensor.matmul(dst[64 * e:64 * e + 64, i * P:(i + 1) * P], lhs, rhs,
                                                start=(x == 0 and i == 0), stop=(v == 2), skip_group_check=True)
                    last.then_inc(sem("p2T_used"), 1)
                    return last

                turn_item(0)
                for x in range(len(items)):
                    if x + 1 < len(items):
                        turn_item(x + 1)
                    last = sum_item(x)
                turn[0] += len(items)

            units = [(n, g) for n in range(NT) for g in range(2)]
            nsa_scores(*units[0], 0)
            for u, (n, g) in enumerate(units):
                if u + 1 < len(units):
                    nsa_scores(*units[u + 1], u + 1)
                fill()
                nsa_weigh(n, g, u)
                if u == 6:
                    fill()

            def rw_prepare(m, step):
                cols = slice(m * P, (m + 1) * P)
                if step == 1:
                    pe.wait_ge(*nth("lora_in", 1))
                    if m:
                        pe.wait_ge(*nth("level_start", 2 * m))
                    nc.tensor.matmul(bank[3][:, :], w2a2[0:64, cols], pin[0:64, 12, :], start=True, stop=True)
                    nc.tensor.matmul(bank[7][:, :], w2a2[64:128, cols], pin[64:128, 12, :], start=True, stop=True)\
                        .then_inc(sem("lora"), 1)
                elif step == 3:
                    pe.wait_ge(*nth("lora_read", m + 1))
                    pe.wait_ge(*nth("rw_square", m + 1))
                    nc.tensor.matmul(bank[3][:, :], head_ones2, sq[:, 0, :], start=True, stop=True)\
                        .then_inc(sem("rw_head_sum"), 1)
                    pe.wait_ge(*nth("rk_product", m + 1))
                    nc.tensor.matmul(bank[7][:, :], head_ones2, sq[:, 1, :], start=True, stop=True)\
                        .then_inc(sem("rw_head_sum"), 1)

            pe.wait_ge(*nth("rwkv_small_in", 4 * 16))
            for step in range(1, 6):
                fill(2 if step < 3 else 1)
                rw_prepare(0, step)
            rounds = [[(2 * half + i, e) for i in range(2) for e in range(2)] for half in range(2)]

            def rw_scores(m, half):
                Bh, Kh, AR = pair_sets[m % 2][:3]
                for u, (n, e) in enumerate(rounds[half]):
                    b = bank[u if half else 4 + u]
                    rows = slice(64 * e, 64 * e + 64)
                    rhs = AR[rows, n, :, :].rearrange("p a t -> p (a t)")
                    nc.tensor.matmul(b[:, 0:2 * P], Bh[rows, n * P:(n + 1) * P], rhs, start=True, stop=True,
                                     skip_group_check=True)
                    nc.tensor.matmul(b[:, 2 * P:], Kh[rows, n * P:(n + 1) * P], rhs, start=True, stop=True,
                                     skip_group_check=True).then_inc(sem("rw_scores"), 1)

            def rw_turn(m, part):
                Bh, Kh, AR = pair_sets[m % 2][:3]
                if part == 0:
                    pe.wait_ge(*nth("hats", 4 * (m + 1)))
                    pe.wait_ge(*nth("bonus_done", m + 1))
                srcs = (AR[:, :, 0, :], by_tile(Bh[:, :]), by_tile(Kh[:, :]), by_tile(pin[:, 8 + m, :]))
                for i in range(2 * part, 2 * part + 2):
                    if part:
                        pe.wait_ge(*nth("rw_tok", 4 * m + i - 1))
                    for n in range(NT):
                        last = nc.tensor.transpose(bank[3 + 4 * (i % 2)][:, n * P:(n + 1) * P], srcs[i][:, n, :],
                                                   ident)
                    last.then_inc(sem("rw_turned"), 1)

            rw_turn(0, 0)
            for m in range(4):
                At, Bt, Kt, Vt = pair_sets[m % 2][3:]
                if m:
                    pe.wait_ge(*nth("chunk_terms_read", 2 * m - 1))
                else:
                    rw_turn(0, 1)
                pe.wait_ge(*nth("rw_tok", 4 * (m + 1)))
                rw_scores(m, 0)
                if m:
                    pe.wait_ge(*nth("chunk_terms_read", 2 * m))
                rw_scores(m, 1)
                for half in range(2):
                    if m < 3 and half == 1:
                        rw_prepare(m + 1, 1)
                    pe.wait_ge(*nth("level_start", 2 * m + half + 1))
                    for u in range(4):
                        last = nc.tensor.transpose(bank[0 if half else 4][:, u * P:(u + 1) * P], OT[:, half, u, :],
                                                   ident)
                    last.then_inc(sem("level_turned"), 1)
                for k in range(1, 6):
                    done = 10 * m + 2 * (k - 1)
                    for half in range(2):
                        pe.wait_ge(*nth("level_mask", done + half + 1))
                        pe.wait_ge(*nth("d_ready", done + half + 1))
                        for u in range(4):
                            last = nc.tensor.matmul(bank[0 if half else 4][:, u * P:(u + 1) * P], OT[:, half, u, :],
                                                    Dm[:, half, u, :], start=True, stop=True, skip_group_check=True)
                        last.then_inc(sem("level_x"), 1)
                    for half in range(2):
                        pe.wait_ge(*nth("level_x_read", done + half + 1))
                        pe.wait_ge(*nth("dt_ready", 12 * m + 2 * (k - 1) + half + 1))
                        if k < 5:
                            for u in range(4):
                                last = nc.tensor.matmul(bank[1 if half else 5][:, u * P:(u + 1) * P],
                                                        DT[:, half, u, :], X[:, half, u, :],
                                                        start=True, stop=True, skip_group_check=True)
                            last.then_inc(sem("level_d"), 1)
                    for half in range(2):
                        for u in range(4):
                            last = nc.tensor.matmul(bank[2 if half else 6][:, u * P:(u + 1) * P], X[:, half, u, :],
                                                    DT[:, half, u, :], start=True, stop=True, skip_group_check=True)
                        last.then_inc(sem("level_dt"), 1)
                    if m < 3:
                        rw_prepare(m + 1, k + 1)
                for half in range(2):
                    for u, (n, e) in enumerate(rounds[half]):
                        last = nc.tensor.matmul(bank[0 if half else 4][:, u * HD:(u + 1) * HD],
                                                mats[:, half, u, 2 * P:3 * P], Vt[:, n, 64 * e:64 * e + 64],
                                                start=True, stop=True, skip_group_check=True)
                    last.then_inc(sem("akv"), 1)
                for half in range(2):
                    pe.wait_ge(*nth("akv_read", 2 * m + half + 1))
                    pe.wait_ge(*nth("dt_ready", 12 * m + 10 + half + 1))
                    for u, (n, e) in enumerate(rounds[half]):
                        b = bank[1 if half else 5]
                        nc.tensor.matmul(b[:, u * P:u * P + HD], DT[:, half, u, :], AkV[:, half, u, :],
                                         start=True, stop=True, skip_group_check=True)
                        last = nc.tensor.matmul(b[:, u * P + HD:(u + 1) * P], DT[:, half, u, :],
                                                At[:, n, 64 * e:64 * e + 64], start=True, stop=True,
                                                skip_group_check=True)
                    last.then_inc(sem("ug"), 1)
                if m < 3:
                    rw_turn(m + 1, 0)
                for half in range(2):
                    if m < 3 and half == 1:
                        rw_turn(m + 1, 1)
                    pe.wait_ge(*nth("ug_read", 2 * m + half + 1))
                    qy = bank[2 if half else 6]
                    for u, (n, e) in enumerate(rounds[half]):
                        rows, at = slice(64 * e, 64 * e + 64), slice((u // 2) * P, (u // 2 + 1) * P)
                        y_at = slice(2 * P + at.start, 2 * P + at.stop)
                        U, G = UG[:, half, u, 0:HD], UG[:, half, u, HD:]
                        V = Vt[:, n, 64 * e:64 * e + 64]
                        nc.tensor.matmul(qy[rows, at], G, mats[:, half, u, P:2 * P], start=True, stop=True,
                                         skip_group_check=True)
                        nc.tensor.matmul(qy[rows, y_at], U, mats[:, half, u, P:2 * P], start=True, stop=False,
                                         skip_group_check=True)
                        nc.tensor.matmul(qy[rows, y_at], V, mats[:, half, u, 3 * P:], start=False, stop=True,
                                         skip_group_check=True)
                        at = slice((u // 2) * HD, (u // 2 + 1) * HD)
                        n_at = slice(P + at.start, P + at.stop)
                        for c in range(2):
                            mn = bank[c if half else 4 + c]
                            tok = slice(64 * c, 64 * c + 64)
                            B, K, V = (x[tok, n, 64 * e:64 * e + 64] for x in (Bt, Kt, Vt))
                            nc.tensor.matmul(mn[rows, at], UG[tok, half, u, HD:], B, start=True, stop=True,
                                             skip_group_check=True)
                            nc.tensor.matmul(mn[rows, n_at], B, UG[tok, half, u, 0:HD], start=True, stop=False,
                                             skip_group_check=True)
                            last = nc.tensor.matmul(mn[rows, n_at], K, V, start=False, stop=True,
                                                    skip_group_check=True)
                    last.then_inc(sem("chunk_terms"), 1)
            pe.wait_ge(*nth("chunk_terms_read", 8))
            for c in range(1, NCH):
                pe.wait_ge(*nth("state", 2 * c))
                if c > 1:
                    pe.wait_ge(*nth("walk_read", 2 * (c - 1)))
                at = slice(c * C, (c + 1) * C)
                for e in range(2):
                    rows = slice(64 * e, 64 * e + 64)
                    if c < NCH - 1:
                        for m in range(4):
                            last = nc.tensor.matmul(bank[2 + e][rows, m * HD:(m + 1) * HD], pin[rows, 4 + m, at],
                                                    state[rows, c % 2, m, :], start=True, stop=True,
                                                    skip_group_check=True)
                        last.then_inc(sem("state_product"), 1)
                for e in range(2):
                    rows = slice(64 * e, 64 * e + 64)
                    for m in range(4):
                        last = nc.tensor.matmul(bank[e][rows, m * HD:(m + 1) * HD], state[rows, c % 2, m, :],
                                                pin[rows, m, at], start=True, stop=True, skip_group_check=True)
                    last.then_inc(sem("walk_y"), 1)
            pe.wait_ge(*nth("walk_read", 2 * (NCH - 1)))
            for m in range(4):
                nc.tensor.matmul(bank[m][:, :], head_ones2, yl[:, m, :], start=True, stop=True)\
                    .then_inc(sem("gn_sum"), 1)
            pe.wait_ge(*nth("g2_in", 16))
            for m in range(4):
                nc.tensor.matmul(bank[4 + m][:, :], g2[:, m * P:(m + 1) * P], pin[:, 13, :], start=True, stop=True)\
                    .then_inc(sem("gn_gate"), 1)
            for m in range(4):
                pe.wait_ge(*nth("gn_sq", m + 1))
                nc.tensor.matmul(bank[m][:, :], head_ones2, gn_work[m], start=True, stop=True)\
                    .then_inc(sem("gn_var"), 1)

            pe.wait_ge(*nth("gn_out", 4))
            pe.wait_ge(*nth("o_ready", KD))

            for m in range(KD):
                if m >= 4:
                    pe.wait_ge(*nth("m_ready", m - 3))
                c, b = FIRST["merge"] + m, 2 * (m % 4)
                chunk(c, c % RING, 0, 4, o_hi, o_lo, bank[b][:, :], True, True)
                chunk(c, c % RING, 4, 8, o_hi, o_lo, bank[b + 1][:, :], True, True, w0=0).then_inc(sem("w_used"), 1)
            pe.wait_ge(*nth("m_ready", KD))
            project("w_out_2", FIRST["w_out_2"], KD, "conv_x_ready", h_ready=False, hi=m_hi, lo=m_lo)

            sum_squares("conv", KD, "conv_in_sq", "conv_in_sq_used")
            ffn_up("conv", FIRST["conv_up"])
            ffn_down("conv", FIRST["conv_down"], "end_x_ready")
            pe.wait_ge(*nth("end_x_ready", KD))
            for n in range(NT):
                for h in range(2):
                    for k in range(4):
                        last = nc.tensor.transpose(bank[2 * n + h][:, k * P:(k + 1) * P],
                                                   xT[:, 4 * h + k, n * P:(n + 1) * P], ident)
                    last.then_inc(sem("out_turned"), 1)

        @block.scalar
        def _(act):
            def inv_rms(tag, ready, count, n=D):
                act.wait_ge(*nth(ready, count))
                nc.scalar.activation(rstd[:, :], bank[0][:, :], ACT.Ln, bias=param("eps"), scale=1.0 / n)\
                    .then_inc(sem(tag + "_ln"), 1)
                act.wait_ge(*nth(tag + "_ln", 1))
                nc.scalar.activation(rstd[:, :], rstd[:, :], ACT.Exp, scale=-0.5).then_inc(sem(tag + "_rstd"), 1)

            def pre_norm(tag, x_ready, count=None, src=xT, k0=0, n=KD):
                for k in range(n):
                    act.wait_ge(*nth(x_ready, k + 1 if count is None else count))
                    if k >= 2:
                        act.wait_ge(*nth(tag + "_in_sq_used", k - 1))
                    nc.scalar.activation(sq[:, k % 2, :], src[:, k0 + k, :], ACT.Square)\
                        .then_inc(sem(tag + "_in_sq"), 1)
                inv_rms(tag + "_in", tag + "_in_sq_used", n, n * P)

            def ffn_up(tag):
                def body(i, first):
                    for u in range(2):
                        act.wait_ge(*nth("w_used", FIRST[tag + "_up"] + 4 * i + 2 * u + 1))
                        if not first:
                            act.wait_ge(*nth(tag + "_pair_read", 2 * i + u - 1))
                        nc.scalar.activation(tmp[:, u, :], bank[2 * u][:, :], ACT.Silu).then_inc(sem(tag + "_silu"), 1)
                body(0, True)
                with act.Fori(1, KF // 2) as i:
                    body(i, False)

            def copy_out(tag, c0, per, y):
                for m in range(KD):
                    act.wait_ge(*nth("w_used", c0 + per * (m + 1)))
                    if m >= 2:
                        act.wait_ge(*nth(tag + "_acc", m - 1))
                    nc.scalar.activation(sq[:, m % 2, :], bank[4 + m % 4][:, :], ACT.Square).then_inc(sem(tag + "_sq"), 1)
                    nc.scalar.activation(y[:, m, :], bank[4 + m % 4][:, :], ACT.Copy).then_inc(sem(tag + "_y_read"), 1)

            act.wait_ge(*nth("params_in", 16))
            pre_norm("ffn1", "start_x_ready")
            ffn_up("ffn1")
            copy_out("ffn1", FIRST["ffn1_down"], 3, yT)
            inv_rms("ffn1_post", "ffn1_post_sum", 1)

            pre_norm("mix", "ffn1_x_ready")
            act.wait_ge(*nth("angle_step", 10))
            nc.scalar.activation(sin_t[:, :], ang[:, 0, :], ACT.Sin).then_inc(sem("sine"), 1)
            nc.scalar.activation(cos_t[:, :], ang[:, 2, :], ACT.Sin, bias=param("half_pi"), scale=-1.0)\
                .then_inc(sem("sine"), 1)
            for m in range(10):
                act.wait_ge(*nth("w_used", FIRST["w_in"] + m + 1))
                nc.scalar.activation(z[:, m, :], bank[4 + m % 4][:, :], ACT.Copy).then_inc(sem("z_read"), 1)
            act.wait_ge(*nth("v_turned", 1))
            nc.scalar.activation(v_tok[:, :, :].rearrange("p n c -> p (n c)"), bank[4][:, :], ACT.Copy)\
                .then_inc(sem("v_read"), 1)
            units = [(n, g) for n in range(NT) for g in range(2)]

            def exps(n, g, unit):
                width = (2 if n else 1) * P
                act.wait_ge(*nth("swa_masked", 4 * (unit + 1)))
                for h in range(4):
                    s = sc[:, unit % 2, h, 0:width]
                    nc.scalar.activation(s, s, ACT.Exp, bias=small[:, unit % 2, 0, h:h + 1], scale=-1.0,
                                         accum_out=small[:, unit % 2, 1, h:h + 1]).then_inc(sem("swa_exp"), 1)
                act.wait_ge(*nth("swa_sink_arg", unit + 1))
                nc.scalar.activation(small[:, unit % 2, 2, :], small[:, unit % 2, 2, :], ACT.Exp)\
                    .then_inc(sem("swa_sink_exp"), 1)

            def copies(n, g, unit):
                act.wait_ge(*nth("swa_turned", unit + 1))
                if unit:
                    act.wait_ge(*nth("swa_out", unit))
                for b in range(2 if n else 1):
                    last = nc.scalar.activation(pT[:, b, :, :].rearrange("p h t -> p (h t)"), bank[4 + b][:, :],
                                                ACT.Copy)
                last.then_inc(sem("swa_turned_read"), 1)

            def store_out(n, g, unit):
                act.wait_ge(*nth("swa_out", unit + 1))
                nc.scalar.activation(mixed[:, 4 + 2 * g:6 + 2 * g, n * P:(n + 1) * P],
                                     bank[6][:, 0:2 * P].rearrange("p (i t) -> p i t", i=2), ACT.Copy)\
                    .then_inc(sem("swa_out_read"), 1)

            exps(*units[0], 0)
            for u, (n, g) in enumerate(units):
                copies(n, g, u)
                if u + 1 < len(units):
                    exps(*units[u + 1], u + 1)
                store_out(n, g, u)
            pre_norm("pool", "pooled", 4, src=mixed, n=4)
            act.wait_ge(*nth("pool_h32", 8))
            pre_norm("attn", "swa_out_read", len(units), src=mixed, k0=4, n=4)
            copy_out("wout", FIRST["w_out"], 1, mixed)
            inv_rms("wout_post", "wout_post_sum", 1)

            pre_norm("ffn2", "wout_x_ready")
            ffn_up("ffn2")
            copy_out("ffn2", FIRST["ffn2_down"], 3, yT)
            inv_rms("ffn2_post", "ffn2_post_sum", 1)

            pre_norm("nsa", "ffn2_x_ready")
            for m in range(11):
                act.wait_ge(*nth("w_used", FIRST["nsa"] + m + 1))
                nc.scalar.activation(zn[:, m, :], bank[4 + m % 4][:, :], ACT.Copy).then_inc(sem("zn_read"), 1)
            act.wait_ge(*nth("zn_read", 11))
            nc.scalar.activation(reverse(oA[0:24, 0, :]), by_tile(zn[0:24, 10, :]), ACT.Sigmoid)\
                .then_inc(sem("gates"), 1)
            filled = [0]

            def fill_out(n=1):
                for f in range(filled[0], filled[0] + n):
                    act.wait_ge(*nth("w_used", FIRST["rwkv"] + f + 1))
                    late = f - NFILL + LATE
                    if f == 0:
                        act.wait_ge(*nth("x_out", 16))
                    elif f >= 8 and f % 4 == 0 and late < 0:
                        act.wait_ge(*nth(f"fill_out{f // 4 % 2}", 64 * (f // 8)))
                    place = stage[:, f % 8, :] if late < 0 else late_stage[:, late, :]
                    nc.scalar.activation(place, bank[fill_bank(f)][:, :], ACT.Copy).then_inc(sem("fill_read"), 1)
                    act.wait_ge(*nth("fill_read", f + 1))
                    act.dma_start(fill_dram.ap()[:, f * S:(f + 1) * S], place)\
                        .then_inc(sem("fill_late" if late >= 0 else f"fill_out{f // 4 % 2}"), 16)
                filled[0] += n

            def head_rms(i, width=S):
                act.wait_ge(*nth("head_sum", i + 1))
                if i >= 2:
                    act.wait_ge(*nth("head_rstd_used", i - 1))
                nc.scalar.activation(tmp[:, i % 2, 0:width], bank[i % 2][:, 0:width], ACT.Ln, bias=param("eps"),
                                     scale=1.0 / HD).then_inc(sem("head_ln"), 1)
                act.wait_ge(*nth("head_ln", i + 1))
                nc.scalar.activation(tmp[:, i % 2, 0:width], tmp[:, i % 2, 0:width], ACT.Exp, scale=-0.5)\
                    .then_inc(sem("head_rstd"), 1)

            for i in range(6):
                nc.scalar.activation(sq[:, i % 2, :], zn[:, i if i < 2 else i + 4, :], ACT.Square)\
                    .then_inc(sem("head_sq"), 1)
                if i:
                    head_rms(i - 1)
                    fill_out()
                if i == 3:
                    act.wait_ge(*nth("nsa_read", 8))
                    act.dma_start(bias_dram.ap(), rv[:, :]).then_inc(sem("bias_out"), 16)
            head_rms(5)
            fill_out(5)
            for v in range(2):
                act.wait_ge(*nth("gelu_arg", v + 1))
                nc.scalar.activation(hid2[:, :, 0:2 * NCMP], hid2[:, :, 0:2 * NCMP], ACT.Tanh, scale=math.sqrt(2.0 / math.pi))\
                    .then_inc(sem("gelu_tanh"), 1)
                if v == 0:
                    act.dma_start(cw1[:, :, :], cmp_w1[1].rearrange("(j p) n -> p j n", p=P))\
                        .then_inc(sem("cw1_in"), 16)
                    fill_out()
                    act.wait_ge(*nth("nsa_read", 15))
                    nc.scalar.activation(sq[:, 0, 0:2 * NCMP], kcn[:, :], ACT.Square).then_inc(sem("head_sq"), 1)
                    head_rms(6, 2 * NCMP)
                    fill_out()
                else:
                    act.wait_ge(*nth("bias_out", 16))
                    act.dma_start(toeplitz[:, :, :], bass.AP(bias_dram, 0, [[1, P], [5 * P, NH], [1, S]]))\
                        .then_inc(sem("toeplitz_in"), 16)
                    fill_out(2)

            def nsa_exps(n, g, unit):
                for i in range(10):
                    act.wait_ge(*nth("nsa_masked", 10 * unit + i + 1))
                    if i < 8:
                        s, c = E[:, unit % 2, i, 0:(n + 1) * P], 4 + i
                        nc.scalar.activation(s, s, ACT.Exp, bias=stat[:, unit % 2, 0, c:c + 1], scale=-1.0,
                                             accum_out=stat[:, unit % 2, 1, c:c + 1]).then_inc(sem("nsa_exp"), 1)
                    else:
                        for k in range(2):
                            c = 2 * k + i - 8
                            s = Ec[:, unit % 2, c, 0:8 * n + 7]
                            nc.scalar.activation(s, s, ACT.Exp, bias=stat[:, unit % 2, 0, c:c + 1], scale=-1.0,
                                                 accum_out=stat[:, unit % 2, 1, c:c + 1])\
                                .then_inc(sem("nsa_exp"), 1)

            turn = [0]

            def nsa_copies(n, g, unit):
                items = 2 * (n + 1) + 1
                c0 = 2 * P * (unit % 2)
                for x in range(items):
                    k = turn[0] + x
                    act.wait_ge(*nth("nsa_turned", k + 1))
                    if k >= 2:
                        act.wait_ge(*nth("p2T_used", k - 1))
                    rows = 8 * n + 7 if x == items - 1 else P
                    nc.scalar.activation(p2T[0:rows, k % 2, :, :].rearrange("p h t -> p (h t)"),
                                         bank[4 + k % 2][0:rows, :], ACT.Copy).then_inc(sem("p2T_ready"), 1)
                turn[0] += items
                act.wait_ge(*nth("p2T_used", turn[0]))
                nc.scalar.activation(oA[:, 2 * g:2 * g + 2, n * P:(n + 1) * P],
                                     bank[6][:, c0:c0 + 2 * P].rearrange("p (i t) -> p i t", i=2), ACT.Copy)\
                    .then_inc(sem("nsa_out_read"), 1)
                if g == 1:
                    act.wait_ge(*nth("nsa_out_read", unit + 1))
                    act.dma_start(oA_dram.ap().rearrange("p (a b) -> p a b", a=4)[:, :, n * P:(n + 1) * P],
                                  oA[:, :, n * P:(n + 1) * P]).then_inc(sem("oA_out"), 16)

            nsa_exps(*units[0], 0)
            for u, (n, g) in enumerate(units):
                if u == 7:
                    fill_out()
                if u + 1 < len(units):
                    nsa_exps(*units[u + 1], u + 1)
                fill_out()
                nsa_copies(n, g, u)

            def rw_prepare(m, step):
                if step == 1:
                    act.wait_ge(*nth("lora", m + 1))
                    nc.scalar.activation(SG[:, :], bank[3][:, :], ACT.Sigmoid, bias=param("w0", m))
                    nc.scalar.activation(RATE[:, :], bank[7][:, :], ACT.Sigmoid, bias=param("a0", m))\
                        .then_inc(sem("lora_read"), 1)
                elif step == 2:
                    act.wait_ge(*nth("kk", m + 1))
                    if m:
                        act.wait_ge(*nth("rw_head_sum", 2 * m))
                    nc.scalar.activation(sq[:, 0, :], pair_sets[m % 2][0][:, :], ACT.Square).then_inc(sem("rw_square"), 1)
                elif step == 3:
                    act.wait_ge(*nth("cumulative", m + 1))
                    nc.scalar.activation(UPTO[:, :], CUM[:, :], ACT.Exp, scale=-KAPPA).then_inc(sem("decays"), 1)
                    nc.scalar.activation(PREV[:, :], PREV[:, :], ACT.Exp, scale=-KAPPA).then_inc(sem("decays"), 1)
                    act.wait_ge(*nth("decays", 3 * m + 2))
                    nc.scalar.activation(INV[:, :], CUM[:, :], ACT.Exp, scale=KAPPA).then_inc(sem("decays"), 1)
                elif step == 5:
                    act.wait_ge(*nth("kk_sum", m + 1))
                    nc.scalar.activation(tmp[:, 0, :], tmp[:, 0, :], ACT.Ln, scale=65536.0).then_inc(sem("kk_ln"), 1)
                    act.wait_ge(*nth("kk_ln", m + 1))
                    nc.scalar.activation(tmp[:, 0, :], tmp[:, 0, :], ACT.Exp, bias=param("ln_256"), scale=-0.5)\
                        .then_inc(sem("kk_rstd"), 1)

            act.wait_ge(*nth("mixed_in", 2))
            nc.scalar.activation(pin[:, 13, :], pin[:, 13, :], ACT.Sigmoid).then_inc(sem("gate_in"), 1)
            nc.scalar.activation(pin[0:64, 12, :], pin[0:64, 12, :], ACT.Tanh).then_inc(sem("lora_in"), 1)
            for step in range(1, 6):
                fill_out(2 if step < 3 else 1)
                rw_prepare(0, step)
            flat = lambda x: x.rearrange("p a b -> p (a b)")

            def rw_turned(m, part):
                for i in range(2 * part, 2 * part + 2):
                    act.wait_ge(*nth("rw_turned", 4 * m + i + 1))
                    nc.scalar.activation(flat(pair_sets[m % 2][3 + i][:, :, :]), bank[3 + 4 * (i % 2)][:, :],
                                         ACT.Copy).then_inc(sem("rw_tok"), 1)

            rw_turned(0, 0)
            rw_turned(0, 1)
            for m in range(4):
                if m < 3:
                    rw_prepare(m + 1, 1)
                for k in range(1, 6):
                    for half in range(2):
                        act.wait_ge(*nth("level_x", 10 * m + 2 * (k - 1) + half + 1))
                        nc.scalar.activation(flat(X[:, half, :, :]), bank[0 if half else 4][:, :], ACT.Copy)\
                            .then_inc(sem("level_x_read"), 1)
                    if m < 3:
                        rw_prepare(m + 1, k + 1)
                for half in range(2):
                    act.wait_ge(*nth("akv", 2 * m + half + 1))
                    nc.scalar.activation(flat(AkV[:, half, :, :]), bank[0 if half else 4][:, 0:4 * HD], ACT.Copy)\
                        .then_inc(sem("akv_read"), 1)
                for half in range(2):
                    act.wait_ge(*nth("ug", 2 * m + half + 1))
                    nc.scalar.activation(flat(UG[:, half, :, :]), bank[1 if half else 5][:, :], ACT.Copy)\
                        .then_inc(sem("ug_read"), 1)
                if m < 3:
                    rw_turned(m + 1, 0)
                    rw_turned(m + 1, 1)
            act.wait_ge(*nth("gates_in", 16))
            for i in range(4):
                g = flat(gates[:, 4 * i:4 * i + 4, :])
                nc.scalar.activation(g, g, ACT.Sigmoid).then_inc(sem("merge_gate"), 1)
            for m in range(4):
                act.wait_ge(*nth("gn_centred", m + 1))
                nc.scalar.activation(gn_work[m], yl[:, m, :], ACT.Square).then_inc(sem("gn_sq"), 1)
            for m in range(4):
                act.wait_ge(*nth("gn_var", m + 1))
                nc.scalar.activation(gn_work[m], bank[m][:, :], ACT.Ln, bias=param("gn_eps"), scale=1.0 / HD)\
                    .then_inc(sem("gn_ln"), 1)
            for m in range(4):
                act.wait_ge(*nth("gn_ln", m + 1))
                nc.scalar.activation(gn_work[m], gn_work[m], ACT.Exp, scale=-0.5).then_inc(sem("gn_rstd"), 1)

            pre_norm("conv", "conv_x_ready")
            with act.Fori(0, KF) as p:
                act.wait_ge(*nth("conv_pair_read", p + 1))
                nc.scalar.activation(sq[:, 0, :], tmp[:, 1, :], ACT.Silu).then_inc(sem("conv_silu"), 1)

        @block.vector
        def _(dve):
            def pre_norm(tag, gain, ready, src=xT, k0=0, n=KD, done=0):
                dve.wait_ge(*nth(tag + "_in_rstd", 1))
                for k in range(n):
                    at = k0 + k
                    for to, name in ((h_hi[:, at, :], "_h32"), (tmp[:, k % 2, :], "_h32")):
                        nc.vector.scalar_tensor_tensor(to, src[:, at, :], param(gain, k), rstd[:, :], ALU.mult,
                                                       ALU.mult).then_inc(sem(tag + name), 1)
                    dve.wait_ge(*nth(tag + "_h32", 2 * k + 2))
                    nc.vector.tensor_tensor(h_lo[:, at, :], tmp[:, k % 2, :], h_hi[:, at, :].bitcast(F32),
                                            ALU.subtract).then_inc(sem(ready), 1)

            def ffn_up(tag):
                def body(i, first):
                    for u in range(2):
                        p = 2 * i + u
                        dve.wait_ge(*nth(tag + "_silu", p + 1))
                        dve.wait_ge(*nth("w_used", FIRST[tag + "_up"] + 4 * i + 2 * u + 2))
                        hi, lo = (a[:, bass.ds(p, 1), :].rearrange("q a t -> q (a t)") for a in (a_hi, a_lo))
                        nc.vector.tensor_tensor(hi, tmp[:, u, :], bank[2 * u + 1][:, :], ALU.mult)\
                            .then_inc(sem(tag + "_a32"), 1)
                        nc.vector.tensor_tensor(sq[:, u, :], tmp[:, u, :], bank[2 * u + 1][:, :], ALU.mult)\
                            .then_inc(sem(tag + "_pair_read"), 1)
                        dve.wait_ge(*nth(tag + "_a32", p + 1))
                        dve.wait_ge(*nth(tag + "_pair_read", p + 1))
                        nc.vector.tensor_tensor(lo, sq[:, u, :], hi.bitcast(F32), ALU.subtract)\
                            .then_inc(sem(tag + "_a_ready"), 1)
                with dve.Fori(0, KF // 2) as i:
                    body(i, False)

            def sum_out(tag):
                nc.vector.memset(acc[:, :], 0.0).then_inc(sem(tag + "_acc_zero"), 1)
                dve.wait_ge(*nth(tag + "_acc_zero", 1))
                for m in range(KD):
                    dve.wait_ge(*nth(tag + "_sq", m + 1))
                    if m:
                        dve.wait_ge(*nth(tag + "_acc", m))
                    nc.vector.tensor_tensor(acc[:, :], acc[:, :], sq[:, m % 2, :], ALU.add).then_inc(sem(tag + "_acc"), 1)

            def post_norm(tag, gain, factor, y):
                dve.wait_ge(*nth(tag + "_post_rstd", 1))
                dve.wait_ge(*nth(tag + "_y_read", KD))
                for k in range(KD):
                    nc.vector.scalar_tensor_tensor(tmp[:, k % 2, :], y[:, k, :], param(gain, k), rstd[:, :],
                                                   ALU.mult, ALU.mult).then_inc(sem(tag + "_scaled"), 1)
                    dve.wait_ge(*nth(tag + "_scaled", k + 1))
                    nc.vector.scalar_tensor_tensor(xT[:, k, :], tmp[:, k % 2, :], factor, xT[:, k, :],
                                                   ALU.mult, ALU.add).then_inc(sem(tag + "_x_ready"), 1)

            for k in range(KD):
                dve.wait_ge(*nth("x_turned", k + 1))
                nc.vector.tensor_copy(xT[:, k, :], bank[k][:, :]).then_inc(sem("start_x_ready"), 1)
            dve.wait_ge(*nth("params_in", 16))
            sinks = prm[:, COL["sinks"]:COL["sinks"] + NH]
            nc.vector.tensor_scalar(sinks, sinks, -1.0, None, ALU.mult).then_inc(sem("sinks_step"), 1)
            dve.wait_ge(*nth("sinks_step", 1))
            pre_norm("ffn1", "ffn1_pre", "ffn1_h_ready")
            ffn_up("ffn1")
            sum_out("ffn1")
            post_norm("ffn1", "ffn1_post", 0.5, yT)

            pre_norm("mix", "mix_pre", "mix_h_ready")
            TURN = (6.28125, 0.0019350051879882812, 3.0199159819e-7)
            step = [0]

            def link(ins):
                step[0] += 1
                ins.then_inc(sem("angle_step"), 1)
                dve.wait_ge(*nth("angle_step", step[0]))

            a0, a1, a2 = (ang[:, i, :] for i in range(3))
            dve.wait_ge(*nth("positions_in", 16))
            link(nc.vector.tensor_copy(a0, pos[:, :]))
            link(nc.vector.tensor_scalar(a0, a0, param("inv_freq"), None, ALU.mult))
            link(nc.vector.tensor_scalar(a1, a0, 1.0 / (2.0 * math.pi), ROUND, ALU.mult, ALU.add))
            link(nc.vector.tensor_scalar(a1, a1, -ROUND, None, ALU.add))
            for part in TURN:
                link(nc.vector.scalar_tensor_tensor(a0, a1, -part, a0, ALU.mult, ALU.add))
            link(nc.vector.tensor_scalar(a0, a0, PI_BELOW, -PI_BELOW, ALU.min, ALU.max))
            link(nc.vector.tensor_scalar(a2, a0, -1.0, None, ALU.mult))
            link(nc.vector.tensor_tensor(a2, a2, a0, ALU.max))
            dve.wait_ge(*nth("sine", 2))
            nc.vector.tensor_scalar(sin_t[:, :], sin_t[:, :], param("rot_sign"), None, ALU.mult)\
                .then_inc(sem("sine_step"), 1)
            dve.wait_ge(*nth("sine_step", 1))
            for i in range(6):
                dve.wait_ge(*nth("rot_done", i + 1))
                if i < 2:
                    b, r, to, factor = bank[2 * i][:, :], bank[2 * i + 1][:, :], k_rot[:, i, :], 1.0
                else:
                    b, to, factor = z[:, i, :], q_rot[:, i - 2, :], -0.125
                    r = bank[(i - 2) % 2 if i < 4 else i - 2][:, :]
                if i:
                    dve.wait_ge(*nth("rot_used", i))
                nc.vector.scalar_tensor_tensor(tmp[:, 0, :], b, factor, cos_t[:, :], ALU.mult, ALU.mult)\
                    .then_inc(sem("rot_step"), 1)
                nc.vector.scalar_tensor_tensor(tmp[:, 1, :], r, factor, sin_t[:, :], ALU.mult, ALU.mult)\
                    .then_inc(sem("rot_step"), 1)
                dve.wait_ge(*nth("rot_step", 2 * i + 2))
                nc.vector.tensor_tensor(to, tmp[:, 0, :], tmp[:, 1, :], ALU.add).then_inc(sem("rot_used"), 1)

            nc.vector.memset(win[:, :, 0:PAD], 0.0).then_inc(sem("win_step"), 1)
            dve.wait_ge(*nth("win_step", 1))
            dve.wait_ge(*nth("z_read", 10))
            dve.wait_ge(*nth("mix_const_in", 16))
            adds = 1
            for g in range(4):
                if g:
                    dve.wait_ge(*nth("pool_product", g))
                nc.vector.tensor_copy(win[:, 0, PAD:], z[:, 6 + g, :]).then_inc(sem("win_step"), 1)
                adds += 1
                dve.wait_ge(*nth("win_step", adds))
                src = 0
                for j in range(g + 1):
                    k = 1 << j
                    nc.vector.tensor_tensor(win[:, 1 - src, PAD:], win[:, src, PAD:], win[:, src, PAD - k:PAD + S - k],
                                            ALU.add).then_inc(sem("win_step"), 1)
                    src = 1 - src
                    adds += 1
                    dve.wait_ge(*nth("win_step", adds))
                u = z[:, 6 + g, :]
                nc.vector.tensor_tensor(win[:, 1 - src, PAD:2 * PAD], win[:, src, PAD:2 * PAD], inv_count[:, g, :],
                                        ALU.mult).then_inc(sem("win_step"), 1)
                adds += 1
                dve.wait_ge(*nth("win_step", adds))
                nc.vector.tensor_tensor(dif[:, 0:PAD], win[:, 1 - src, PAD:2 * PAD], u[:, 0:PAD], ALU.subtract)\
                    .then_inc(sem("win_step"), 1)
                adds += 1
                nc.vector.scalar_tensor_tensor(dif[:, PAD:], win[:, src, 2 * PAD:], 1.0 / (2 << g), u[:, PAD:],
                                               ALU.mult, ALU.subtract).then_inc(sem("pool_diff"), 1)
                dve.wait_ge(*nth("pool_product", g + 1))
                nc.vector.tensor_scalar(mixed[:, g, :], bank[7][:, :], param("pool_scale", g), None, ALU.mult)\
                    .then_inc(sem("pooled"), 1)

            units = [(n, g) for n in range(NT) for g in range(2)]

            def mask(n, g, unit):
                width = (2 if n else 1) * P
                dve.wait_ge(*nth("swa_scores", 2 * (unit + 1)))
                if unit >= 2:
                    dve.wait_ge(*nth("swa_turned", unit - 1))
                for h in range(4):
                    e, i = h % 2, h // 2
                    nc.vector.tensor_tensor_reduce(sc[:, unit % 2, h, 0:width],
                                                   bank[2 * (unit % 2) + e][:, i * width:(i + 1) * width],
                                                   band[:, 2 * P - width:], 1.0, param("sinks", 4 * g + h),
                                                   ALU.add, ALU.min, small[:, unit % 2, 0, h:h + 1])\
                        .then_inc(sem("swa_masked"), 1)
                dve.wait_ge(*nth("swa_masked", 4 * (unit + 1)))
                c = COL["sinks"] + 4 * g
                nc.vector.tensor_tensor(small[:, unit % 2, 2, :], small[:, unit % 2, 0, :], prm[:, c:c + 4],
                                        ALU.subtract).then_inc(sem("swa_sink_arg"), 1)

            def normalise(n, g, unit):
                width = (2 if n else 1) * P
                sm = small[:, unit % 2, :, :]
                dve.wait_ge(*nth("swa_sink_exp", unit + 1))
                dve.wait_ge(*nth("swa_exp", 4 * (unit + 1)))
                nc.vector.tensor_tensor(sm[:, 3, :], sm[:, 1, :], sm[:, 2, :], ALU.add).then_inc(sem("swa_step"), 1)
                dve.wait_ge(*nth("swa_step", 2 * unit + 1))
                nc.vector.reciprocal(sm[:, 3, :], sm[:, 3, :]).then_inc(sem("swa_step"), 1)
                dve.wait_ge(*nth("swa_step", 2 * unit + 2))
                for h in range(4):
                    nc.vector.tensor_scalar(sc[:, unit % 2, h, 0:width], sc[:, unit % 2, h, 0:width],
                                            sm[:, 3, h:h + 1], None, ALU.mult).then_inc(sem("swa_probs"), 1)

            mask(*units[0], 0)
            for u, (n, g) in enumerate(units):
                if u + 1 < len(units):
                    mask(*units[u + 1], u + 1)
                normalise(n, g, u)
            pre_norm("pool", "g_pool", "wout_h_ready", src=mixed, n=4)
            pre_norm("attn", "g_attn", "wout_h_ready", src=mixed, k0=4, n=4)
            sum_out("wout")
            post_norm("wout", "mix_post", 1.0, mixed)

            pre_norm("ffn2", "ffn2_pre", "ffn2_h_ready")
            ffn_up("ffn2")
            sum_out("ffn2")
            post_norm("ffn2", "ffn2_post", 0.5, yT)

            pre_norm("nsa", "attn_norm", "nsa_h_ready")
            dve.wait_ge(*nth("nsa_small_in", 8 * 16))
            nc.vector.memset(rel[32:33, :], 1.0).then_inc(sem("rel_one"), 1)
            job = [0]

            def job_bank():
                job[0] += 1
                dve.wait_ge(*nth("nsa_job", job[0]))
                return bank[2 + (job[0] - 1) % 2]

            for v in range(2):
                nc.vector.tensor_copy(v2_tok[:, v, :, :].rearrange("p n c -> p (n c)"), job_bank()[:, :])\
                    .then_inc(sem("nsa_read"), 1)
            for v in range(2):
                for g in range(2):
                    b = job_bank()[:, :].rearrange("p (t o) -> p o t", o=2)
                    for o in range(2):
                        last = nc.vector.tensor_copy(pair[64 * o:64 * o + 64, v, g, :], b[64 * o:64 * o + 64, o, :])
                    last.then_inc(sem("nsa_read"), 1)
            for a, b in ((0, S), (S, 5 * P)):
                nc.vector.tensor_copy(rv[:, a:b], job_bank()[0:NH, 0:b - a]).then_inc(sem("nsa_read"), 1)
            nc.vector.tensor_copy(gate_tok[:, :, :].rearrange("p n c -> p (n c)"), job_bank()[:, 0:NT * 24])\
                .then_inc(sem("nsa_read"), 1)
            for v in range(2):
                dve.wait_ge(*nth("nsa_read", 6))
                for half in range(2):
                    at = slice(8 * half, 8 * half + 8)
                    nc.vector.tensor_tensor(
                        cmp_blocks[v][:, at, :, :],
                        pair[:, v, :, :].rearrange("p g (b j) -> p j g b", j=8)[:, :, :, half:half + NCMP],
                        pe_in[:, v, at].unsqueeze(2).unsqueeze(3).to_broadcast([P, 8, 2, NCMP]), ALU.add)\
                        .then_inc(sem("blocks_ready"), 1)
            for i in range(2):
                dve.wait_ge(*nth("head_rstd", i + 1))
                nc.vector.tensor_tensor(zn[:, i, :], zn[:, i, :], tmp[:, i, :], ALU.mult)\
                    .then_inc(sem("head_rstd_used"), 1)
            for i in range(2, 6):
                dve.wait_ge(*nth("head_rstd", i + 1))
                nc.vector.scalar_tensor_tensor(reverse(qn[:, i - 2, :]), by_tile(zn[:, i + 4, :]), param("q_norm"),
                                               by_tile(tmp[:, i % 2, :]),
                                               ALU.mult, ALU.mult).then_inc(sem("head_rstd_used"), 1)
            for c in range(4):
                nc.vector.tensor_scalar(kd[:, c, :], job_bank()[:, :], param("k_norm"), -HD ** -0.5, ALU.mult,
                                        ALU.mult).then_inc(sem("nsa_read"), 1)
            chain = [0]

            def link(ins):
                chain[0] += 1
                ins.then_inc(sem("cmp_step"), 1)
                dve.wait_ge(*nth("cmp_step", chain[0]))

            for v in range(2):
                w = 2 * NCMP
                b = job_bank()[:, 0:2 * 64].rearrange("p (h c) -> p h c", h=2)
                nc.vector.tensor_copy(hid[:, :, 0:w], b[:, :, 0:w]).then_inc(sem("nsa_read"), 1)
                dve.wait_ge(*nth("nsa_read", job[0]))
                x, t = hid[:, :, 0:w], hid2[:, :, 0:w]
                link(nc.vector.tensor_tensor(t, x, x, ALU.mult))
                link(nc.vector.scalar_tensor_tensor(t, t, 0.044715, x, ALU.mult, ALU.mult))
                nc.vector.tensor_tensor(t, t, x, ALU.add).then_inc(sem("gelu_arg"), 1)
                dve.wait_ge(*nth("gelu_tanh", v + 1))
                link(nc.vector.scalar_tensor_tensor(t, t, 1.0, x, ALU.add, ALU.mult))
                nc.vector.tensor_scalar(x, t, 0.5, None, ALU.mult).then_inc(sem("gelu"), 1)
                dve.wait_ge(*nth("gelu", v + 1))
                if v == 0:
                    nc.vector.tensor_copy(kcn[:, :], job_bank()[:, 0:w]).then_inc(sem("nsa_read"), 1)
                    dve.wait_ge(*nth("head_rstd", 7))
                    link(nc.vector.tensor_tensor(kcn[:, :], kcn[:, :], tmp[:, 0, 0:w], ALU.mult))
                    nc.vector.tensor_scalar(kcn[:, :], kcn[:, :], param("k_norm"), -HD ** -0.5, ALU.mult, ALU.mult)\
                        .then_inc(sem("kc_normed"), 1)
                else:
                    nc.vector.tensor_copy(vct[:, :, :].rearrange("n g d -> n (g d)"), job_bank()[0:NCMP, 0:2 * HD])\
                        .then_inc(sem("nsa_read"), 1)
            dve.wait_ge(*nth("toeplitz_in", 16))

            def nsa_mask(n, g, unit):
                if unit >= 2:
                    dve.wait_ge(*nth("nsa_out_read", unit - 1))
                for i in range(10):
                    b = bank[i % 4] if unit % 2 == 0 else bank[(i + 2) % 4]
                    dve.wait_ge(*nth("nsa_scores", 10 * unit + i + 1))
                    if i < 8:
                        nc.vector.tensor_tensor_reduce(E[:, unit % 2, i, 0:(n + 1) * P], b[:, 0:(n + 1) * P],
                                                       toeplitz[:, 4 * g + i % 4, (3 - n) * P:], 1.0, 3.0e38,
                                                       ALU.add, ALU.min, stat[:, unit % 2, 0, 4 + i:5 + i])\
                            .then_inc(sem("nsa_masked"), 1)
                    else:
                        c0 = 31 + (3 - n) * P
                        for k in range(2):
                            h = 2 * k + i - 8
                            last = nc.vector.tensor_tensor_reduce(
                                Ec[:, unit % 2, h, 0:8 * n + 7], b[:, k * 32:k * 32 + 8 * n + 7],
                                toeplitz[:, 4 * g + h, c0:c0 + 16 * (8 * n + 6) + 1:16], 1.0, 3.0e38,
                                ALU.add, ALU.min, stat[:, unit % 2, 0, h:h + 1])
                        last.then_inc(sem("nsa_masked"), 1)

            wstep = [0]

            def nsa_weights(n, g, unit):
                def link(ins):
                    wstep[0] += 1
                    ins.then_inc(sem("nsa_weight_step"), 1)
                    dve.wait_ge(*nth("nsa_weight_step", wstep[0]))
                st = stat[:, unit % 2, :, :]
                dve.wait_ge(*nth("nsa_exp", 12 * (unit + 1)))
                link(nc.vector.reciprocal(st[:, 2, :], st[:, 1, :]))
                gates = gate_tok[:, n, 12 * g:12 * g + 12].rearrange("p (h b) -> p b h", b=3)
                link(nc.vector.tensor_tensor(st[:, 2, :].rearrange("p (b h) -> p b h", b=3),
                                             st[:, 2, :].rearrange("p (b h) -> p b h", b=3), gates, ALU.mult))
                if n == 0:
                    link(nc.vector.tensor_scalar(st[:, 2, 0:4], st[:, 2, 0:4], param("sees_block"), None, ALU.mult))
                for h in range(4):
                    s = Ec[:, unit % 2, h, 0:8 * n + 7]
                    nc.vector.tensor_scalar(s, s, st[:, 2, h:h + 1], None, ALU.mult)
                for i in range(8):
                    s = E[:, unit % 2, i, 0:(n + 1) * P]
                    last = nc.vector.tensor_scalar(s, s, st[:, 2, 4 + i:5 + i], None, ALU.mult)
                last.then_inc(sem("nsa_weighed"), 1)

            nsa_mask(*units[0], 0)
            for u, (n, g) in enumerate(units):
                if u + 1 < len(units):
                    nsa_mask(*units[u + 1], u + 1)
                nsa_weights(n, g, u)

            dve.wait_ge(*nth("rwkv_small_in", 4 * 16))
            steps = [0]

            def link(ins):
                steps[0] += 1
                ins.then_inc(sem("rw_step"), 1)
                dve.wait_ge(*nth("rw_step", steps[0]))

            def mix(j):
                for i, (a, _) in enumerate(RW_GROUPS):
                    if j == a:
                        dve.wait_ge(*nth(f"pin_in{i}", 16))
                if j:
                    dve.wait_ge(*nth("mixed_in", j))
                c = RW_ORDER[j]
                x, d = pin[:, c, :], tmp[:, 1, :]
                nc.vector.tensor_scalar(d[:, 0:1], x[:, 0:1], -1.0, None, ALU.mult)
                link(nc.vector.tensor_tensor(d[:, 1:], x[:, 0:S - 1], x[:, 1:], ALU.subtract))
                nc.vector.scalar_tensor_tensor(x, d, param("mu", c), x, ALU.mult, ALU.add)\
                    .then_inc(sem("mixed_in"), 1)

            def rw_prepare(m, step):
                r_, k_, v_ = pin[:, m, :], pin[:, 4 + m, :], pin[:, 8 + m, :]
                KK, MOD, AR = pair_sets[m % 2][:3]
                if step == 1:
                    dve.wait_ge(*nth("mixed_in", 3 * m + 5))
                    nc.vector.tensor_scalar(KK[:, :], k_, param("k_k", m), None, ALU.mult).then_inc(sem("kk"), 1)
                elif step == 2:
                    dve.wait_ge(*nth("lora_read", m + 1))
                    link(nc.vector.tensor_tensor_scan(CUM[:, :], reset[:, :], SG[:, :], 0.0, ALU.mult, ALU.add))
                    nc.vector.tensor_tensor(PREV[:, :], CUM[:, :], SG[:, :], ALU.subtract)\
                        .then_inc(sem("cumulative"), 1)
                    link(nc.vector.tensor_scalar(MOD[:, :], RATE[:, :], 1.0, param("k_a", m), ALU.subtract,
                                                 ALU.mult))
                    link(nc.vector.scalar_tensor_tensor(MOD[:, :], MOD[:, :], 1.0, k_, ALU.add, ALU.mult))
                    nc.vector.scalar_tensor_tensor(sq[:, 1, :], r_, param("r_k", m), MOD[:, :], ALU.mult, ALU.mult)\
                        .then_inc(sem("rk_product"), 1)
                elif step == 4:
                    dve.wait_ge(*nth("rw_head_sum", 2 * m + 2))
                    nc.vector.tensor_scalar(tmp[:, 0, :], bank[3][:, :], 1e-24, None, ALU.max)\
                        .then_inc(sem("kk_sum"), 1)
                    nc.vector.tensor_tensor(bonus[:, m, :], bank[7][:, :], v_, ALU.mult)\
                        .then_inc(sem("bonus_done"), 1)
                elif step == 6:
                    dve.wait_ge(*nth("decays", 3 * (m + 1)))
                    dve.wait_ge(*nth("kk_rstd", m + 1))
                    link(nc.vector.tensor_tensor(KK[:, :], KK[:, :], tmp[:, 0, :], ALU.mult))
                    link(nc.vector.scalar_tensor_tensor(AR[:, :, 0, :], by_tile(KK[:, :]), -1.0, by_tile(PREV[:, :]),
                                                        ALU.mult, ALU.mult))
                    nc.vector.tensor_tensor(AR[:, :, 1, :], by_tile(r_), by_tile(UPTO[:, :]), ALU.mult)\
                        .then_inc(sem("hats"), 1)
                    link(nc.vector.tensor_tensor(KK[:, :], KK[:, :], RATE[:, :], ALU.mult))
                    nc.vector.tensor_tensor(KK[:, :], KK[:, :], INV[:, :], ALU.mult).then_inc(sem("hats"), 1)
                    nc.vector.tensor_tensor(MOD[:, :], MOD[:, :], INV[:, :], ALU.mult).then_inc(sem("hats"), 1)
                    nc.vector.tensor_copy(PC[:, m, :], UPTO[:, C - 1::C]).then_inc(sem("hats"), 1)
                    dve.wait_ge(*nth("hats", 4 * (m + 1)))

            for j in range(14):
                mix(j)
                if j in PREPARE_AT:
                    rw_prepare(0, PREPARE_AT[j])
            wide = lambda b: b[:, :].rearrange("p (u t) -> p u t", u=4)
            eye = ident.unsqueeze(1).to_broadcast([P, 4, P])
            dve.wait_ge(*nth("mixed_in", 14))
            dve.wait_ge(*nth("fill_late", 16 * LATE))
            for m in range(4):
                AR = pair_sets[m % 2][2]
                for half in range(2):
                    for u in range(4):
                        dve.wait_ge(*nth("rw_scores", 8 * m + 4 * half + u + 1))
                        link(nc.vector.tensor_tensor(mats[:, half, u, :], bank[u if half else 4 + u][:, :],
                                                     mask4[:, :], ALU.mult))
                    nc.vector.tensor_tensor(OT[:, half, :, :], mats[:, half, :, 0:P],
                                            level[0].unsqueeze(1).to_broadcast([P, 4, P]), ALU.mult)\
                        .then_inc(sem("level_start"), 1)
                    dve.wait_ge(*nth("level_start", 2 * m + half + 1))
                    nc.vector.tensor_tensor(DT[:, half, :, :], OT[:, half, :, :], eye, ALU.add)\
                        .then_inc(sem("dt_ready"), 1)
                for half in range(2):
                    dve.wait_ge(*nth("level_turned", 2 * m + half + 1))
                    dve.wait_ge(*nth("dt_ready", 12 * m + half + 1))
                    nc.vector.tensor_tensor(Dm[:, half, :, :], wide(bank[0 if half else 4]), eye, ALU.add)\
                        .then_inc(sem("d_ready"), 1)
                if m < 3:
                    rw_prepare(m + 1, 1)
                for k in range(1, 6):
                    if k < 5:
                        for half in range(2):
                            dve.wait_ge(*nth("level_d", 8 * m + 2 * (k - 1) + half + 1))
                            dve.wait_ge(*nth("d_ready", 10 * m + 2 * (k - 1) + half + 1))
                            nc.vector.tensor_tensor(Dm[:, half, :, :], Dm[:, half, :, :],
                                                    wide(bank[1 if half else 5]), ALU.add)\
                                .then_inc(sem("d_ready"), 1)
                    for half in range(2):
                        dve.wait_ge(*nth("level_dt", 10 * m + 2 * (k - 1) + half + 1))
                        dve.wait_ge(*nth("dt_ready", 12 * m + 2 * (k - 1) + half + 1))
                        nc.vector.tensor_tensor(DT[:, half, :, :], DT[:, half, :, :], wide(bank[2 if half else 6]),
                                                ALU.add).then_inc(sem("dt_ready"), 1)
                    if m < 3:
                        rw_prepare(m + 1, k + 1)
                for half in range(2):
                    dve.wait_ge(*nth("chunk_terms", 2 * m + half + 1))
                    at = slice(half * 2 * P, (half + 1) * 2 * P)
                    qy = bank[2 if half else 6]
                    pair_of = lambda x: x.rearrange("p (n t) -> p n t", n=2)
                    nc.vector.tensor_tensor(pair_of(pin[:, m, at]), pair_of(qy[:, 0:2 * P]),
                                            AR[:, 2 * half:2 * half + 2, 1, :], ALU.add)
                    nc.vector.tensor_copy(yl[:, m, at], qy[:, 2 * P:])
                    for c in range(2):
                        mn = bank[c if half else 4 + c]
                        to = pin[:, 4 + m, at].rearrange("p (n c t) -> p c n t", n=2, c=2)[:, c, :, :]
                        nc.vector.tensor_tensor(to, pair_of(mn[:, 0:P]), eye2.unsqueeze(1).to_broadcast([P, 2, HD]),
                                                ALU.add)
                        to = pin[:, 8 + m, at].rearrange("p (n c t) -> p c n t", n=2, c=2)[:, c, :, :]
                        last = nc.vector.tensor_copy(to, pair_of(mn[:, P:2 * P]))
                    last.then_inc(sem("chunk_terms_read"), 1)
                dve.wait_ge(*nth("chunk_terms_read", 2 * m + 2))
            dve.wait_ge(*nth("rw_head_sum", 8))
            for c in range(NCH):
                at = slice(c * C, (c + 1) * C)
                if c < NCH - 1:
                    for e in range(2):
                        rows = slice(64 * e, 64 * e + 64)
                        to, n_ = state[rows, (c + 1) % 2, :, :], pin[rows, 8:12, at]
                        if c:
                            dve.wait_ge(*nth("state_product", 2 * (c - 1) + e + 1))
                            if c > 1:
                                dve.wait_ge(*nth("walk_y", 2 * (c - 1)))
                            link(nc.vector.tensor_tensor(to, bank[2 + e][rows, 0:4 * HD]
                                                         .rearrange("p (m i) -> p m i", m=4), n_, ALU.add))
                            n_ = to
                        nc.vector.tensor_tensor(to, n_, PC[rows, :, c:c + 1].to_broadcast([64, 4, HD]), ALU.mult)\
                            .then_inc(sem("state"), 1)
                if c:
                    for e in range(2):
                        rows = slice(64 * e, 64 * e + 64)
                        dve.wait_ge(*nth("walk_y", 2 * (c - 1) + e + 1))
                        y = yl[rows, :, at]
                        nc.vector.tensor_tensor(y, y, bank[e][rows, 0:4 * HD].rearrange("p (m i) -> p m i", m=4),
                                                ALU.add).then_inc(sem("walk_read"), 1)
            dve.wait_ge(*nth("walk_read", 2 * (NCH - 1)))
            for m in range(4):
                dve.wait_ge(*nth("gn_sum", m + 1))
                y = yl[:, m, :]
                nc.vector.scalar_tensor_tensor(y, bank[m][:, :], -1.0 / HD, y, ALU.mult, ALU.add)\
                    .then_inc(sem("gn_centred"), 1)
            for m in range(4):
                y = yl[:, m, :]
                dve.wait_ge(*nth("gn_rstd", m + 1))
                link(nc.vector.scalar_tensor_tensor(y, y, param("ln_g", m), gn_work[m], ALU.mult, ALU.mult))
                link(nc.vector.scalar_tensor_tensor(y, y, param("ln_b", m), bonus[:, m, :], ALU.add, ALU.add))
                dve.wait_ge(*nth("gn_gate", m + 1))
                nc.vector.tensor_tensor(o_hi[:, 4 + m, :], y, bank[4 + m][:, :], ALU.mult)
                nc.vector.tensor_tensor(y, y, bank[4 + m][:, :], ALU.mult).then_inc(sem("gn_out"), 1)
                dve.wait_ge(*nth("gn_out", m + 1))
                nc.vector.tensor_tensor(o_lo[:, 4 + m, :], y, o_hi[:, 4 + m, :].bitcast(F32), ALU.subtract)\
                    .then_inc(sem("o_ready"), 1)
            dve.wait_ge(*nth("oA_in", 16))
            for m in range(4):
                link(nc.vector.tensor_copy(o_hi[:, m, :], oA2[:, m, :]))
                nc.vector.tensor_tensor(o_lo[:, m, :], oA2[:, m, :], o_hi[:, m, :].bitcast(F32), ALU.subtract)\
                    .then_inc(sem("o_ready"), 1)

            dve.wait_ge(*nth("merge_gate", 4))
            for m in range(KD):
                dve.wait_ge(*nth("w_used", FIRST["merge"] + m + 1))
                b = 2 * (m % 4)
                if m:
                    dve.wait_ge(*nth("m_ready", m))
                for j in range(2):
                    link(nc.vector.tensor_tensor(sq[:, j, :], gates[:, KD * j + m, :], bank[b + j][:, :], ALU.mult))
                nc.vector.tensor_tensor(m_hi[:, m, :], sq[:, 0, :], sq[:, 1, :], ALU.add).then_inc(sem("gates_used"), 1)
                dve.wait_ge(*nth("gates_used", m + 1))
                link(nc.vector.tensor_tensor(sq[:, 0, :], sq[:, 0, :], sq[:, 1, :], ALU.add))
                nc.vector.tensor_tensor(m_lo[:, m, :], sq[:, 0, :], m_hi[:, m, :].bitcast(F32), ALU.subtract)\
                    .then_inc(sem("m_ready"), 1)
            dve.wait_ge(*nth("x_back", 16))
            for m in range(KD):
                dve.wait_ge(*nth("w_used", FIRST["w_out_2"] + m + 1))
                nc.vector.tensor_tensor(xT[:, m, :], xT[:, m, :], bank[4 + m % 4][:, :], ALU.add)\
                    .then_inc(sem("conv_x_ready"), 1)

            pre_norm("conv", "ffn_norm", "conv_h_ready")

            def conv_pair(i, first):
                for u in range(2):
                    p = 2 * i + u
                    for v in range(2):
                        dve.wait_ge(*nth("w_used", FIRST["conv_up"] + 4 * i + 2 * u + v + 1))
                        b, c = bank[2 * u + v], tmp[:, v, :]
                        if v == 1 and not (first and u == 0):
                            dve.wait_ge(*nth("conv_silu", p))
                        w = [prm[:, bass.ds(p + (COL[f"conv_{x}"] + KF * v), 1)] for x in ("w0", "w1", "w2", "b")]
                        nc.vector.tensor_scalar(c, b[:, :], w[2], w[3], ALU.mult, ALU.add)\
                            .then_inc(sem("conv_step"), 1)
                        dve.wait_ge(*nth("conv_step", 4 * p + 2 * v + 1))
                        nc.vector.scalar_tensor_tensor(c[:, 1:], b[:, 0:S - 1], w[1], c[:, 1:], ALU.mult, ALU.add)\
                            .then_inc(sem("conv_step"), 1)
                        dve.wait_ge(*nth("conv_step", 4 * p + 2 * v + 2))
                        last = nc.vector.scalar_tensor_tensor(c[:, 2:], b[:, 0:S - 2], w[0], c[:, 2:], ALU.mult,
                                                              ALU.add)
                        last.then_inc(sem("conv_pair_read" if v else "conv_value"), 1)
                    hi, lo = (a[:, bass.ds(p, 1), :].rearrange("q a t -> q (a t)") for a in (a_hi, a_lo))
                    dve.wait_ge(*nth("conv_value", p + 1))
                    dve.wait_ge(*nth("conv_silu", p + 1))
                    nc.vector.tensor_tensor(hi, tmp[:, 0, :], sq[:, 0, :], ALU.mult).then_inc(sem("conv_a32"), 1)
                    nc.vector.tensor_tensor(sq[:, 1, :], tmp[:, 0, :], sq[:, 0, :], ALU.mult)\
                        .then_inc(sem("conv_a32"), 1)
                    dve.wait_ge(*nth("conv_a32", 2 * p + 2))
                    nc.vector.tensor_tensor(lo, sq[:, 1, :], hi.bitcast(F32), ALU.subtract)\
                        .then_inc(sem("conv_a_ready"), 1)
            conv_pair(0, True)
            with dve.Fori(1, KF // 2) as i:
                conv_pair(i, False)
            for m in range(KD):
                dve.wait_ge(*nth("w_used", FIRST["conv_down"] + 3 * (m + 1)))
                nc.vector.tensor_tensor(xT[:, m, :], xT[:, m, :], bank[4 + m % 4][:, :], ALU.add)\
                    .then_inc(sem("end_x_ready"), 1)
            for i in range(2 * NT):
                dve.wait_ge(*nth("out_turned", i + 1))
                nc.vector.tensor_copy(yT[:, i, :], bank[i][:, :]).then_inc(sem("out_copied"), 1)


def _layouts(inputs):
    import numpy as np
    f32 = np.float32

    def blocks(w):
        k, n = w.shape
        return w.reshape(k // P, P, n // P, P).transpose(2, 1, 0, 3).reshape(n // P, P, k)

    def pairs(w):
        b = blocks(w)
        return np.stack([b[:KF], b[KF:]], 1).reshape(2 * KF, P, D)

    def columns(v):
        return v.reshape(-1, P).T

    one = {name: (a[0] if a.shape[0] == 1 and name not in ("x", "positions") else a) for name, a in inputs.items()}
    cols = lambda name: columns(one[name].reshape(-1))
    conv_w = one["conv_w_2"]
    ch = np.arange(P)
    rope_of = ch % HD
    freq = 500000.0 ** (-(np.arange(0, 16, 2, dtype=f32)) / f32(16))
    values = {
        "ffn1_pre": cols("ffn1_pre"), "ffn1_post": cols("ffn1_post"), "mix_pre": cols("mix_pre"),
        "mix_post": cols("mix_post"), "ffn2_pre": cols("ffn2_pre"), "ffn2_post": cols("ffn2_post"),
        "attn_norm": cols("attn_norm_g_2"), "ffn_norm": cols("ffn_norm_g_2"), "pool_scale": cols("pool_scale"),
        "g_pool": cols("g_pool"), "g_attn": cols("g_attn"), "sinks": np.tile(one["sinks"], (P, 1)),
        "eps": np.full((P, 1), EPS), "half_pi": np.full((P, 1), math.pi / 2),
        "inv_freq": np.where(rope_of < 16, freq.astype(f32)[rope_of % 8], 0)[:, None],
        "rot_sign": np.where(rope_of < 8, -1, 1)[:, None],
        "q_norm": np.tile(one["q_norm_g_2"], 2)[:, None], "k_norm": np.tile(one["k_norm_g_2"], 2)[:, None],
        "sees_block": (P - 1 - ch >= 31)[:, None], "mu": cols("rwkv_mu_2"), "w0": cols("rwkv_w0_2"), "a0": cols("rwkv_a0_2"),
        "k_k": cols("rwkv_k_k_2"), "k_a": cols("rwkv_k_a_2"), "r_k": cols("rwkv_r_k_2"), "ln_g": cols("rwkv_ln_g_2"),
        "ln_b": cols("rwkv_ln_b_2"), "gn_eps": np.full((P, 1), 64e-5), "ln_256": np.full((P, 1), 8 * math.log(2)),
        "conv_b": cols("conv_b_2"), "conv_w0": columns(conv_w[0]), "conv_w1": columns(conv_w[1]),
        "conv_w2": columns(conv_w[2])}
    params = np.concatenate([values[name].astype(f32) for name, _ in PARAMS], 1)

    def takes(from_of):
        a = np.zeros((P, P), f32)
        a[from_of(ch), ch] = 1
        return a

    def rotated(c):
        d = c % HD
        return np.where(d < 8, c + 8, np.where(d < 16, c - 8, c))
    dup = [takes(lambda c, g=g: HD * g + c % HD) for g in range(2)]
    dup_rot = [takes(lambda c, g=g: HD * g + rotated(c % HD)) for g in range(2)]
    diff = ch[:, None] + P - np.arange(2 * P)[None]
    band = np.where((diff >= 0) & (diff < P), 0, 1e30).astype(f32)
    first = np.arange(16) + 1
    inv_count = np.stack([1 / np.minimum(first, w) for w in (2, 4, 8, 16)]).astype(f32).reshape(1, 64).repeat(P, 0)
    mix_const = np.concatenate([takes(rotated)] + dup + dup_rot + [band, inv_count], 1)

    dist = S - 1 - np.arange(5 * P)
    n = np.maximum(dist, 0)
    ratio = np.log(np.maximum(n, 1).astype(f32) / f32(16)) / f32(math.log(128 / 16))
    bucket = np.where(n < 16, n, np.minimum(16 + (ratio * f32(16)).astype(np.int32), 31))
    code = np.zeros((33, 5 * P), f32)
    code[bucket, np.arange(5 * P)] = -1
    code[:, dist < 0] = 0
    code[32, dist < 0] = 1e30
    head_ones = np.kron(np.eye(2), np.ones((HD, HD))).astype(f32)

    s, t = ch[:, None], ch[None]
    before, upto = (s // C == t // C) & (s < t), (s // C == t // C) & (s <= t)
    levels = [(s >> (k + 1) == t >> (k + 1)) & ((s >> k) % 2 == 0) & ((t >> k) % 2 == 1) for k in range(6)]
    reset = np.tile(np.arange(S) % C != 0, (P, 1))
    rwkv_const = np.concatenate([before, upto, before, upto, reset] + levels
                                + [head_ones, np.tile(np.eye(HD), (2, 1))], 1).astype(f32)

    w2 = one["w_in_2"]
    part = lambda a, b: blocks(w2[:, a:b])
    merge = np.concatenate([blocks(one["w_proj_a_2"]), blocks(one["w_proj_b_2"])], 2)
    pe = [one[n].reshape(16, P).T for n in ("cmp_pe_k_2", "cmp_pe_v_2")]
    return dict(
        x=inputs["x"], positions=inputs["positions"], params=params,
        const=np.concatenate([np.eye(P), np.ones((P, P))], 1).astype(f32), mix_const=mix_const,
        w_pool=one["w_pool"], w_ffn1_gu=pairs(one["ffn1_w_gu"]), w_ffn1_down=blocks(one["ffn1_w_down"]),
        w_in=blocks(one["w_in"])[[8, 9, 4, 5, 6, 7, 0, 1, 2, 3]], w_out=blocks(one["w_out"]),
        w_ffn2_gu=pairs(one["ffn2_w_gu"]), w_ffn2_down=blocks(one["ffn2_w_down"]),
        w_nsa=np.concatenate([part(768, 896), part(1024, 1152), part(896, 1024), part(1152, 1280), part(512, 640),
                              part(640, 768), part(0, 512), part(1280, 1408)]),
        nsa_const=np.concatenate(dup + [head_ones, np.eye(P)[::-1]], 1).astype(f32), rel_bias=inputs["rel_bias_2"], distance_code=code,
        cmp_pe=np.stack(pe), cmp_w1=np.stack([one["cmp_w1_k_2"], one["cmp_w1_v_2"]]),
        cmp_w2=np.stack([one["cmp_w2_k_2"], one["cmp_w2_v_2"]]), w_rwkv=part(1304, 3096)[list(RW_ORDER)], rwkv_const=rwkv_const,
        rwkv_w2a2=np.concatenate([one["rwkv_w2_2"], one["rwkv_a2_2"]]), rwkv_g2=one["rwkv_g2_2"],
        w_gates=part(3096, 5144),
        w_merge=merge, w_out_2=blocks(one["w_out_2"]), w_conv_up=pairs(one["w_up_2"]),
        w_conv_down=blocks(one["w_down_2"]))


def kernel(**inputs):
    import numpy as _np
    import concourse.bacc as _bacc
    from concourse import mybir as _mybir
    from concourse.bass_utils import run_bass_kernel_spmd as _run

    nc = _bacc.Bacc("TRN2", target_bir_lowering=False, num_devices=1)
    laid_out = _layouts({name: _np.asarray(a) for name, a in inputs.items()})
    arrays, args = {}, {}
    for name, a in laid_out.items():
        a = _np.ascontiguousarray(a)
        arrays[f"{name}_dram"] = a
        args[name] = nc.dram_tensor(f"{name}_dram", a.shape, _mybir.dt.from_np(a.dtype), kind="ExternalInput").ap()
    out = nc.dram_tensor("out_dram", (1, S, D), F32, kind="ExternalOutput").ap()
    build(nc, out=out, **args)
    r = _run(nc, [arrays], core_ids=[0])
    return r.results[0]["out_dram"]
```

```python
import math
from contextlib import ExitStack

import concourse.bass as bass
from concourse import mybir

F32 = mybir.dt.float32
F32R = mybir.dt.float32r
I32 = mybir.dt.int32
ACT = mybir.ActivationFunctionType
ALU = mybir.AluOpType

P = 128
S = 512
D = 1024
KD = D // P
NT = S // P
FF = 2816
KF = FF // P
EPS = 1e-6
NH = 8
HD = 64
C = 64
NCH = S // C
KAPPA = math.exp(-0.5)
CMP_H = 256
NCMP = S // 16 - 1
ROUND = 12582912.0
PI_BELOW = 3.1415925
RING = 4
CHUNK = KD * P
DOWN_SPLIT = ((0, 8), (8, 15), (15, 22))

STREAM = (("ffn1_up", 2 * KF), ("ffn1_down", 3 * KD), ("w_in", 10), ("w_out", KD), ("ffn2_up", 2 * KF),
          ("ffn2_down", 3 * KD), ("nsa", 11), ("rwkv", 14), ("gates", 2 * KD), ("merge", KD), ("w_out_2", KD),
          ("conv_up", 2 * KF), ("conv_down", 3 * KD), ("end", 0))
FIRST = {}
_n = 0
for _stage, _count in STREAM:
    FIRST[_stage] = _n
    _n += _count

PARAMS = (("ffn1_pre", KD), ("ffn1_post", KD), ("mix_pre", KD), ("mix_post", KD), ("ffn2_pre", KD),
          ("ffn2_post", KD), ("attn_norm", KD), ("ffn_norm", KD), ("pool_scale", 4), ("g_pool", 4),
          ("g_attn", 4), ("sinks", 8), ("eps", 1), ("half_pi", 1), ("inv_freq", 1), ("rot_sign", 1), ("q_norm", 1),
          ("k_norm", 1), ("sees_block", 1), ("mu", 14), ("w0", 4), ("a0", 4), ("k_k", 4), ("k_a", 4), ("r_k", 4),
          ("ln_g", 4), ("ln_b", 4), ("gn_eps", 1), ("ln_256", 1), ("conv_b", 2 * KF), ("conv_w0", 2 * KF),
          ("conv_w1", 2 * KF), ("conv_w2", 2 * KF))
COL = {}
_n = 0
for _name, _count in PARAMS:
    COL[_name] = _n
    _n += _count
NPARAM = _n

RW_ORDER = (12, 13, 0, 4, 8, 1, 5, 9, 2, 6, 10, 3, 7, 11)
RW_GROUPS = ((0, 2), (2, 5), (5, 8), (8, 11), (11, 14))
PREPARE_AT = {4: 1, 5: 2, 6: 4, 8: 6}
NFILL, LATE = 14 + 2 * KD, 7
NUNIT = 2 * NT
NORMS = (("ffn1", KD), ("mix", KD), ("pool", 4), ("attn", 4), ("ffn2", KD), ("nsa", KD), ("conv", KD))
RSQRTS = (("ffn1_in", 1), ("ffn1_post", 1), ("mix_in", 1), ("pool_in", 1), ("attn_in", 1), ("wout_post", 1),
          ("ffn2_in", 1), ("ffn2_post", 1), ("nsa_in", 1), ("head", 7), ("kk", 4), ("gn", 4), ("conv_in", 1))
UPS = (("ffn1", KF), ("ffn2", KF))
AHEAD = ("ffn1", "mix", "attn", "ffn2", "conv")
OUTS = (("ffn1", KD), ("wout", KD), ("ffn2", KD))
FAMILIES = {
    "in_sq": NORMS, "in_sq_used": NORMS, "h32": tuple((tag, n) for tag, n in NORMS if tag not in AHEAD),
    "gate_scaled": UPS, "silu_scaled": UPS,
    "h_hi": (("ffn1", KD), ("mix", KD), ("attn", 4), ("pool", 4), ("ffn2", KD), ("nsa", KD), ("conv", KD)),
    "h_ready": (("ffn1", KD), ("mix", KD), ("wout", KD), ("ffn2", KD), ("nsa", KD), ("conv", KD)),
    "x_ready": (("start", KD), ("ffn1", KD), ("wout", KD), ("ffn2", KD), ("conv", KD), ("end", KD)),
    "ln": RSQRTS, "rstd": RSQRTS, "post_sum": tuple((tag, 1) for tag, _ in OUTS),
    "pair_read": UPS + (("conv", KF),), "silu": UPS + (("conv", KF),), "a32": UPS + (("conv", 2 * KF),),
    "a_ready": UPS + (("conv", KF),), "sq": OUTS, "acc": OUTS, "y_read": (("ffn1", KD), ("ffn2", KD)), "scaled": OUTS,
    "acc_zero": tuple((tag, 1) for tag, _ in OUTS),
    "scores": (("swa", 2 * NUNIT), ("nsa", 10 * NUNIT)), "masked": (("swa", 4 * NUNIT), ("nsa", 10 * NUNIT)),
    "exp": (("swa", 4 * NUNIT), ("nsa", 12 * NUNIT)), "turned": (("swa", NUNIT), ("nsa", 0)),
    "out_read": (("swa", NUNIT), ("nsa", NUNIT)),
    "step": (("sinks", 1), ("angle", 10), ("sine", 2), ("rot", 12), ("win", 27), ("cmp", 7),
             ("nsa_weight", 2 * NUNIT + 2), ("rw", 0)),
}
SHARED = {}
for _kind, _stages in FAMILIES.items():
    _n = 0
    for _stage, _count in _stages:
        SHARED[_stage + "_" + _kind] = (_kind, _n)
        _n += _count


def build(nc, x, positions, params, const, mix_const, w_pool, w_ffn1_gu, w_ffn1_down, w_in, w_out, w_ffn2_gu,
          w_ffn2_down, w_nsa, nsa_const, rel_bias, distance_code, cmp_pe, cmp_w1, cmp_w2,
          w_rwkv, rwkv_const, rwkv_w2a2, rwkv_g2, w_gates, w_merge, w_out_2, w_conv_up, w_conv_down, out):
    with ExitStack() as ctx:
        def sb(name, shape, dt=F32):
            return ctx.enter_context(nc.sbuf_tensor(name, shape, dt))

        sems = {}

        def sem(name):
            name = SHARED.get(name, (name, 0))[0]
            if name not in sems:
                sems[name] = ctx.enter_context(nc.semaphore(name))
            return sems[name]

        def nth(name, count):
            return sem(name), count + SHARED.get(name, (name, 0))[1]

        with ExitStack() as scope:
            xT = scope.enter_context(nc.sbuf_tensor("xT", [P, KD, S], F32))
        with ExitStack() as scope:
            KK0, MOD0, SG, RATE, CUM, UPTO = (scope.enter_context(nc.sbuf_tensor(n, [P, S], F32))
                                            for n in ("KK0", "MOD0", "SG", "RATE", "CUM", "UPTO"))
            UG = scope.enter_context(nc.sbuf_tensor("UG", [P, 2, 4, P], F32))
        with ExitStack() as scope:
            stage = scope.enter_context(nc.sbuf_tensor("stage", [P, 8, S], F32))
        x_place = ctx.enter_context(nc.sbuf_tensor("x_place", [P, KD * S], F32))
        prm = sb("prm", [P, NPARAM])
        cst = sb("cst", [P, 2, P])
        ident, ones = cst[:, 0, :], cst[:, 1, :]
        w_raw = sb("w_raw", [P, RING, CHUNK])
        w_hi = sb("w_hi", [P, RING, CHUNK], F32R)
        w_lo = sb("w_lo", [P, RING, CHUNK], F32R)
        one = sb("one", [P, 1])
        sq = sb("sq", [P, 2, S])
        acc = sb("acc", [P, S])
        rstd = sb("rstd", [P, S])
        tmp = sb("tmp", [P, 2, S])
        AkV = sb("AkV", [P, 2, 4, HD])
        rcs = sb("rcs", [P, 6 * P + P + HD])
        level = [rcs[:, P * i:P * (i + 1)] for i in range(6)]
        head_ones2, eye2 = rcs[:, 6 * P:7 * P], rcs[:, 7 * P:7 * P + HD]
        w2a2 = sb("w2a2", [P, 4 * P])
        PC = sb("PC", [P, 4, NCH])
        bank = [ctx.enter_context(nc.psum_tensor(f"bank{i}", [P, S], F32)) for i in range(8)]

        with ExitStack() as scope:
            h_hi = scope.enter_context(nc.sbuf_tensor("h_hi", [P, KD, S], F32R))
            h_lo = scope.enter_context(nc.sbuf_tensor("h_lo", [P, KD, S], F32R))
        with ExitStack() as scope:
            yT = scope.enter_context(nc.sbuf_tensor("yT", [P, KD, S], F32))
        def rw_pair_set(place, name, KK, MOD):
            return [KK, MOD, place("AR" + name, [P, NT, 2, P])] + [place(n + name, [P, NT, P])
                                                                   for n in ("At", "Bt", "Kt", "Vt")]
        with ExitStack() as scope:
            in_h = lambda name, shape: scope.enter_context(nc.sbuf_tensor(name, shape, F32))
            odd_set = rw_pair_set(in_h, "1", in_h("KK1", [P, S]), in_h("MOD1", [P, S]))
        with ExitStack() as scope:
            gates = scope.enter_context(nc.sbuf_tensor("gates", [P, 2 * KD, S], F32))
        hole = ctx.enter_context(nc.sbuf_tensor("hole", [P, 2 * KD * S], F32))
        with ExitStack() as scope:
            a_hi = scope.enter_context(nc.sbuf_tensor("a_hi", [P, KF, S], F32R))
            a_lo = scope.enter_context(nc.sbuf_tensor("a_lo", [P, KF, S], F32R))
        with ExitStack() as scope:
            x_tok = scope.enter_context(nc.sbuf_tensor("x_tok", [P, NT, D], F32))

        with ExitStack() as scope:
            def in_a(name, shape, dt=F32):
                return scope.enter_context(nc.sbuf_tensor(name, shape, dt))
            z = in_a("z", [P, 10, S])
            mixed = in_a("mixed", [P, KD, S])
            mcs = in_a("mcs", [P, 5 * P + 2 * P + 64])
            rot_of, dup_of = mcs[:, 0:P], [mcs[:, P * (1 + g):P * (2 + g)] for g in range(2)]
            dup_rot_of = [mcs[:, P * (3 + g):P * (4 + g)] for g in range(2)]
            band = mcs[:, 5 * P:7 * P]
            inv_count = mcs[:, 7 * P:7 * P + 64].rearrange("p (g t) -> p g t", g=4)
            wp = in_a("wp", [P, 4, P])
            pos = in_a("pos", [P, S], I32)
            ang = in_a("ang", [P, 3, S])
            cos_t, sin_t = in_a("cos_t", [P, S]), in_a("sin_t", [P, S])
            q_rot = in_a("q_rot", [P, 4, S])
            k_rot = in_a("k_rot", [P, 2, S])
            v_tok = in_a("v_tok", [P, NT, P])
            PAD = 16
            win = in_a("win", [P, 2, PAD + S])
            dif_of = [in_a("dif", [P, S])[:, :], ang[:, 1, :]]
            sc = in_a("sc", [P, 2, 4, 2 * P])
            pT = in_a("pT", [P, 2, 4, P])
            small = in_a("small", [P, 2, 4, 4])
        with ExitStack() as scope:
            with ExitStack() as early:
                def in_e(name, shape, dt=F32):
                    return early.enter_context(nc.sbuf_tensor(name, shape, dt))
                zn = in_e("zn", [P, 11, S])
                pair = in_e("pair", [P, 2, 2, S // 2])
                code = in_e("code", [33, 5 * P])
                rv = in_e("rv", [NH, 5 * P])
            cmp_blocks = [zn[:, a:a + 2, :].rearrange("p a b -> p (a b)")[:, 0:32 * NCMP]
                          .rearrange("p (j g b) -> p j g b", j=16, g=2) for a in (4, 2)]
            E = in_a("E", [P, 2, 8, S])
            with ExitStack() as early:
                cw1 = early.enter_context(nc.sbuf_tensor("cw1", [P, 16, CMP_H], F32))
            toeplitz = in_a("toeplitz", [P, NH, S])
            qn = in_a("qn", [P, 4, S])
            kd = in_a("kd", [P, 4, S])
            v2_tok = in_a("v2_tok", [P, 2, NT, P])
            p2T = in_a("p2T", [P, 2, 4, P])
            oA = in_a("oA", [P, 4, S])
            ncs = in_a("ncs", [P, 4 * P])
            flip = ncs[:, 3 * P:4 * P]
            dup2 = [ncs[:, P * g:P * (g + 1)] for g in range(2)]
            head_ones = ncs[:, 2 * P:3 * P]
            rel = in_a("rel", [33, NH])
            cw2 = in_a("cw2", [P, 2, 2, 2 * HD])
            pe_in = in_a("pe_in", [P, 2, 16])
            hid = in_a("hid", [P, 2, 64])
            hid2 = in_a("hid2", [P, 2, 64])
            kcn = in_a("kcn", [P, 2 * NCMP])
            vct = in_a("vct", [NCMP, 2, HD])
            gate_tok = in_a("gate_tok", [P, NT, 24])
            Ec = in_a("Ec", [P, 2, 4, 32])
            stat = in_a("stat", [P, 2, 3, 12])

        def fill_bank(f):
            return 4 + f % 4 if f < 14 else 7 if f < NFILL - LATE else (0, 1, 2, 4, 5, 6, 0)[f - NFILL + LATE]

        def by_tile(x):
            return x.rearrange("p (n t) -> p n t", n=NT)

        def reverse(x):
            return by_tile(x)[:, :, ::-1]

        def param(name, k=0):
            return prm[:, COL[name] + k:COL[name] + k + 1]

        with ExitStack() as scope:
            pin = in_a("pin", [P, 14, S])
            yl = in_a("yl", [P, 4, S])
            bonus = in_a("bonus", [P, 4, S])
            pair_sets = [rw_pair_set(in_a, "0", KK0, MOD0), odd_set]
            with ExitStack() as early:
                late_stage = early.enter_context(nc.sbuf_tensor("late_stage", [P, LATE, S], F32))
            mats = in_a("mats", [P, 2, 4, 4 * P])
            Dm, DT, X, OT = (in_a(n, [P, 2, 4, P]) for n in ("Dm", "DT", "X", "OT"))
        g2 = UG[:, 0, :, :].rearrange("p a b -> p (a b)")
        PREV, INV = SG, CUM
        gn_work = [sq[:, 0, :], sq[:, 1, :], tmp[:, 0, :], tmp[:, 1, :]]
        mask4, reset = rstd, acc
        state = sq[:, :, 0:4 * HD].rearrange("p s (m i) -> p s m i", m=4)
        with ExitStack() as scope:
            m_hi, m_lo = in_a("m_hi", [P, KD, S], F32R), in_a("m_lo", [P, KD, S], F32R)
            in_a("merge_pad", [P, 6 * S])
            o_hi, o_lo = in_a("o_hi", [P, KD, S], F32R), in_a("o_lo", [P, KD, S], F32R)
            oA2 = in_a("oA2", [P, 4, S])
        oA_dram = nc.dram_tensor("nsa_out", (P, 4 * S), F32)
        fill_dram = nc.dram_tensor("rwkv_and_gates", (P, NFILL * S), F32)
        x_dram = nc.dram_tensor("x_between", (P, KD * S), F32)
        bias_dram = nc.dram_tensor("bias_by_distance", (NH, 5 * P), F32)

        block = ctx.enter_context(nc.Block())

        @block.sync
        def _(sp):
            sp.dma_start(cst[:, :, :], const.rearrange("p (a b) -> p a b", a=2)).then_inc(sem("const_in"), 16)
            for n in range(NT):
                sp.dma_start(x_tok[:, n, :], x[0, n * P:(n + 1) * P, :]).then_inc(sem(f"x_in{n}"), 16)
            sp.dma_start(prm[:, :], params).then_inc(sem("params_in"), 16)

            def load(c, s, source, width=CHUNK, first=False):
                if not first:
                    sp.wait_ge(*nth("w_split", c - RING + 1))
                sp.dma_start(w_raw[:, s, 0:width], source).then_inc(sem(f"w_in{s}"), 16)

            def stream(c0, n, source, first=False):
                if first:
                    for u in range(RING):
                        load(u, u, source(u), first=True)
                with sp.Fori(1 if first else 0, n // RING) as i:
                    for u in range(RING):
                        load(i * RING + (c0 + u), (c0 + u) % RING, source(i * RING + u))
                for u in range(n - n % RING, n):
                    load(c0 + u, (c0 + u) % RING, source(u))

            def stream_down(c0, w):
                with sp.Fori(0, KD // RING) as i:
                    for u in range(RING):
                        for j, (a, b) in enumerate(DOWN_SPLIT):
                            v = c0 + 3 * u + j
                            load(i * (3 * RING) + v, v % RING, w[bass.ds(i * RING + u, 1), :, a * P:b * P]
                                 .rearrange("a p n -> (a p) n"), (b - a) * P)

            def begin(c0, source):
                for u in range(RING):
                    load(c0 + u, (c0 + u) % RING, source(u))

            def rest(c0, n, source):
                stream(c0 + RING, n - RING, lambda c: source(c + RING))

            def whole(w):
                return lambda c: w[bass.ds(c, 1), :, :].rearrange("a p n -> (a p) n")

            stream(FIRST["ffn1_up"], 2 * KF, whole(w_ffn1_gu), first=True)
            stream_down(FIRST["ffn1_down"], w_ffn1_down)

            begin(FIRST["w_in"], whole(w_in))
            sp.wait_ge(*nth("w_used", FIRST["w_in"]))
            sp.dma_start(mcs[:, :], mix_const).then_inc(sem("mix_const_in"), 16)
            sp.dma_start(pos[:, :], positions.partition_broadcast(P)).then_inc(sem("positions_in"), 16)
            sp.dma_start(wp[:, :, :], w_pool.rearrange("g c d -> c g d")).then_inc(sem("w_pool_in"), 16)
            rest(FIRST["w_in"], 10, whole(w_in))
            stream(FIRST["w_out"], KD, whole(w_out))
            stream(FIRST["ffn2_up"], 2 * KF, whole(w_ffn2_gu))
            stream_down(FIRST["ffn2_down"], w_ffn2_down)

            begin(FIRST["nsa"], whole(w_nsa))
            sp.wait_ge(*nth("w_used", FIRST["nsa"]))
            sp.dma_start(ncs[:, :], nsa_const).then_inc(sem("nsa_small_in"), 16)
            sp.dma_start(rel[0:32, :], rel_bias).then_inc(sem("nsa_small_in"), 16)
            sp.dma_start(code[:, :], distance_code).then_inc(sem("nsa_small_in"), 16)
            sp.dma_start(pe_in[:, :, :], cmp_pe.rearrange("v p j -> p v j")).then_inc(sem("nsa_small_in"), 16)
            for v in range(2):
                for c in range(2):
                    sp.dma_start(cw2[:, v, :, c * HD:(c + 1) * HD], cmp_w2[v].rearrange("(h p) d -> p h d", p=P))\
                        .then_inc(sem("nsa_small_in"), 16)
            sp.dma_start(cw1[:, :, :], cmp_w1[0].rearrange("(j p) n -> p j n", p=P)).then_inc(sem("cw1_in"), 16)
            rest(FIRST["nsa"], 11, whole(w_nsa))
            sp.wait_ge(*nth("nsa_h_ready", KD))
            sp.dma_start(x_dram.ap(), xT[:, :, :].rearrange("p a b -> p (a b)")).then_inc(sem("x_out"), 16)
            sp.dma_start(rcs[:, :], rwkv_const[:, 2 * S:]).then_inc(sem("rwkv_small_in"), 16)
            sp.dma_start(mask4[:, :], rwkv_const[:, 0:S]).then_inc(sem("rwkv_small_in"), 16)
            sp.dma_start(reset[:, :], rwkv_const[:, S:2 * S]).then_inc(sem("rwkv_small_in"), 16)
            sp.dma_start(w2a2[:, :], rwkv_w2a2).then_inc(sem("rwkv_small_in"), 16)
            stream(FIRST["rwkv"], 14, whole(w_rwkv))
            stream(FIRST["gates"], 2 * KD, whole(w_gates))

            sp.wait_ge(*nth("oA_out", 16 * NT))
            for group in range(2):
                sp.wait_ge(*nth(f"fill_out{group}", 16 * sum(f // 4 % 2 == group for f in range(NFILL - LATE))))
            for i, (a, b) in enumerate(RW_GROUPS):
                c = RW_ORDER[a]
                to = pin[:, 12:14, :] if i == 0 else pin[:, c:12:4, :]
                sp.dma_start(to, fill_dram.ap()[:, a * S:b * S].rearrange("p (a b) -> p a b", b=S))\
                    .then_inc(sem(f"pin_in{i}"), 16)
            stream(FIRST["merge"], RING, whole(w_merge))
            sp.wait_ge(*nth("chunk_terms", 8))
            sp.dma_start(g2, rwkv_g2).then_inc(sem("g2_in"), 16)
            sp.wait_ge(*nth("chunk_terms_read", 8))
            sp.dma_start(oA2[:, :, :].rearrange("p a b -> p (a b)"), oA_dram.ap()).then_inc(sem("oA_in"), 16)
            sp.wait_ge(*nth("fill_late", 16 * LATE))
            sp.dma_start(gates[:, :, :].rearrange("p a b -> p (a b)"), fill_dram.ap()[:, 14 * S:])\
                .then_inc(sem("gates_in"), 16)
            sp.wait_ge(*nth("x_out", 16))
            sp.wait_ge(*nth("gn_gate", 4))
            sp.dma_start(xT[:, :, :].rearrange("p a b -> p (a b)"), x_dram.ap()).then_inc(sem("x_back"), 16)
            stream(FIRST["merge"] + RING, KD - RING, lambda c: whole(w_merge)(c + RING))
            stream(FIRST["w_out_2"], KD, whole(w_out_2))
            stream(FIRST["conv_up"], 2 * KF, whole(w_conv_up))
            stream_down(FIRST["conv_down"], w_conv_down)
            for n in range(NT):
                sp.wait_ge(*nth("out_copied", 2 * (n + 1)))
                sp.dma_start(out[0, n * P:(n + 1) * P, :],
                             yT[:, 2 * n:2 * n + 2, :].rearrange("p a b -> p (a b)")).then_inc(sem("out_done"), 16)
            sp.wait_ge(*nth("out_done", 16 * NT))

        @block.gpsimd
        def _(pool):
            def split(c, turn, s, width=CHUNK, first=False):
                pool.wait_ge(*nth(f"w_in{s}", (turn + 1) * 16))
                if not first:
                    pool.wait_ge(*nth("w_used", c - RING + 1))
                raw = w_raw[:, s, 0:width]
                nc.gpsimd.tensor_tensor(w_hi[:, s, 0:width], raw, one[:, 0:1].to_broadcast([P, width]), ALU.mult).then_inc(sem("w_rounded"), 1)
                pool.wait_ge(*nth("w_rounded", c + 1))
                nc.gpsimd.tensor_tensor(w_lo[:, s, 0:width], raw, w_hi[:, s, 0:width].bitcast(F32),
                                        ALU.subtract).then_inc(sem("w_split"), 1)

            def stream(c0, n, first=False):
                if first:
                    for u in range(RING):
                        split(u, 0, u, first=True)
                with pool.Fori(1 if first else 0, n // RING) as i:
                    for u in range(RING):
                        v = c0 + u
                        split(i * RING + v, i + v // RING, v % RING)
                for u in range(n - n % RING, n):
                    v = c0 + u
                    split(v, v // RING, v % RING)

            def stream_down(c0):
                with pool.Fori(0, KD // RING) as i:
                    for u in range(3 * RING):
                        a, b = DOWN_SPLIT[u % 3]
                        v = c0 + u
                        split(i * (3 * RING) + v, i * 3 + v // RING, v % RING, (b - a) * P)

            nc.gpsimd.memset(one[:, :], 1.0).then_inc(sem("one_set"), 1)
            pool.wait_ge(*nth("one_set", 1))
            stream(FIRST["ffn1_up"], 2 * KF, first=True)
            stream_down(FIRST["ffn1_down"])
            stream(FIRST["w_in"], 10)
            stream(FIRST["w_out"], KD)
            stream(FIRST["ffn2_up"], 2 * KF)
            stream_down(FIRST["ffn2_down"])
            stream(FIRST["nsa"], 11)
            stream(FIRST["rwkv"], 14)
            stream(FIRST["gates"], 2 * KD)
            stream(FIRST["merge"], RING)
            for m in range(4):
                for k in range(1, 6):
                    for half in range(2):
                        if k == 1:
                            pool.wait_ge(*nth("d_ready", 10 * m + half + 1))
                        else:
                            pool.wait_ge(*nth("level_x", 10 * m + 2 * (k - 2) + half + 1))
                        nc.gpsimd.tensor_tensor(OT[:, half, :, :], mats[:, half, :, 0:P],
                                                level[k].unsqueeze(1).to_broadcast([P, 4, P]), ALU.mult)\
                            .then_inc(sem("level_mask"), 1)
            pool.wait_ge(*nth("oA_in", 16))
            for m in range(4):
                nc.gpsimd.tensor_tensor(o_hi[:, m, :], oA2[:, m, :], one[:, 0:1].to_broadcast([P, S]), ALU.mult)\
                    .then_inc(sem("oA_rounded"), 1)
                pool.wait_ge(*nth("oA_rounded", m + 1))
                nc.gpsimd.tensor_tensor(o_lo[:, m, :], oA2[:, m, :], o_hi[:, m, :].bitcast(F32), ALU.subtract)\
                    .then_inc(sem("o_ready"), 1)
            for m in range(4):
                pool.wait_ge(*nth("gn_out", m + 1))
                nc.gpsimd.tensor_tensor(o_lo[:, 4 + m, :], yl[:, m, :], o_hi[:, 4 + m, :].bitcast(F32), ALU.subtract)\
                    .then_inc(sem("o_ready"), 1)
            stream(FIRST["merge"] + RING, KD - RING)
            stream(FIRST["w_out_2"], KD)
            stream(FIRST["conv_up"], 2 * KF)
            stream_down(FIRST["conv_down"])

        @block.tensor
        def _(pe):
            def chunk(c, s, k0, k1, rhs_hi, rhs_lo, dst, start, stop, each=None, w0=None, also=None,
                      shift=0):
                w0 = k0 if w0 is None else w0
                pe.wait_ge(*nth("w_split", c + 1))
                for k in range(k0, k1):
                    if each:
                        pe.wait_ge(*nth(each, k + 1 + shift))
                    hi = w_hi[:, s, (k - w0) * P:(k - w0 + 1) * P]
                    lo = w_lo[:, s, (k - w0) * P:(k - w0 + 1) * P]
                    nc.tensor.matmul(dst, hi, rhs_hi[:, k, :], start=start and k == k0, stop=False)
                    nc.tensor.matmul(dst, hi, rhs_lo[:, k, :], start=False, stop=False)
                    last = nc.tensor.matmul(dst, lo, rhs_hi[:, k, :], start=False, stop=stop and k == k1 - 1)
                    if also:
                        also(k)
                return last

            def ffn_up(tag, c0):
                squares = lambda k: sum_square(k, KD, tag + "_in_sq", tag + "_in_sq_used", 4)
                def body(i, first):
                    for u in range(2):
                        if not first:
                            pe.wait_ge(*nth(tag + "_pair_read", 2 * i + u - 1))
                        for v in range(2):
                            c = 4 * i + (c0 + 2 * u + v)
                            begin = first and u == v == 0
                            last = chunk(c, (c0 + 2 * u + v) % RING, 0, KD, h_hi, h_lo, bank[2 * u + v][:, :],
                                         True, True, tag + "_h_ready" if begin else None,
                                         also=squares if begin else None)
                            last.then_inc(sem("w_used"), 1)
                body(0, True)
                with pe.Fori(1, KF // 2) as i:
                    body(i, False)

            def ffn_down(tag, c0, read):
                def body(i, first):
                    for u in range(4):
                        if not first:
                            pe.wait_ge(*nth(read, 4 * i + u - 3))
                        for j, (a, b) in enumerate(DOWN_SPLIT):
                            v = 3 * u + j
                            if first and u == 0:
                                pe.wait_ge(*nth(tag + "_a_ready", b))
                            last = chunk(12 * i + (c0 + v), (c0 + v) % RING, a, b, a_hi, a_lo, bank[4 + u][:, :],
                                         j == 0, j == 2)
                            last.then_inc(sem("w_used"), 1)
                body(0, True)
                body(1, False)

            def sum_squares(tag, n, ready, used, b=0):
                for k in range(n):
                    sum_square(k, n, ready, used, b)

            def sum_square(k, n, ready, used, b):
                pe.wait_ge(*nth(ready, k + 1))
                nc.tensor.matmul(bank[b][:, :], ones, sq[:, k % 2, :], start=(k == 0),
                                 stop=(k == n - 1)).then_inc(sem(used), 1)

            def project(tag, c0, n, read, h_ready=True, hi=h_hi, lo=h_lo):
                def tile(c, u, first, wait=None):
                    if wait is not None:
                        pe.wait_ge(*nth(read, wait))
                    chunk(c, (c0 + u) % RING, 0, KD, hi, lo, bank[4 + u % 4][:, :], True, True,
                          tag + "_h_ready" if first else None).then_inc(sem("w_used"), 1)
                for u in range(4):
                    tile(c0 + u, u, u == 0 and h_ready)
                with pe.Fori(1, n // 4) as i:
                    for u in range(4):
                        tile(i * 4 + (c0 + u), u, False, wait=i * 4 + (u - 3))
                for m in range(n - n % 4, n):
                    tile(c0 + m, m % 4, False, wait=m - 3)

            def attend_window(n, g, unit):
                keys = slice(max(0, n - 1) * P, (n + 1) * P)
                width = keys.stop - keys.start
                if unit >= 2:
                    pe.wait_ge(*nth("swa_masked", 4 * (unit - 1)))
                for h in range(4):
                    e, i = h % 2, h // 2
                    last = nc.tensor.matmul(bank[2 * (unit % 2) + e][:, i * width:(i + 1) * width],
                                            q_rot[64 * e:64 * e + 64, 2 * g + i, n * P:(n + 1) * P],
                                            k_rot[64 * e:64 * e + 64, g, keys], start=(i == 0), stop=(i == 1),
                                            skip_group_check=True)
                    if i == 1:
                        last.then_inc(sem("swa_scores"), 1)

            def weigh_window(n, g, unit):
                tiles = [j for j in (n - 1, n) if j >= 0]
                pe.wait_ge(*nth("swa_probs", 4 * (unit + 1)))
                if unit:
                    pe.wait_ge(*nth("swa_turned_read", unit))
                for b, j in enumerate(tiles):
                    for h in range(4):
                        last = nc.tensor.transpose(bank[4 + b][:, h * P:(h + 1) * P],
                                                   sc[:, unit % 2, h, b * P:(b + 1) * P], ident)
                last.then_inc(sem("swa_turned"), 1)
                pe.wait_ge(*nth("swa_turned_read", unit + 1))
                if unit:
                    pe.wait_ge(*nth("swa_out_read", unit))
                for h in range(4):
                    e, i = h % 2, h // 2
                    for b, j in enumerate(tiles):
                        last = nc.tensor.matmul(bank[6][64 * e:64 * e + 64, i * P:(i + 1) * P],
                                                v_tok[:, j, 64 * g:64 * g + 64], pT[:, b, h, :],
                                                start=(b == 0), stop=(b == len(tiles) - 1), skip_group_check=True)
                last.then_inc(sem("swa_out"), 1)

            pe.wait_ge(*nth("const_in", 16))
            for n in range(NT):
                pe.wait_ge(*nth(f"x_in{n}", 16))
                for k in range(KD):
                    last = nc.tensor.transpose(bank[k][:, n * P:(n + 1) * P], x_tok[:, n, k * P:(k + 1) * P], ident)
                    if n == NT - 1:
                        last.then_inc(sem("x_turned"), 1)
            pe.wait_ge(*nth("start_x_ready", 5))
            ffn_up("ffn1", FIRST["ffn1_up"])
            ffn_down("ffn1", FIRST["ffn1_down"], "ffn1_y_read")
            pe.wait_ge(*nth("ffn1_acc", KD))
            nc.tensor.matmul(bank[0][:, :], ones, acc[:, :], start=True, stop=True).then_inc(sem("ffn1_post_sum"), 1)

            def mix_in(j):
                if j >= 4:
                    pe.wait_ge(*nth("z_read", j - 3 if j < 6 else j))
                c = FIRST["w_in"] + j
                chunk(c, c % RING, 0, KD, h_hi, h_lo, bank[4 + j % 4 if j < 6 else 7][:, :], True, True,
                      "mix_h_ready" if j == 0 else None,
                      also=(lambda k: sum_square(k, KD, "mix_in_sq", "mix_in_sq_used", 0)) if j == 0 else None)\
                    .then_inc(sem("w_used"), 1)

            def rotate_q(i):
                pe.wait_ge(*nth("z_read", 3 + i))
                pe.wait_ge(*nth("rot_used", 1 + i // 2 if i < 2 else 1 + i))
                nc.tensor.matmul(bank[i % 2 if i < 2 else i][:, :], rot_of, z[:, 2 + i, :], start=True, stop=True)\
                    .then_inc(sem("rot_done"), 1)

            mix_in(0)
            mix_in(1)
            pe.wait_ge(*nth("mix_const_in", 16))
            pe.wait_ge(*nth("z_read", 1))
            for g in range(2):
                nc.tensor.matmul(bank[2 * g][:, :], dup_of[g], z[:, 0, :], start=True, stop=True)
                nc.tensor.matmul(bank[2 * g + 1][:, :], dup_rot_of[g], z[:, 0, :], start=True, stop=True)\
                    .then_inc(sem("rot_done"), 1)
            mix_in(2)
            mix_in(3)
            rotate_q(0)
            mix_in(4)
            rotate_q(1)
            mix_in(5)
            rotate_q(2)
            pe.wait_ge(*nth("v_scaled", 1))
            for n in range(NT):
                last = nc.tensor.transpose(bank[6][:, n * P:(n + 1) * P], z[:, 1, n * P:(n + 1) * P], ident)
            last.then_inc(sem("v_turned"), 1)
            rotate_q(3)
            pe.wait_ge(*nth("w_pool_in", 16))
            pe.wait_ge(*nth("rot_used", 6))
            pe.wait_ge(*nth("v_read", 1))
            units = [(n, g) for n in range(NT) for g in range(2)]
            attend_window(*units[0], 0)
            for u, (n, g) in enumerate(units):
                if u + 1 < len(units):
                    attend_window(*units[u + 1], u + 1)
                if u < 4:
                    mix_in(6 + u)
                else:
                    pe.wait_ge(*nth("z_read", 10))
                    pe.wait_ge(*nth("pool_diff", u - 3))
                    if u > 4:
                        pe.wait_ge(*nth("pooled", u - 4))
                    nc.tensor.matmul(bank[7][:, :], wp[:, u - 4, :], dif_of[u % 2], start=True, stop=True)\
                        .then_inc(sem("pool_product"), 1)
                weigh_window(n, g, u)
            pe.wait_ge(*nth("swa_masked", 4 * len(units)))
            sum_squares("pool", 4, "pool_in_sq", "pool_in_sq_used")
            pe.wait_ge(*nth("swa_out_read", len(units)))
            pe.wait_ge(*nth("pooled", 4))

            def out_half(u, k0, begin=False):
                c = FIRST["w_out"] + u
                return chunk(c, c % RING, k0, k0 + 4, h_hi, h_lo, bank[k0 + u % 4][:, :], True, True,
                             "wout_h_ready" if begin else None, w0=0, shift=-4 if k0 else 4)
            for u in range(4):
                out_half(u, 4, u == 0)
            for u in range(4):
                if u == 2:
                    sum_squares("attn", 4, "attn_in_sq", "attn_in_sq_used", 3)
                if u == 3:
                    pe.wait_ge(*nth("attn_in_ln", 1))
                out_half(u, 0, u == 0).then_inc(sem("w_used"), 1)
            for u in range(4, KD):
                pe.wait_ge(*nth("wout_y_read", u - 3))
                out_half(u, 4)
                out_half(u, 0).then_inc(sem("w_used"), 1)
            pe.wait_ge(*nth("wout_acc", KD))
            nc.tensor.matmul(bank[0][:, :], ones, acc[:, :], start=True, stop=True).then_inc(sem("wout_post_sum"), 1)

            ffn_up("ffn2", FIRST["ffn2_up"])
            ffn_down("ffn2", FIRST["ffn2_down"], "ffn2_y_read")
            pe.wait_ge(*nth("ffn2_acc", KD))
            nc.tensor.matmul(bank[0][:, :], ones, acc[:, :], start=True, stop=True).then_inc(sem("ffn2_post_sum"), 1)

            sum_squares("nsa", KD, "nsa_in_sq", "nsa_in_sq_used")
            project("nsa", FIRST["nsa"], 11, "zn_read")
            pe.wait_ge(*nth("nsa_small_in", 8 * 16))
            job = [0]

            def job_bank():
                if job[0] >= 2:
                    pe.wait_ge(*nth("nsa_read", job[0] - 1))
                job[0] += 1
                return bank[2 + (job[0] - 1) % 2]

            filled = [0]

            def fill(n=1):
                for f in range(filled[0], filled[0] + n):
                    if f == NFILL - 1:
                        pe.wait_ge(*nth("fill_read", NFILL - LATE + 1))
                    elif 4 <= f <= NFILL - LATE:
                        pe.wait_ge(*nth("fill_read", f - 3 if f < 14 else f))
                    chunk(FIRST["rwkv"] + f, (FIRST["rwkv"] + f) % RING, 0, KD, h_hi, h_lo,
                          bank[fill_bank(f)][:, :], True, True).then_inc(sem("w_used"), 1)
                filled[0] += n

            pe.wait_ge(*nth("zn_read", 11))
            for v in range(2):
                b = job_bank()
                for n in range(NT):
                    last = nc.tensor.transpose(b[:, n * P:(n + 1) * P], zn[:, 2 + v, n * P:(n + 1) * P], ident)
                last.then_inc(sem("nsa_job"), 1)
            fill()
            for v in range(2):
                for g in range(2):
                    nc.tensor.matmul(job_bank()[:, :], dup2[g], zn[:, 4 + v, :], start=True, stop=True)\
                        .then_inc(sem("nsa_job"), 1)
            fill()
            pe.wait_ge(*nth("rel_one", 1))
            for a, b in ((0, S), (S, 5 * P)):
                nc.tensor.matmul(job_bank()[0:NH, 0:b - a], rel[:, :], code[:, a:b], start=True, stop=True)\
                    .then_inc(sem("nsa_job"), 1)
            pe.wait_ge(*nth("gates", 1))
            b = job_bank()
            for n in range(NT):
                last = nc.tensor.transpose(b[:, n * 24:(n + 1) * 24], oA[0:24, 0, n * P:(n + 1) * P],
                                           ident[0:24, 0:24])
            last.then_inc(sem("nsa_job"), 1)
            for i in range(6):
                pe.wait_ge(*nth("head_sq", i + 1))
                nc.tensor.matmul(bank[i % 2][:, :], head_ones, sq[:, i % 2, :], start=True, stop=True)\
                    .then_inc(sem("head_sum"), 1)
                fill()
            for v in range(2):
                pe.wait_ge(*nth("head_rstd_used", v + 1))
                for g in range(2):
                    nc.tensor.matmul(job_bank()[:, :], dup2[g], zn[:, v, :], start=True, stop=True)\
                        .then_inc(sem("nsa_job"), 1)
                fill()
            for v in range(2):
                pe.wait_ge(*nth("cw1_in", 16 * (v + 1)))
                pe.wait_ge(*nth("blocks_ready", 2 * v + 2))
                b = job_bank()
                for h in range(2):
                    for j in range(16):
                        last = nc.tensor.matmul(b[:, h * 64:h * 64 + 2 * NCMP], cw1[:, j, h * P:(h + 1) * P],
                                                cmp_blocks[v][:, j, :, :], start=(j == 0), stop=(j == 15),
                                                skip_group_check=True)
                last.then_inc(sem("nsa_job"), 1)
                fill()
                pe.wait_ge(*nth("gelu", v + 1))
                b = job_bank()
                if v == 0:
                    for h in range(2):
                        last = nc.tensor.matmul(b[:, 0:2 * NCMP], cw2[:, 0, h, :], hid[:, h, 0:2 * NCMP],
                                                start=(h == 0), stop=(h == 1))
                    last.then_inc(sem("nsa_job"), 1)
                    fill()
                    pe.wait_ge(*nth("head_sq", 7))
                    nc.tensor.matmul(bank[0][:, 0:2 * NCMP], head_ones, sq[:, 0, 0:2 * NCMP], start=True, stop=True)\
                        .then_inc(sem("head_sum"), 1)
                else:
                    for g in range(2):
                        for h in range(2):
                            last = nc.tensor.matmul(b[0:NCMP, g * HD:(g + 1) * HD], hid[:, h, g * NCMP:(g + 1) * NCMP],
                                                    cw2[:, 1, h, 0:HD], start=(h == 0), stop=(h == 1),
                                                    skip_group_check=True)
                    last.then_inc(sem("nsa_job"), 1)
            fill()
            pe.wait_ge(*nth("nsa_read", 17))
            pe.wait_ge(*nth("kc_normed", 1))

            def nsa_scores(n, g, unit):
                for i in range(10):
                    b = bank[i % 4] if unit % 2 == 0 else bank[(i + 2) % 4]
                    if 10 * unit + i >= 4:
                        pe.wait_ge(*nth("nsa_masked", 10 * unit + i - 3))
                    if i < 8:
                        h, e = i % 4, i % 2
                        last = nc.tensor.matmul(b[:, 0:(n + 1) * P],
                                                qn[64 * e:64 * e + 64, 2 * g + h // 2, n * P:(n + 1) * P],
                                                kd[64 * e:64 * e + 64, 2 * (i // 4) + g, 0:(n + 1) * P],
                                                start=True, stop=True)
                    else:
                        e = i - 8
                        for h in range(2):
                            last = nc.tensor.matmul(b[:, h * 32:h * 32 + 8 * n + 7],
                                                    qn[64 * e:64 * e + 64, 2 * g + h, n * P:(n + 1) * P],
                                                    kcn[64 * e:64 * e + 64, g * NCMP:g * NCMP + 8 * n + 7],
                                                    start=(h == 0), stop=(h == 1), skip_group_check=True)
                    last.then_inc(sem("nsa_scores"), 1)

            turn = [0]

            def nsa_weigh(n, g, unit):
                c0 = 2 * P * (unit % 2)
                dst = bank[6][:, c0:c0 + 2 * P]
                if unit >= 2:
                    pe.wait_ge(*nth("nsa_out_read", unit - 1))
                items = [(v, j) for v in range(2) for j in range(n + 1)] + [(2, 0)]
                pe.wait_ge(*nth("nsa_weighed", unit + 1))

                def turn_item(x):
                    v, j = items[x]
                    k = turn[0] + x
                    if k >= 2:
                        pe.wait_ge(*nth("p2T_ready", k - 1))
                    for h in range(4):
                        src = Ec[:, unit % 2, h, 0:8 * n + 7] if v == 2 else E[:, unit % 2, 4 * v + h, j * P:(j + 1) * P]
                        rows = 8 * n + 7 if v == 2 else P
                        last = nc.tensor.transpose(bank[4 + k % 2][0:rows, h * P:(h + 1) * P], src, flip)
                    last.then_inc(sem("nsa_turned"), 1)

                def sum_item(x):
                    v, j = items[x]
                    k = turn[0] + x
                    pe.wait_ge(*nth("p2T_ready", k + 1))
                    for h in range(4):
                        e, i = h % 2, h // 2
                        if v == 2:
                            lhs, rhs = vct[0:8 * n + 7, g, :], p2T[0:8 * n + 7, k % 2, h, :]
                        else:
                            lhs, rhs = v2_tok[:, v, j, 64 * g:64 * g + 64], p2T[:, k % 2, h, :]
                        last = nc.tensor.matmul(dst[64 * e:64 * e + 64, i * P:(i + 1) * P], lhs, rhs,
                                                start=(x == 0 and i == 0), stop=(v == 2), skip_group_check=True)
                    last.then_inc(sem("p2T_used"), 1)
                    return last

                turn_item(0)
                for x in range(len(items)):
                    if x + 1 < len(items):
                        turn_item(x + 1)
                    last = sum_item(x)
                turn[0] += len(items)

            units = [(n, g) for n in range(NT) for g in range(2)]
            nsa_scores(*units[0], 0)
            fill()
            for u, (n, g) in enumerate(units):
                if u + 1 < len(units):
                    nsa_scores(*units[u + 1], u + 1)
                fill()
                nsa_weigh(n, g, u)

            def rw_prepare(m, step):
                cols = slice(m * P, (m + 1) * P)
                if step == 1:
                    pe.wait_ge(*nth("lora_in", 1))
                    if m:
                        pe.wait_ge(*nth("level_start", 2 * m))
                    nc.tensor.matmul(bank[3][:, :], w2a2[0:64, cols], pin[0:64, 12, :], start=True, stop=True)
                    nc.tensor.matmul(bank[7][:, :], w2a2[64:128, cols], pin[64:128, 12, :], start=True, stop=True)\
                        .then_inc(sem("lora"), 1)
                elif step == 3:
                    pe.wait_ge(*nth("lora_read", m + 1))
                    pe.wait_ge(*nth("rw_square", m + 1))
                    nc.tensor.matmul(bank[3][:, :], head_ones2, sq[:, 0, :], start=True, stop=True)\
                        .then_inc(sem("rw_head_sum"), 1)
                    pe.wait_ge(*nth("rk_product", m + 1))
                    nc.tensor.matmul(bank[7][:, :], head_ones2, sq[:, 1, :], start=True, stop=True)\
                        .then_inc(sem("rw_head_sum"), 1)

            pe.wait_ge(*nth("rwkv_small_in", 4 * 16))
            for step in range(1, 6):
                fill(2 if step < 3 else 1)
                rw_prepare(0, step)
            rounds = [[(2 * half + i, e) for i in range(2) for e in range(2)] for half in range(2)]

            def rw_scores(m, half):
                Bh, Kh, AR = pair_sets[m % 2][:3]
                for u, (n, e) in enumerate(rounds[half]):
                    b = bank[u if half else 4 + u]
                    rows = slice(64 * e, 64 * e + 64)
                    rhs = AR[rows, n, :, :].rearrange("p a t -> p (a t)")
                    nc.tensor.matmul(b[:, 0:2 * P], Bh[rows, n * P:(n + 1) * P], rhs, start=True, stop=True,
                                     skip_group_check=True)
                    nc.tensor.matmul(b[:, 2 * P:], Kh[rows, n * P:(n + 1) * P], rhs, start=True, stop=True,
                                     skip_group_check=True).then_inc(sem("rw_scores"), 1)

            def rw_turn(m, part):
                Bh, Kh, AR = pair_sets[m % 2][:3]
                if part == 0:
                    pe.wait_ge(*nth("hats", 4 * (m + 1)))
                    pe.wait_ge(*nth("bonus_done", m + 1))
                srcs = (AR[:, :, 0, :], by_tile(Bh[:, :]), by_tile(Kh[:, :]), by_tile(pin[:, 8 + m, :]))
                for i in range(2 * part, 2 * part + 2):
                    if part:
                        pe.wait_ge(*nth("rw_tok", 4 * m + i - 1))
                    for n in range(NT):
                        last = nc.tensor.transpose(bank[3 + 4 * (i % 2)][:, n * P:(n + 1) * P], srcs[i][:, n, :],
                                                   ident)
                    last.then_inc(sem("rw_turned"), 1)

            rw_turn(0, 0)
            for m in range(4):
                At, Bt, Kt, Vt = pair_sets[m % 2][3:]
                if m:
                    pe.wait_ge(*nth("chunk_terms_read", 2 * m - 1))
                else:
                    rw_turn(0, 1)
                pe.wait_ge(*nth("rw_tok", 4 * (m + 1)))
                rw_scores(m, 0)
                if m:
                    pe.wait_ge(*nth("chunk_terms_read", 2 * m))
                rw_scores(m, 1)
                for half in range(2):
                    if m < 3 and half == 1:
                        rw_prepare(m + 1, 1)
                    pe.wait_ge(*nth("level_start", 2 * m + half + 1))
                    for u in range(4):
                        last = nc.tensor.transpose(bank[0 if half else 4][:, u * P:(u + 1) * P], OT[:, half, u, :],
                                                   ident)
                    last.then_inc(sem("level_turned"), 1)
                for k in range(1, 6):
                    done = 10 * m + 2 * (k - 1)
                    for half in range(2):
                        pe.wait_ge(*nth("level_mask", done + half + 1))
                        pe.wait_ge(*nth("d_ready", done + half + 1))
                        for u in range(4):
                            last = nc.tensor.matmul(bank[0 if half else 4][:, u * P:(u + 1) * P], OT[:, half, u, :],
                                                    Dm[:, half, u, :], start=True, stop=True, skip_group_check=True)
                        last.then_inc(sem("level_x"), 1)
                    for half in range(2):
                        pe.wait_ge(*nth("level_x_read", done + half + 1))
                        pe.wait_ge(*nth("dt_ready", 12 * m + 2 * (k - 1) + half + 1))
                        if k < 5:
                            for u in range(4):
                                last = nc.tensor.matmul(bank[1 if half else 5][:, u * P:(u + 1) * P],
                                                        DT[:, half, u, :], X[:, half, u, :],
                                                        start=True, stop=True, skip_group_check=True)
                            last.then_inc(sem("level_d"), 1)
                    for half in range(2):
                        for u in range(4):
                            last = nc.tensor.matmul(bank[2 if half else 6][:, u * P:(u + 1) * P], X[:, half, u, :],
                                                    DT[:, half, u, :], start=True, stop=True, skip_group_check=True)
                        last.then_inc(sem("level_dt"), 1)
                    if m < 3:
                        rw_prepare(m + 1, k + 1)
                for half in range(2):
                    for u, (n, e) in enumerate(rounds[half]):
                        last = nc.tensor.matmul(bank[0 if half else 4][:, u * HD:(u + 1) * HD],
                                                mats[:, half, u, 2 * P:3 * P], Vt[:, n, 64 * e:64 * e + 64],
                                                start=True, stop=True, skip_group_check=True)
                    last.then_inc(sem("akv"), 1)
                for half in range(2):
                    pe.wait_ge(*nth("akv_read", 2 * m + half + 1))
                    pe.wait_ge(*nth("dt_ready", 12 * m + 10 + half + 1))
                    for u, (n, e) in enumerate(rounds[half]):
                        b = bank[1 if half else 5]
                        nc.tensor.matmul(b[:, u * P:u * P + HD], DT[:, half, u, :], AkV[:, half, u, :],
                                         start=True, stop=True, skip_group_check=True)
                        last = nc.tensor.matmul(b[:, u * P + HD:(u + 1) * P], DT[:, half, u, :],
                                                At[:, n, 64 * e:64 * e + 64], start=True, stop=True,
                                                skip_group_check=True)
                    last.then_inc(sem("ug"), 1)
                if m < 3:
                    rw_turn(m + 1, 0)
                for half in range(2):
                    if m < 3 and half == 1:
                        rw_turn(m + 1, 1)
                    pe.wait_ge(*nth("ug_read", 2 * m + half + 1))
                    qy = bank[2 if half else 6]
                    for u, (n, e) in enumerate(rounds[half]):
                        rows, at = slice(64 * e, 64 * e + 64), slice((u // 2) * P, (u // 2 + 1) * P)
                        y_at = slice(2 * P + at.start, 2 * P + at.stop)
                        U, G = UG[:, half, u, 0:HD], UG[:, half, u, HD:]
                        V = Vt[:, n, 64 * e:64 * e + 64]
                        nc.tensor.matmul(qy[rows, at], G, mats[:, half, u, P:2 * P], start=True, stop=True,
                                         skip_group_check=True)
                        nc.tensor.matmul(qy[rows, y_at], U, mats[:, half, u, P:2 * P], start=True, stop=False,
                                         skip_group_check=True)
                        nc.tensor.matmul(qy[rows, y_at], V, mats[:, half, u, 3 * P:], start=False, stop=True,
                                         skip_group_check=True)
                        at = slice((u // 2) * HD, (u // 2 + 1) * HD)
                        n_at = slice(P + at.start, P + at.stop)
                        for c in range(2):
                            mn = bank[c if half else 4 + c]
                            tok = slice(64 * c, 64 * c + 64)
                            B, K, V = (x[tok, n, 64 * e:64 * e + 64] for x in (Bt, Kt, Vt))
                            nc.tensor.matmul(mn[rows, at], UG[tok, half, u, HD:], B, start=True, stop=True,
                                             skip_group_check=True)
                            nc.tensor.matmul(mn[rows, n_at], B, UG[tok, half, u, 0:HD], start=True, stop=False,
                                             skip_group_check=True)
                            last = nc.tensor.matmul(mn[rows, n_at], K, V, start=False, stop=True,
                                                    skip_group_check=True)
                    last.then_inc(sem("chunk_terms"), 1)
            pe.wait_ge(*nth("chunk_terms_read", 8))
            for c in range(1, NCH):
                pe.wait_ge(*nth("state", 2 * c))
                if c > 1:
                    pe.wait_ge(*nth("walk_read", 2 * (c - 1)))
                at = slice(c * C, (c + 1) * C)
                for e in range(2):
                    rows = slice(64 * e, 64 * e + 64)
                    if c < NCH - 1:
                        for m in range(4):
                            last = nc.tensor.matmul(bank[2 + e][rows, m * HD:(m + 1) * HD], pin[rows, 4 + m, at],
                                                    state[rows, c % 2, m, :], start=True, stop=True,
                                                    skip_group_check=True)
                        last.then_inc(sem("state_product"), 1)
                for e in range(2):
                    rows = slice(64 * e, 64 * e + 64)
                    for m in range(4):
                        last = nc.tensor.matmul(bank[e][rows, m * HD:(m + 1) * HD], state[rows, c % 2, m, :],
                                                pin[rows, m, at], start=True, stop=True, skip_group_check=True)
                    last.then_inc(sem("walk_y"), 1)
            pe.wait_ge(*nth("walk_read", 2 * (NCH - 1)))
            for m in range(4):
                nc.tensor.matmul(bank[m][:, :], head_ones2, yl[:, m, :], start=True, stop=True)\
                    .then_inc(sem("gn_sum"), 1)
            pe.wait_ge(*nth("g2_in", 16))
            for m in range(4):
                nc.tensor.matmul(bank[4 + m][:, :], g2[:, m * P:(m + 1) * P], pin[:, 13, :], start=True, stop=True)\
                    .then_inc(sem("gn_gate"), 1)
            for m in range(4):
                pe.wait_ge(*nth("gn_sq", m + 1))
                nc.tensor.matmul(bank[m][:, :], head_ones2, gn_work[m], start=True, stop=True)\
                    .then_inc(sem("gn_var"), 1)

            def project_a(m):
                c = FIRST["merge"] + m
                chunk(c, c % RING, 0, 4, o_hi, o_lo, bank[2 * (m % 4)][:, :], True, True)

            def project_b(m):
                c = FIRST["merge"] + m
                chunk(c, c % RING, 4, 8, o_hi, o_lo, bank[2 * (m % 4) + 1][:, :], True, True,
                      "o_ready" if m == 0 else None, w0=0).then_inc(sem("w_used"), 1)

            pe.wait_ge(*nth("o_ready", 4))
            for m in range(2):
                pe.wait_ge(*nth("gn_ln", 2 * m + 1))
                project_a(m)
            pe.wait_ge(*nth("gn_ln", 4))
            for m in range(2):
                project_b(m)
            pe.wait_ge(*nth("gn_out", 4))
            for m in range(2, KD):
                if m >= 4:
                    pe.wait_ge(*nth("m_ready", m - 3))
                project_a(m)
                project_b(m)
            pe.wait_ge(*nth("m_ready", KD))
            project("w_out_2", FIRST["w_out_2"], KD, "conv_x_ready", h_ready=False, hi=m_hi, lo=m_lo)

            pe.wait_ge(*nth("conv_x_ready", 5))
            ffn_up("conv", FIRST["conv_up"])
            ffn_down("conv", FIRST["conv_down"], "end_x_ready")
            pe.wait_ge(*nth("end_x_ready", KD))
            for n in range(NT):
                for h in range(2):
                    for k in range(4):
                        last = nc.tensor.transpose(bank[2 * n + h][:, k * P:(k + 1) * P],
                                                   xT[:, 4 * h + k, n * P:(n + 1) * P], ident)
                    last.then_inc(sem("out_turned"), 1)

        @block.scalar
        def _(act):
            def logs():
                nc.scalar.preload_act_table_set("natural_log_exp_and_others")

            def round_h(tag, k0, n):
                for k in range(n):
                    act.wait_ge(*nth(tag + "_h32", k + 1))
                    nc.scalar.activation(h_hi[:, k0 + k, :], tmp[:, k % 2, :], ACT.Copy).then_inc(sem(tag + "_h_hi"), 1)

            def inv_rms(tag, ready, count, n=D, b=0):
                act.wait_ge(*nth(ready, count))
                nc.scalar.activation(rstd[:, :], bank[b][:, :], ACT.Ln, bias=param("eps"), scale=1.0 / n)\
                    .then_inc(sem(tag + "_ln"), 1)
                act.wait_ge(*nth(tag + "_ln", 1))
                nc.scalar.activation(rstd[:, :], rstd[:, :], ACT.Exp, scale=-0.5).then_inc(sem(tag + "_rstd"), 1)

            def pre_norm_sums(tag, x_ready, count, src, k0, n, b):
                for k in range(n):
                    act.wait_ge(*nth(x_ready, k + 1 if count is None else count))
                    if k >= 2:
                        act.wait_ge(*nth(tag + "_in_sq_used", k - 1))
                    nc.scalar.activation(sq[:, k % 2, :], src[:, k0 + k, :], ACT.Square)\
                        .then_inc(sem(tag + "_in_sq"), 1)
                inv_rms(tag + "_in", tag + "_in_sq_used", n, n * P, b)

            def pre_norm(tag, x_ready, count=None, src=xT, k0=0, n=KD, b=0):
                pre_norm_sums(tag, x_ready, count, src, k0, n, b)
                round_h(tag, k0, n)

            def norm_ahead(tag, gain, x_ready, b=4):
                logs()
                for k in range(KD):
                    act.wait_ge(*nth(x_ready, k + 1))
                    nc.scalar.activation(h_hi[:, k, :], xT[:, k, :], ACT.Copy, scale=param(gain, k))\
                        .then_inc(sem(tag + "_h_hi"), 1)
                    if k >= 2:
                        act.wait_ge(*nth(tag + "_in_sq_used", k - 1))
                    nc.scalar.activation(sq[:, k % 2, :], xT[:, k, :], ACT.Square).then_inc(sem(tag + "_in_sq"), 1)
                inv_rms(tag + "_in", tag + "_in_sq_used", KD, b=b)

            def ffn_up(tag):
                nc.scalar.preload_act_table(ACT.Silu)
                with act.Fori(0, KF // 2) as i:
                    for u in range(2):
                        act.wait_ge(*nth(tag + "_gate_scaled", 2 * i + u + 1))
                        nc.scalar.activation(tmp[:, u, :], tmp[:, u, :], ACT.Silu).then_inc(sem(tag + "_silu"), 1)

            def copy_out(tag, c0, per, y):
                logs()
                for m in range(KD):
                    act.wait_ge(*nth("w_used", c0 + per * (m + 1)))
                    if m >= 2:
                        act.wait_ge(*nth(tag + "_acc", m - 1))
                    nc.scalar.activation(sq[:, m % 2, :], bank[4 + m % 4][:, :], ACT.Square).then_inc(sem(tag + "_sq"), 1)
                    nc.scalar.activation(y[:, m, :], bank[4 + m % 4][:, :], ACT.Copy).then_inc(sem(tag + "_y_read"), 1)

            logs()
            act.wait_ge(*nth("params_in", 16))
            norm_ahead("ffn1", "ffn1_pre", "start_x_ready")
            ffn_up("ffn1")
            copy_out("ffn1", FIRST["ffn1_down"], 3, yT)
            inv_rms("ffn1_post", "ffn1_post_sum", 1)

            norm_ahead("mix", "mix_pre", "ffn1_x_ready", b=0)
            nc.scalar.preload_act_table(ACT.Sin)
            act.wait_ge(*nth("angle_step", 10))
            nc.scalar.activation(sin_t[:, :], ang[:, 0, :], ACT.Sin).then_inc(sem("sine"), 1)
            nc.scalar.activation(cos_t[:, :], ang[:, 2, :], ACT.Sin, bias=param("half_pi"), scale=-1.0)\
                .then_inc(sem("sine"), 1)

            logs()

            def copy_in(m):
                act.wait_ge(*nth("w_used", FIRST["w_in"] + m + 1))
                nc.scalar.activation(z[:, m, :], bank[4 + m % 4 if m < 6 else 7][:, :], ACT.Copy)\
                    .then_inc(sem("z_read"), 1)
            for m in range(6):
                copy_in(m)
            act.wait_ge(*nth("v_turned", 1))
            nc.scalar.activation(v_tok[:, :, :].rearrange("p n c -> p (n c)"), bank[6][:, :], ACT.Copy)\
                .then_inc(sem("v_read"), 1)
            units = [(n, g) for n in range(NT) for g in range(2)]

            def exps(n, g, unit):
                width = (2 if n else 1) * P
                act.wait_ge(*nth("swa_masked", 4 * (unit + 1)))
                for h in range(4):
                    s = sc[:, unit % 2, h, 0:width]
                    nc.scalar.activation(s, s, ACT.Exp, bias=small[:, unit % 2, 0, h:h + 1], scale=-1.0,
                                         accum_out=small[:, unit % 2, 1, h:h + 1]).then_inc(sem("swa_exp"), 1)
                act.wait_ge(*nth("swa_sink_arg", unit + 1))
                nc.scalar.activation(small[:, unit % 2, 2, :], small[:, unit % 2, 2, :], ACT.Exp)\
                    .then_inc(sem("swa_sink_exp"), 1)

            def copies(n, g, unit):
                act.wait_ge(*nth("swa_turned", unit + 1))
                if unit:
                    act.wait_ge(*nth("swa_out", unit))
                for b in range(2 if n else 1):
                    last = nc.scalar.activation(pT[:, b, :, :].rearrange("p h t -> p (h t)"), bank[4 + b][:, :],
                                                ACT.Copy)
                last.then_inc(sem("swa_turned_read"), 1)

            def store_out(n, g, unit):
                act.wait_ge(*nth("swa_out", unit + 1))
                nc.scalar.activation(mixed[:, 4 + 2 * g:6 + 2 * g, n * P:(n + 1) * P],
                                     bank[6][:, 0:2 * P].rearrange("p (i t) -> p i t", i=2), ACT.Copy)\
                    .then_inc(sem("swa_out_read"), 1)

            def pool_squares(k0):
                for k in range(k0, k0 + 2):
                    act.wait_ge(*nth("pooled", k + 1))
                    if k >= 2:
                        act.wait_ge(*nth("pool_in_sq_used", k - 1))
                    nc.scalar.activation(sq[:, k % 2, :], mixed[:, k, :], ACT.Square).then_inc(sem("pool_in_sq"), 1)

            exps(*units[0], 0)
            for u, (n, g) in enumerate(units):
                if u < 4:
                    exps(*units[u + 1], u + 1)
                    copy_in(6 + u)
                copies(n, g, u)
                if 4 <= u < len(units) - 1:
                    exps(*units[u + 1], u + 1)
                if u == len(units) - 1:
                    pool_squares(0)
                store_out(n, g, u)
            pool_squares(2)
            act.wait_ge(*nth("swa_out_read", len(units)))
            for k in range(4):
                nc.scalar.activation(h_hi[:, 4 + k, :], mixed[:, 4 + k, :], ACT.Copy, scale=param("g_attn", k))\
                    .then_inc(sem("attn_h_hi"), 1)
            inv_rms("pool_in", "pool_in_sq_used", 4, 4 * P)
            round_h("pool", 0, 4)
            pre_norm_sums("attn", "swa_out_read", len(units), mixed, 4, 4, 3)
            for m in range(KD):
                act.wait_ge(*nth("wout_y_read", m + 1))
                if m >= 2:
                    act.wait_ge(*nth("wout_acc", m - 1))
                nc.scalar.activation(sq[:, m % 2, :], mixed[:, m, :], ACT.Square).then_inc(sem("wout_sq"), 1)
            inv_rms("wout_post", "wout_post_sum", 1)

            norm_ahead("ffn2", "ffn2_pre", "wout_x_ready")
            ffn_up("ffn2")
            copy_out("ffn2", FIRST["ffn2_down"], 3, yT)
            inv_rms("ffn2_post", "ffn2_post_sum", 1)

            pre_norm("nsa", "ffn2_x_ready")
            for m in range(11):
                act.wait_ge(*nth("w_used", FIRST["nsa"] + m + 1))
                nc.scalar.activation(zn[:, m, :], bank[4 + m % 4][:, :], ACT.Copy).then_inc(sem("zn_read"), 1)
            act.wait_ge(*nth("zn_read", 11))
            nc.scalar.activation(reverse(oA[0:24, 0, :]), by_tile(zn[0:24, 10, :]), ACT.Sigmoid)\
                .then_inc(sem("gates"), 1)
            logs()
            filled = [0]

            def fill_out(n=1):
                for f in range(filled[0], filled[0] + n):
                    act.wait_ge(*nth("w_used", FIRST["rwkv"] + f + 1))
                    late = f - NFILL + LATE
                    if f == 0:
                        act.wait_ge(*nth("x_out", 16))
                    elif f >= 8 and f % 4 == 0 and late < 0:
                        act.wait_ge(*nth(f"fill_out{f // 4 % 2}", 64 * (f // 8)))
                    place = stage[:, f % 8, :] if late < 0 else late_stage[:, late, :]
                    nc.scalar.activation(place, bank[fill_bank(f)][:, :], ACT.Copy).then_inc(sem("fill_read"), 1)
                    act.wait_ge(*nth("fill_read", f + 1))
                    act.dma_start(fill_dram.ap()[:, f * S:(f + 1) * S], place)\
                        .then_inc(sem("fill_late" if late >= 0 else f"fill_out{f // 4 % 2}"), 16)
                filled[0] += n

            def head_rms(i, width=S):
                act.wait_ge(*nth("head_sum", i + 1))
                if i >= 2:
                    act.wait_ge(*nth("head_rstd_used", i - 1))
                nc.scalar.activation(tmp[:, i % 2, 0:width], bank[i % 2][:, 0:width], ACT.Ln, bias=param("eps"),
                                     scale=1.0 / HD).then_inc(sem("head_ln"), 1)
                act.wait_ge(*nth("head_ln", i + 1))
                nc.scalar.activation(tmp[:, i % 2, 0:width], tmp[:, i % 2, 0:width], ACT.Exp, scale=-0.5)\
                    .then_inc(sem("head_rstd"), 1)

            for i in range(6):
                nc.scalar.activation(sq[:, i % 2, :], zn[:, i if i < 2 else i + 4, :], ACT.Square)\
                    .then_inc(sem("head_sq"), 1)
                if i:
                    head_rms(i - 1)
                    fill_out()
                if i == 3:
                    act.wait_ge(*nth("nsa_read", 8))
                    act.dma_start(bias_dram.ap(), rv[:, :]).then_inc(sem("bias_out"), 16)
            head_rms(5)
            fill_out(5)
            for v in range(2):
                act.wait_ge(*nth("gelu_arg", v + 1))
                nc.scalar.activation(hid2[:, :, 0:2 * NCMP], hid2[:, :, 0:2 * NCMP], ACT.Tanh, scale=math.sqrt(2.0 / math.pi))\
                    .then_inc(sem("gelu_tanh"), 1)
                if v == 0:
                    act.dma_start(cw1[:, :, :], cmp_w1[1].rearrange("(j p) n -> p j n", p=P))\
                        .then_inc(sem("cw1_in"), 16)
                    fill_out()
                    act.wait_ge(*nth("nsa_read", 15))
                    nc.scalar.activation(sq[:, 0, 0:2 * NCMP], kcn[:, :], ACT.Square).then_inc(sem("head_sq"), 1)
                    head_rms(6, 2 * NCMP)
                    fill_out()
                else:
                    act.wait_ge(*nth("bias_out", 16))
                    act.dma_start(toeplitz[:, :, :], bass.AP(bias_dram, 0, [[1, P], [5 * P, NH], [1, S]]))\
                        .then_inc(sem("toeplitz_in"), 16)
                    fill_out(2)

            logs()

            def nsa_exps(n, g, unit):
                for i in range(10):
                    act.wait_ge(*nth("nsa_masked", 10 * unit + i + 1))
                    if i < 8:
                        s, c = E[:, unit % 2, i, 0:(n + 1) * P], 4 + i
                        nc.scalar.activation(s, s, ACT.Exp, bias=stat[:, unit % 2, 0, c:c + 1], scale=-1.0,
                                             accum_out=stat[:, unit % 2, 1, c:c + 1]).then_inc(sem("nsa_exp"), 1)
                    else:
                        for k in range(2):
                            c = 2 * k + i - 8
                            s = Ec[:, unit % 2, c, 0:8 * n + 7]
                            nc.scalar.activation(s, s, ACT.Exp, bias=stat[:, unit % 2, 0, c:c + 1], scale=-1.0,
                                                 accum_out=stat[:, unit % 2, 1, c:c + 1])\
                                .then_inc(sem("nsa_exp"), 1)

            turn = [0]

            def nsa_copies(n, g, unit):
                items = 2 * (n + 1) + 1
                c0 = 2 * P * (unit % 2)
                for x in range(items):
                    k = turn[0] + x
                    act.wait_ge(*nth("nsa_turned", k + 1))
                    if k >= 2:
                        act.wait_ge(*nth("p2T_used", k - 1))
                    rows = 8 * n + 7 if x == items - 1 else P
                    nc.scalar.activation(p2T[0:rows, k % 2, :, :].rearrange("p h t -> p (h t)"),
                                         bank[4 + k % 2][0:rows, :], ACT.Copy).then_inc(sem("p2T_ready"), 1)
                turn[0] += items
                act.wait_ge(*nth("p2T_used", turn[0]))
                nc.scalar.activation(oA[:, 2 * g:2 * g + 2, n * P:(n + 1) * P],
                                     bank[6][:, c0:c0 + 2 * P].rearrange("p (i t) -> p i t", i=2), ACT.Copy)\
                    .then_inc(sem("nsa_out_read"), 1)
                if g == 1:
                    act.wait_ge(*nth("nsa_out_read", unit + 1))
                    act.dma_start(oA_dram.ap().rearrange("p (a b) -> p a b", a=4)[:, :, n * P:(n + 1) * P],
                                  oA[:, :, n * P:(n + 1) * P]).then_inc(sem("oA_out"), 16)

            nsa_exps(*units[0], 0)
            fill_out()
            for u, (n, g) in enumerate(units):
                if u + 1 < len(units):
                    nsa_exps(*units[u + 1], u + 1)
                fill_out()
                nsa_copies(n, g, u)

            def rw_prepare(m, step):
                if step == 1:
                    act.wait_ge(*nth("lora", m + 1))
                    nc.scalar.activation(SG[:, :], bank[3][:, :], ACT.Sigmoid, bias=param("w0", m))
                    nc.scalar.activation(RATE[:, :], bank[7][:, :], ACT.Sigmoid, bias=param("a0", m))\
                        .then_inc(sem("lora_read"), 1)
                elif step == 2:
                    act.wait_ge(*nth("kk", m + 1))
                    if m:
                        act.wait_ge(*nth("rw_head_sum", 2 * m))
                    nc.scalar.activation(sq[:, 0, :], pair_sets[m % 2][0][:, :], ACT.Square).then_inc(sem("rw_square"), 1)
                elif step == 3:
                    act.wait_ge(*nth("cumulative", m + 1))
                    nc.scalar.activation(UPTO[:, :], CUM[:, :], ACT.Exp, scale=-KAPPA).then_inc(sem("decays"), 1)
                    nc.scalar.activation(PREV[:, :], PREV[:, :], ACT.Exp, scale=-KAPPA).then_inc(sem("decays"), 1)
                    act.wait_ge(*nth("decays", 3 * m + 2))
                    nc.scalar.activation(INV[:, :], CUM[:, :], ACT.Exp, scale=KAPPA).then_inc(sem("decays"), 1)
                elif step == 5:
                    act.wait_ge(*nth("kk_sum", m + 1))
                    nc.scalar.activation(tmp[:, 0, :], tmp[:, 0, :], ACT.Ln, scale=65536.0).then_inc(sem("kk_ln"), 1)
                    act.wait_ge(*nth("kk_ln", m + 1))
                    nc.scalar.activation(tmp[:, 0, :], tmp[:, 0, :], ACT.Exp, bias=param("ln_256"), scale=-0.5)\
                        .then_inc(sem("kk_rstd"), 1)

            act.wait_ge(*nth("mixed_in", 2))
            nc.scalar.activation(pin[:, 13, :], pin[:, 13, :], ACT.Sigmoid)
            nc.scalar.activation(pin[0:64, 12, :], pin[0:64, 12, :], ACT.Tanh).then_inc(sem("lora_in"), 1)
            for step in range(1, 6):
                rw_prepare(0, step)
                fill_out((1, 1, 1, 1, 3)[step - 1])
            flat = lambda x: x.rearrange("p a b -> p (a b)")

            def rw_turned(m, part):
                for i in range(2 * part, 2 * part + 2):
                    act.wait_ge(*nth("rw_turned", 4 * m + i + 1))
                    nc.scalar.activation(flat(pair_sets[m % 2][3 + i][:, :, :]), bank[3 + 4 * (i % 2)][:, :],
                                         ACT.Copy).then_inc(sem("rw_tok"), 1)

            rw_turned(0, 0)
            rw_turned(0, 1)
            for m in range(4):
                if m < 3:
                    rw_prepare(m + 1, 1)
                for k in range(1, 6):
                    for half in range(2):
                        act.wait_ge(*nth("level_x", 10 * m + 2 * (k - 1) + half + 1))
                        nc.scalar.activation(flat(X[:, half, :, :]), bank[0 if half else 4][:, :], ACT.Copy)\
                            .then_inc(sem("level_x_read"), 1)
                    if m < 3:
                        rw_prepare(m + 1, k + 1)
                for half in range(2):
                    act.wait_ge(*nth("akv", 2 * m + half + 1))
                    nc.scalar.activation(flat(AkV[:, half, :, :]), bank[0 if half else 4][:, 0:4 * HD], ACT.Copy)\
                        .then_inc(sem("akv_read"), 1)
                for half in range(2):
                    act.wait_ge(*nth("ug", 2 * m + half + 1))
                    nc.scalar.activation(flat(UG[:, half, :, :]), bank[1 if half else 5][:, :], ACT.Copy)\
                        .then_inc(sem("ug_read"), 1)
                if m < 3:
                    rw_turned(m + 1, 0)
                    rw_turned(m + 1, 1)
            nc.scalar.preload_act_table(ACT.Sigmoid)
            act.wait_ge(*nth("gates_in", 16))
            for i in range(4):
                g = flat(gates[:, 4 * i:4 * i + 4, :])
                nc.scalar.activation(g, g, ACT.Sigmoid).then_inc(sem("merge_gate"), 1)
            logs()
            for m in range(4):
                act.wait_ge(*nth("gn_centred", m + 1))
                nc.scalar.activation(gn_work[m], yl[:, m, :], ACT.Square).then_inc(sem("gn_sq"), 1)
            for m in range(4):
                act.wait_ge(*nth("gn_var", m + 1))
                nc.scalar.activation(gn_work[m], bank[m][:, :], ACT.Ln, bias=param("gn_eps"), scale=1.0 / HD)\
                    .then_inc(sem("gn_ln"), 1)
            for m in range(4):
                act.wait_ge(*nth("gn_ln", m + 1))
                nc.scalar.activation(gn_work[m], gn_work[m], ACT.Exp, scale=-0.5).then_inc(sem("gn_rstd"), 1)

            norm_ahead("conv", "ffn_norm", "conv_x_ready")
            nc.scalar.preload_act_table(ACT.Silu)
            with act.Fori(0, KF) as p:
                act.wait_ge(*nth("conv_pair_read", p + 1))
                nc.scalar.activation(sq[:, 0, :], tmp[:, 1, :], ACT.Silu).then_inc(sem("conv_silu"), 1)

        @block.vector
        def _(dve):
            def pre_norm(tag, gain, ready, src=xT, k0=0, n=KD, done=0):
                dve.wait_ge(*nth(tag + "_in_rstd", 1))
                def rest(k):
                    dve.wait_ge(*nth(tag + "_h_hi", k + 1))
                    nc.vector.tensor_tensor(h_lo[:, k0 + k, :], tmp[:, k % 2, :], h_hi[:, k0 + k, :].bitcast(F32),
                                            ALU.subtract).then_inc(sem(ready), 1)
                for k in range(n):
                    if k >= 2 or done:
                        dve.wait_ge(*nth(ready, done + k - 1))
                    nc.vector.scalar_tensor_tensor(tmp[:, k % 2, :], src[:, k0 + k, :], param(gain, k), rstd[:, :],
                                                   ALU.mult, ALU.mult).then_inc(sem(tag + "_h32"), 1)
                    if k:
                        rest(k - 1)
                rest(n - 1)

            def low_part(tag, gain, k, src=xT, k0=0, ready=None):
                dve.wait_ge(*nth(tag + "_h_hi", k + 1))
                nc.vector.scalar_tensor_tensor(h_lo[:, k0 + k, :], src[:, k0 + k, :], param(gain, k),
                                               h_hi[:, k0 + k, :].bitcast(F32), ALU.mult, ALU.subtract)\
                    .then_inc(sem(ready or tag + "_h_ready"), 1)

            def ffn_up(tag):
                dve.wait_ge(*nth(tag + "_in_rstd", 1))
                def body(i, first):
                    for u in range(2):
                        p = 2 * i + u
                        dve.wait_ge(*nth("w_used", FIRST[tag + "_up"] + 4 * i + 2 * u + 1))
                        nc.vector.tensor_tensor(tmp[:, u, :], bank[2 * u][:, :], rstd[:, :], ALU.mult)\
                            .then_inc(sem(tag + "_gate_scaled"), 1)
                        dve.wait_ge(*nth(tag + "_silu", p + 1))
                        nc.vector.tensor_tensor(tmp[:, u, :], tmp[:, u, :], rstd[:, :], ALU.mult)\
                            .then_inc(sem(tag + "_silu_scaled"), 1)
                        dve.wait_ge(*nth(tag + "_silu_scaled", p + 1))
                        dve.wait_ge(*nth("w_used", FIRST[tag + "_up"] + 4 * i + 2 * u + 2))
                        hi, lo = (a[:, bass.ds(p, 1), :].rearrange("q a t -> q (a t)") for a in (a_hi, a_lo))
                        nc.vector.tensor_tensor(hi, tmp[:, u, :], bank[2 * u + 1][:, :], ALU.mult)\
                            .then_inc(sem(tag + "_a32"), 1)
                        nc.vector.tensor_tensor(sq[:, u, :], tmp[:, u, :], bank[2 * u + 1][:, :], ALU.mult)\
                            .then_inc(sem(tag + "_pair_read"), 1)
                        dve.wait_ge(*nth(tag + "_a32", p + 1))
                        dve.wait_ge(*nth(tag + "_pair_read", p + 1))
                        nc.vector.tensor_tensor(lo, sq[:, u, :], hi.bitcast(F32), ALU.subtract)\
                            .then_inc(sem(tag + "_a_ready"), 1)
                with dve.Fori(0, KF // 2) as i:
                    body(i, False)

            def sum_out(tag):
                nc.vector.memset(acc[:, :], 0.0).then_inc(sem(tag + "_acc_zero"), 1)
                dve.wait_ge(*nth(tag + "_acc_zero", 1))
                for m in range(KD):
                    dve.wait_ge(*nth(tag + "_sq", m + 1))
                    if m:
                        dve.wait_ge(*nth(tag + "_acc", m))
                    nc.vector.tensor_tensor(acc[:, :], acc[:, :], sq[:, m % 2, :], ALU.add).then_inc(sem(tag + "_acc"), 1)

            def post_norm(tag, gain, factor, y, after=None):
                dve.wait_ge(*nth(tag + "_post_rstd", 1))
                dve.wait_ge(*nth(tag + "_y_read", KD))
                for k in range(KD):
                    nc.vector.scalar_tensor_tensor(tmp[:, k % 2, :], y[:, k, :], param(gain, k), rstd[:, :],
                                                   ALU.mult, ALU.mult).then_inc(sem(tag + "_scaled"), 1)
                    dve.wait_ge(*nth(tag + "_scaled", k + 1))
                    nc.vector.scalar_tensor_tensor(xT[:, k, :], tmp[:, k % 2, :], factor, xT[:, k, :],
                                                   ALU.mult, ALU.add).then_inc(sem(tag + "_x_ready"), 1)
                    if after and k:
                        after(k - 1)
                if after:
                    after(KD - 1)

            dve.wait_ge(*nth("params_in", 16))
            for k in range(KD):
                dve.wait_ge(*nth("x_turned", k + 1))
                nc.vector.tensor_copy(xT[:, k, :], bank[k][:, :]).then_inc(sem("start_x_ready"), 1)
                if k:
                    low_part("ffn1", "ffn1_pre", k - 1)
            low_part("ffn1", "ffn1_pre", KD - 1)
            sinks = prm[:, COL["sinks"]:COL["sinks"] + NH]
            nc.vector.tensor_scalar(sinks, sinks, -1.0, None, ALU.mult).then_inc(sem("sinks_step"), 1)
            dve.wait_ge(*nth("sinks_step", 1))
            ffn_up("ffn1")
            sum_out("ffn1")
            post_norm("ffn1", "ffn1_post", 0.5, yT, after=lambda k: low_part("mix", "mix_pre", k))

            TURN = (6.28125, 0.0019350051879882812, 3.0199159819e-7)
            step = [0]

            def link(ins):
                step[0] += 1
                ins.then_inc(sem("angle_step"), 1)
                dve.wait_ge(*nth("angle_step", step[0]))

            a0, a1, a2 = (ang[:, i, :] for i in range(3))
            dve.wait_ge(*nth("positions_in", 16))
            link(nc.vector.tensor_copy(a0, pos[:, :]))
            link(nc.vector.tensor_scalar(a0, a0, param("inv_freq"), None, ALU.mult))
            link(nc.vector.tensor_scalar(a1, a0, 1.0 / (2.0 * math.pi), ROUND, ALU.mult, ALU.add))
            link(nc.vector.tensor_scalar(a1, a1, -ROUND, None, ALU.add))
            for part in TURN:
                link(nc.vector.scalar_tensor_tensor(a0, a1, -part, a0, ALU.mult, ALU.add))
            link(nc.vector.tensor_scalar(a0, a0, PI_BELOW, -PI_BELOW, ALU.min, ALU.max))
            link(nc.vector.tensor_scalar(a2, a0, -1.0, None, ALU.mult))
            link(nc.vector.tensor_tensor(a2, a2, a0, ALU.max))
            dve.wait_ge(*nth("sine", 2))
            dve.wait_ge(*nth("mix_in_rstd", 1))
            nc.vector.scalar_tensor_tensor(sin_t[:, :], sin_t[:, :], param("rot_sign"), rstd[:, :], ALU.mult, ALU.mult)\
                .then_inc(sem("sine_step"), 1)
            nc.vector.tensor_tensor(cos_t[:, :], cos_t[:, :], rstd[:, :], ALU.mult).then_inc(sem("sine_step"), 1)
            dve.wait_ge(*nth("z_read", 2))
            nc.vector.tensor_tensor(z[:, 1, :], z[:, 1, :], rstd[:, :], ALU.mult).then_inc(sem("v_scaled"), 1)
            dve.wait_ge(*nth("sine_step", 2))
            for i in range(6):
                dve.wait_ge(*nth("rot_done", i + 1))
                if i < 2:
                    b, r, to, factor = bank[2 * i][:, :], bank[2 * i + 1][:, :], k_rot[:, i, :], 1.0
                else:
                    b, to, factor = z[:, i, :], q_rot[:, i - 2, :], -0.125
                    r = bank[(i - 2) % 2 if i < 4 else i - 2][:, :]
                if i:
                    dve.wait_ge(*nth("rot_used", i))
                nc.vector.scalar_tensor_tensor(tmp[:, 0, :], b, factor, cos_t[:, :], ALU.mult, ALU.mult)\
                    .then_inc(sem("rot_step"), 1)
                nc.vector.scalar_tensor_tensor(tmp[:, 1, :], r, factor, sin_t[:, :], ALU.mult, ALU.mult)\
                    .then_inc(sem("rot_step"), 1)
                dve.wait_ge(*nth("rot_step", 2 * i + 2))
                nc.vector.tensor_tensor(to, tmp[:, 0, :], tmp[:, 1, :], ALU.add).then_inc(sem("rot_used"), 1)

            nc.vector.memset(win[:, :, 0:PAD], 0.0).then_inc(sem("win_step"), 1)
            dve.wait_ge(*nth("win_step", 1))
            dve.wait_ge(*nth("mix_const_in", 16))
            adds = [1]

            def pool_link(ins):
                adds[0] += 1
                ins.then_inc(sem("win_step"), 1)
                dve.wait_ge(*nth("win_step", adds[0]))

            def pool_difference(g):
                dve.wait_ge(*nth("z_read", 7 + g))
                if g >= 2:
                    dve.wait_ge(*nth("pool_product", g - 1))
                dif, u = dif_of[g % 2], z[:, 6 + g, :]
                pool_link(nc.vector.tensor_tensor(u, u, rstd[:, :], ALU.mult))
                pool_link(nc.vector.tensor_copy(win[:, 0, PAD:], u))
                src = 0
                for j in range(g + 1):
                    k = 1 << j
                    pool_link(nc.vector.tensor_tensor(win[:, 1 - src, PAD:], win[:, src, PAD:],
                                                      win[:, src, PAD - k:PAD + S - k], ALU.add))
                    src = 1 - src
                pool_link(nc.vector.tensor_tensor(win[:, 1 - src, PAD:2 * PAD], win[:, src, PAD:2 * PAD],
                                                  inv_count[:, g, :], ALU.mult))
                pool_link(nc.vector.tensor_tensor(dif[:, 0:PAD], win[:, 1 - src, PAD:2 * PAD], u[:, 0:PAD],
                                                  ALU.subtract))
                nc.vector.scalar_tensor_tensor(dif[:, PAD:], win[:, src, 2 * PAD:], 1.0 / (2 << g), u[:, PAD:],
                                               ALU.mult, ALU.subtract).then_inc(sem("pool_diff"), 1)
                dve.wait_ge(*nth("pool_diff", g + 1))

            def pooled(g):
                dve.wait_ge(*nth("pool_product", g + 1))
                nc.vector.tensor_scalar(mixed[:, g, :], bank[7][:, :], param("pool_scale", g), None, ALU.mult)\
                    .then_inc(sem("pooled"), 1)

            units = [(n, g) for n in range(NT) for g in range(2)]

            def mask(n, g, unit):
                width = (2 if n else 1) * P
                dve.wait_ge(*nth("swa_scores", 2 * (unit + 1)))
                if unit >= 2:
                    dve.wait_ge(*nth("swa_turned", unit - 1))
                for h in range(4):
                    e, i = h % 2, h // 2
                    nc.vector.tensor_tensor_reduce(sc[:, unit % 2, h, 0:width],
                                                   bank[2 * (unit % 2) + e][:, i * width:(i + 1) * width],
                                                   band[:, 2 * P - width:], 1.0, param("sinks", 4 * g + h),
                                                   ALU.add, ALU.min, small[:, unit % 2, 0, h:h + 1])\
                        .then_inc(sem("swa_masked"), 1)
                dve.wait_ge(*nth("swa_masked", 4 * (unit + 1)))
                c = COL["sinks"] + 4 * g
                nc.vector.tensor_tensor(small[:, unit % 2, 2, :], small[:, unit % 2, 0, :], prm[:, c:c + 4],
                                        ALU.subtract).then_inc(sem("swa_sink_arg"), 1)

            def normalise(n, g, unit):
                width = (2 if n else 1) * P
                sm = small[:, unit % 2, :, :]
                dve.wait_ge(*nth("swa_sink_exp", unit + 1))
                dve.wait_ge(*nth("swa_exp", 4 * (unit + 1)))
                nc.vector.tensor_tensor(sm[:, 3, :], sm[:, 1, :], sm[:, 2, :], ALU.add).then_inc(sem("swa_step"), 1)
                dve.wait_ge(*nth("swa_step", 2 * unit + 1))
                nc.vector.reciprocal(sm[:, 3, :], sm[:, 3, :]).then_inc(sem("swa_step"), 1)
                dve.wait_ge(*nth("swa_step", 2 * unit + 2))
                for h in range(4):
                    nc.vector.tensor_scalar(sc[:, unit % 2, h, 0:width], sc[:, unit % 2, h, 0:width],
                                            sm[:, 3, h:h + 1], None, ALU.mult).then_inc(sem("swa_probs"), 1)

            mask(*units[0], 0)
            for u, (n, g) in enumerate(units):
                normalise(n, g, u)
                if u + 1 < len(units):
                    mask(*units[u + 1], u + 1)
                if u >= 4:
                    pooled(u - 4)
                if u in (1, 2, 4, 5):
                    pool_difference({1: 0, 2: 1, 4: 2, 5: 3}[u])
            for k in range(4):
                low_part("attn", "g_attn", k, mixed, 4, "wout_h_ready")
            pre_norm("pool", "g_pool", "wout_h_ready", src=mixed, n=4, done=4)
            nc.vector.memset(acc[:, :], 0.0).then_inc(sem("wout_acc_zero"), 1)
            dve.wait_ge(*nth("wout_acc_zero", 1))
            dve.wait_ge(*nth("attn_in_rstd", 1))

            def add_square(m):
                dve.wait_ge(*nth("wout_sq", m + 1))
                if m:
                    dve.wait_ge(*nth("wout_acc", m))
                nc.vector.tensor_tensor(acc[:, :], acc[:, :], sq[:, m % 2, :], ALU.add).then_inc(sem("wout_acc"), 1)

            for m in range(KD):
                dve.wait_ge(*nth("w_used", FIRST["w_out"] + m + 1))
                if m >= 2:
                    dve.wait_ge(*nth("wout_y_read", m - 1))
                nc.vector.tensor_tensor(tmp[:, m % 2, :], bank[4 + m % 4][:, :], rstd[:, :], ALU.mult)\
                    .then_inc(sem("wout_half"), 1)
                dve.wait_ge(*nth("wout_half", m + 1))
                nc.vector.tensor_tensor(mixed[:, m, :], tmp[:, m % 2, :], bank[m % 4][:, :], ALU.add)\
                    .then_inc(sem("wout_y_read"), 1)
                if m:
                    add_square(m - 1)
            add_square(KD - 1)
            post_norm("wout", "mix_post", 1.0, mixed, after=lambda k: low_part("ffn2", "ffn2_pre", k))

            ffn_up("ffn2")
            sum_out("ffn2")
            post_norm("ffn2", "ffn2_post", 0.5, yT)

            pre_norm("nsa", "attn_norm", "nsa_h_ready")
            dve.wait_ge(*nth("nsa_small_in", 8 * 16))
            nc.vector.memset(rel[32:33, :], 1.0).then_inc(sem("rel_one"), 1)
            job = [0]

            def job_bank():
                job[0] += 1
                dve.wait_ge(*nth("nsa_job", job[0]))
                return bank[2 + (job[0] - 1) % 2]

            for v in range(2):
                nc.vector.tensor_copy(v2_tok[:, v, :, :].rearrange("p n c -> p (n c)"), job_bank()[:, :])\
                    .then_inc(sem("nsa_read"), 1)
            for v in range(2):
                for g in range(2):
                    b = job_bank()[:, :].rearrange("p (t o) -> p o t", o=2)
                    for o in range(2):
                        last = nc.vector.tensor_copy(pair[64 * o:64 * o + 64, v, g, :], b[64 * o:64 * o + 64, o, :])
                    last.then_inc(sem("nsa_read"), 1)
            for a, b in ((0, S), (S, 5 * P)):
                nc.vector.tensor_copy(rv[:, a:b], job_bank()[0:NH, 0:b - a]).then_inc(sem("nsa_read"), 1)
            nc.vector.tensor_copy(gate_tok[:, :, :].rearrange("p n c -> p (n c)"), job_bank()[:, 0:NT * 24])\
                .then_inc(sem("nsa_read"), 1)
            for v in range(2):
                dve.wait_ge(*nth("nsa_read", 6))
                for half in range(2):
                    at = slice(8 * half, 8 * half + 8)
                    nc.vector.tensor_tensor(
                        cmp_blocks[v][:, at, :, :],
                        pair[:, v, :, :].rearrange("p g (b j) -> p j g b", j=8)[:, :, :, half:half + NCMP],
                        pe_in[:, v, at].unsqueeze(2).unsqueeze(3).to_broadcast([P, 8, 2, NCMP]), ALU.add)\
                        .then_inc(sem("blocks_ready"), 1)
            for i in range(2):
                dve.wait_ge(*nth("head_rstd", i + 1))
                nc.vector.tensor_tensor(zn[:, i, :], zn[:, i, :], tmp[:, i, :], ALU.mult)\
                    .then_inc(sem("head_rstd_used"), 1)
            for i in range(2, 6):
                dve.wait_ge(*nth("head_rstd", i + 1))
                nc.vector.scalar_tensor_tensor(reverse(qn[:, i - 2, :]), by_tile(zn[:, i + 4, :]), param("q_norm"),
                                               by_tile(tmp[:, i % 2, :]),
                                               ALU.mult, ALU.mult).then_inc(sem("head_rstd_used"), 1)
            for c in range(4):
                nc.vector.tensor_scalar(kd[:, c, :], job_bank()[:, :], param("k_norm"), -HD ** -0.5, ALU.mult,
                                        ALU.mult).then_inc(sem("nsa_read"), 1)
            chain = [0]

            def link(ins):
                chain[0] += 1
                ins.then_inc(sem("cmp_step"), 1)
                dve.wait_ge(*nth("cmp_step", chain[0]))

            for v in range(2):
                w = 2 * NCMP
                b = job_bank()[:, 0:2 * 64].rearrange("p (h c) -> p h c", h=2)
                nc.vector.tensor_copy(hid[:, :, 0:w], b[:, :, 0:w]).then_inc(sem("nsa_read"), 1)
                dve.wait_ge(*nth("nsa_read", job[0]))
                x, t = hid[:, :, 0:w], hid2[:, :, 0:w]
                link(nc.vector.tensor_tensor(t, x, x, ALU.mult))
                link(nc.vector.scalar_tensor_tensor(t, t, 0.044715, x, ALU.mult, ALU.mult))
                nc.vector.tensor_tensor(t, t, x, ALU.add).then_inc(sem("gelu_arg"), 1)
                dve.wait_ge(*nth("gelu_tanh", v + 1))
                link(nc.vector.scalar_tensor_tensor(t, t, 1.0, x, ALU.add, ALU.mult))
                nc.vector.tensor_scalar(x, t, 0.5, None, ALU.mult).then_inc(sem("gelu"), 1)
                dve.wait_ge(*nth("gelu", v + 1))
                if v == 0:
                    nc.vector.tensor_copy(kcn[:, :], job_bank()[:, 0:w]).then_inc(sem("nsa_read"), 1)
                    dve.wait_ge(*nth("head_rstd", 7))
                    link(nc.vector.tensor_tensor(kcn[:, :], kcn[:, :], tmp[:, 0, 0:w], ALU.mult))
                    nc.vector.tensor_scalar(kcn[:, :], kcn[:, :], param("k_norm"), -HD ** -0.5, ALU.mult, ALU.mult)\
                        .then_inc(sem("kc_normed"), 1)
                else:
                    nc.vector.tensor_copy(vct[:, :, :].rearrange("n g d -> n (g d)"), job_bank()[0:NCMP, 0:2 * HD])\
                        .then_inc(sem("nsa_read"), 1)
            dve.wait_ge(*nth("toeplitz_in", 16))

            def nsa_mask(n, g, unit):
                if unit >= 2:
                    dve.wait_ge(*nth("nsa_out_read", unit - 1))
                for i in range(10):
                    b = bank[i % 4] if unit % 2 == 0 else bank[(i + 2) % 4]
                    dve.wait_ge(*nth("nsa_scores", 10 * unit + i + 1))
                    if i < 8:
                        nc.vector.tensor_tensor_reduce(E[:, unit % 2, i, 0:(n + 1) * P], b[:, 0:(n + 1) * P],
                                                       toeplitz[:, 4 * g + i % 4, (3 - n) * P:], 1.0, 3.0e38,
                                                       ALU.add, ALU.min, stat[:, unit % 2, 0, 4 + i:5 + i])\
                            .then_inc(sem("nsa_masked"), 1)
                    else:
                        c0 = 31 + (3 - n) * P
                        for k in range(2):
                            h = 2 * k + i - 8
                            last = nc.vector.tensor_tensor_reduce(
                                Ec[:, unit % 2, h, 0:8 * n + 7], b[:, k * 32:k * 32 + 8 * n + 7],
                                toeplitz[:, 4 * g + h, c0:c0 + 16 * (8 * n + 6) + 1:16], 1.0, 3.0e38,
                                ALU.add, ALU.min, stat[:, unit % 2, 0, h:h + 1])
                        last.then_inc(sem("nsa_masked"), 1)

            wstep = [0]

            def nsa_weights(n, g, unit):
                def link(ins):
                    wstep[0] += 1
                    ins.then_inc(sem("nsa_weight_step"), 1)
                    dve.wait_ge(*nth("nsa_weight_step", wstep[0]))
                st = stat[:, unit % 2, :, :]
                dve.wait_ge(*nth("nsa_exp", 12 * (unit + 1)))
                link(nc.vector.reciprocal(st[:, 2, :], st[:, 1, :]))
                gates = gate_tok[:, n, 12 * g:12 * g + 12].rearrange("p (h b) -> p b h", b=3)
                link(nc.vector.tensor_tensor(st[:, 2, :].rearrange("p (b h) -> p b h", b=3),
                                             st[:, 2, :].rearrange("p (b h) -> p b h", b=3), gates, ALU.mult))
                if n == 0:
                    link(nc.vector.tensor_scalar(st[:, 2, 0:4], st[:, 2, 0:4], param("sees_block"), None, ALU.mult))
                for h in range(4):
                    s = Ec[:, unit % 2, h, 0:8 * n + 7]
                    nc.vector.tensor_scalar(s, s, st[:, 2, h:h + 1], None, ALU.mult)
                for i in range(8):
                    s = E[:, unit % 2, i, 0:(n + 1) * P]
                    last = nc.vector.tensor_scalar(s, s, st[:, 2, 4 + i:5 + i], None, ALU.mult)
                last.then_inc(sem("nsa_weighed"), 1)

            nsa_mask(*units[0], 0)
            for u, (n, g) in enumerate(units):
                nsa_weights(n, g, u)
                if u + 1 < len(units):
                    nsa_mask(*units[u + 1], u + 1)

            dve.wait_ge(*nth("rwkv_small_in", 4 * 16))
            steps = [0]

            def link(ins):
                steps[0] += 1
                ins.then_inc(sem("rw_step"), 1)
                dve.wait_ge(*nth("rw_step", steps[0]))

            def mix(j):
                for i, (a, _) in enumerate(RW_GROUPS):
                    if j == a:
                        dve.wait_ge(*nth(f"pin_in{i}", 16))
                if j:
                    dve.wait_ge(*nth("mixed_in", j))
                c = RW_ORDER[j]
                x, d = pin[:, c, :], tmp[:, 1, :]
                nc.vector.tensor_scalar(d[:, 0:1], x[:, 0:1], -1.0, None, ALU.mult)
                link(nc.vector.tensor_tensor(d[:, 1:], x[:, 0:S - 1], x[:, 1:], ALU.subtract))
                nc.vector.scalar_tensor_tensor(x, d, param("mu", c), x, ALU.mult, ALU.add)\
                    .then_inc(sem("mixed_in"), 1)

            def rw_prepare(m, step):
                r_, k_, v_ = pin[:, m, :], pin[:, 4 + m, :], pin[:, 8 + m, :]
                KK, MOD, AR = pair_sets[m % 2][:3]
                if step == 1:
                    dve.wait_ge(*nth("mixed_in", 3 * m + 5))
                    nc.vector.tensor_scalar(KK[:, :], k_, param("k_k", m), None, ALU.mult).then_inc(sem("kk"), 1)
                elif step == 2:
                    dve.wait_ge(*nth("lora_read", m + 1))
                    link(nc.vector.tensor_tensor_scan(CUM[:, :], reset[:, :], SG[:, :], 0.0, ALU.mult, ALU.add))
                    nc.vector.tensor_tensor(PREV[:, :], CUM[:, :], SG[:, :], ALU.subtract)\
                        .then_inc(sem("cumulative"), 1)
                    link(nc.vector.tensor_scalar(MOD[:, :], RATE[:, :], 1.0, param("k_a", m), ALU.subtract,
                                                 ALU.mult))
                    link(nc.vector.scalar_tensor_tensor(MOD[:, :], MOD[:, :], 1.0, k_, ALU.add, ALU.mult))
                    nc.vector.scalar_tensor_tensor(sq[:, 1, :], r_, param("r_k", m), MOD[:, :], ALU.mult, ALU.mult)\
                        .then_inc(sem("rk_product"), 1)
                elif step == 4:
                    dve.wait_ge(*nth("rw_head_sum", 2 * m + 2))
                    nc.vector.tensor_scalar(tmp[:, 0, :], bank[3][:, :], 1e-24, None, ALU.max)\
                        .then_inc(sem("kk_sum"), 1)
                    nc.vector.tensor_tensor(bonus[:, m, :], bank[7][:, :], v_, ALU.mult)\
                        .then_inc(sem("bonus_done"), 1)
                elif step == 6:
                    dve.wait_ge(*nth("decays", 3 * (m + 1)))
                    dve.wait_ge(*nth("kk_rstd", m + 1))
                    link(nc.vector.tensor_tensor(KK[:, :], KK[:, :], tmp[:, 0, :], ALU.mult))
                    link(nc.vector.scalar_tensor_tensor(AR[:, :, 0, :], by_tile(KK[:, :]), -1.0, by_tile(PREV[:, :]),
                                                        ALU.mult, ALU.mult))
                    nc.vector.tensor_tensor(AR[:, :, 1, :], by_tile(r_), by_tile(UPTO[:, :]), ALU.mult)\
                        .then_inc(sem("hats"), 1)
                    link(nc.vector.tensor_tensor(KK[:, :], KK[:, :], RATE[:, :], ALU.mult))
                    nc.vector.tensor_tensor(KK[:, :], KK[:, :], INV[:, :], ALU.mult).then_inc(sem("hats"), 1)
                    nc.vector.tensor_tensor(MOD[:, :], MOD[:, :], INV[:, :], ALU.mult).then_inc(sem("hats"), 1)
                    nc.vector.tensor_copy(PC[:, m, :], UPTO[:, C - 1::C]).then_inc(sem("hats"), 1)
                    dve.wait_ge(*nth("hats", 4 * (m + 1)))

            for j in range(14):
                mix(j)
                if j in PREPARE_AT:
                    rw_prepare(0, PREPARE_AT[j])
            wide = lambda b: b[:, :].rearrange("p (u t) -> p u t", u=4)
            eye = ident.unsqueeze(1).to_broadcast([P, 4, P])
            dve.wait_ge(*nth("mixed_in", 14))
            dve.wait_ge(*nth("fill_late", 16 * LATE))
            for m in range(4):
                AR = pair_sets[m % 2][2]
                for half in range(2):
                    for u in range(4):
                        dve.wait_ge(*nth("rw_scores", 8 * m + 4 * half + u + 1))
                        link(nc.vector.tensor_tensor(mats[:, half, u, :], bank[u if half else 4 + u][:, :],
                                                     mask4[:, :], ALU.mult))
                    nc.vector.tensor_tensor(OT[:, half, :, :], mats[:, half, :, 0:P],
                                            level[0].unsqueeze(1).to_broadcast([P, 4, P]), ALU.mult)\
                        .then_inc(sem("level_start"), 1)
                    dve.wait_ge(*nth("level_start", 2 * m + half + 1))
                    nc.vector.tensor_tensor(DT[:, half, :, :], OT[:, half, :, :], eye, ALU.add)\
                        .then_inc(sem("dt_ready"), 1)
                for half in range(2):
                    dve.wait_ge(*nth("level_turned", 2 * m + half + 1))
                    dve.wait_ge(*nth("dt_ready", 12 * m + half + 1))
                    nc.vector.tensor_tensor(Dm[:, half, :, :], wide(bank[0 if half else 4]), eye, ALU.add)\
                        .then_inc(sem("d_ready"), 1)
                if m < 3:
                    rw_prepare(m + 1, 1)
                for k in range(1, 6):
                    if k < 5:
                        for half in range(2):
                            dve.wait_ge(*nth("level_d", 8 * m + 2 * (k - 1) + half + 1))
                            dve.wait_ge(*nth("d_ready", 10 * m + 2 * (k - 1) + half + 1))
                            nc.vector.tensor_tensor(Dm[:, half, :, :], Dm[:, half, :, :],
                                                    wide(bank[1 if half else 5]), ALU.add)\
                                .then_inc(sem("d_ready"), 1)
                    for half in range(2):
                        dve.wait_ge(*nth("level_dt", 10 * m + 2 * (k - 1) + half + 1))
                        dve.wait_ge(*nth("dt_ready", 12 * m + 2 * (k - 1) + half + 1))
                        nc.vector.tensor_tensor(DT[:, half, :, :], DT[:, half, :, :], wide(bank[2 if half else 6]),
                                                ALU.add).then_inc(sem("dt_ready"), 1)
                    if m < 3:
                        rw_prepare(m + 1, k + 1)
                for half in range(2):
                    dve.wait_ge(*nth("chunk_terms", 2 * m + half + 1))
                    at = slice(half * 2 * P, (half + 1) * 2 * P)
                    qy = bank[2 if half else 6]
                    pair_of = lambda x: x.rearrange("p (n t) -> p n t", n=2)
                    nc.vector.tensor_tensor(pair_of(pin[:, m, at]), pair_of(qy[:, 0:2 * P]),
                                            AR[:, 2 * half:2 * half + 2, 1, :], ALU.add)
                    nc.vector.tensor_copy(yl[:, m, at], qy[:, 2 * P:])
                    for c in range(2):
                        mn = bank[c if half else 4 + c]
                        to = pin[:, 4 + m, at].rearrange("p (n c t) -> p c n t", n=2, c=2)[:, c, :, :]
                        nc.vector.tensor_tensor(to, pair_of(mn[:, 0:P]), eye2.unsqueeze(1).to_broadcast([P, 2, HD]),
                                                ALU.add)
                        to = pin[:, 8 + m, at].rearrange("p (n c t) -> p c n t", n=2, c=2)[:, c, :, :]
                        last = nc.vector.tensor_copy(to, pair_of(mn[:, P:2 * P]))
                    last.then_inc(sem("chunk_terms_read"), 1)
                dve.wait_ge(*nth("chunk_terms_read", 2 * m + 2))
            dve.wait_ge(*nth("rw_head_sum", 8))
            for c in range(NCH):
                at = slice(c * C, (c + 1) * C)
                if c < NCH - 1:
                    for e in range(2):
                        rows = slice(64 * e, 64 * e + 64)
                        to, n_ = state[rows, (c + 1) % 2, :, :], pin[rows, 8:12, at]
                        if c:
                            dve.wait_ge(*nth("state_product", 2 * (c - 1) + e + 1))
                            if c > 1:
                                dve.wait_ge(*nth("walk_y", 2 * (c - 1)))
                            link(nc.vector.tensor_tensor(to, bank[2 + e][rows, 0:4 * HD]
                                                         .rearrange("p (m i) -> p m i", m=4), n_, ALU.add))
                            n_ = to
                        nc.vector.tensor_tensor(to, n_, PC[rows, :, c:c + 1].to_broadcast([64, 4, HD]), ALU.mult)\
                            .then_inc(sem("state"), 1)
                if c:
                    for e in range(2):
                        rows = slice(64 * e, 64 * e + 64)
                        dve.wait_ge(*nth("walk_y", 2 * (c - 1) + e + 1))
                        y = yl[rows, :, at]
                        nc.vector.tensor_tensor(y, y, bank[e][rows, 0:4 * HD].rearrange("p (m i) -> p m i", m=4),
                                                ALU.add).then_inc(sem("walk_read"), 1)
            dve.wait_ge(*nth("walk_read", 2 * (NCH - 1)))
            for m in range(4):
                dve.wait_ge(*nth("gn_sum", m + 1))
                y = yl[:, m, :]
                nc.vector.scalar_tensor_tensor(y, bank[m][:, :], -1.0 / HD, y, ALU.mult, ALU.add)\
                    .then_inc(sem("gn_centred"), 1)
            for m in range(4):
                y = yl[:, m, :]
                dve.wait_ge(*nth("gn_rstd", m + 1))
                link(nc.vector.scalar_tensor_tensor(y, y, param("ln_g", m), gn_work[m], ALU.mult, ALU.mult))
                link(nc.vector.scalar_tensor_tensor(y, y, param("ln_b", m), bonus[:, m, :], ALU.add, ALU.add))
                dve.wait_ge(*nth("gn_gate", m + 1))
                nc.vector.tensor_tensor(o_hi[:, 4 + m, :], y, bank[4 + m][:, :], ALU.mult)
                nc.vector.tensor_tensor(y, y, bank[4 + m][:, :], ALU.mult).then_inc(sem("gn_out"), 1)

            dve.wait_ge(*nth("merge_gate", 4))
            for m in range(KD):
                dve.wait_ge(*nth("w_used", FIRST["merge"] + m + 1))
                b = 2 * (m % 4)
                if m:
                    dve.wait_ge(*nth("m_ready", m))
                for j in range(2):
                    link(nc.vector.tensor_tensor(sq[:, j, :], gates[:, KD * j + m, :], bank[b + j][:, :], ALU.mult))
                nc.vector.tensor_tensor(m_hi[:, m, :], sq[:, 0, :], sq[:, 1, :], ALU.add).then_inc(sem("gates_used"), 1)
                dve.wait_ge(*nth("gates_used", m + 1))
                link(nc.vector.tensor_tensor(sq[:, 0, :], sq[:, 0, :], sq[:, 1, :], ALU.add))
                nc.vector.tensor_tensor(m_lo[:, m, :], sq[:, 0, :], m_hi[:, m, :].bitcast(F32), ALU.subtract)\
                    .then_inc(sem("m_ready"), 1)
            dve.wait_ge(*nth("x_back", 16))
            for m in range(KD):
                dve.wait_ge(*nth("w_used", FIRST["w_out_2"] + m + 1))
                nc.vector.tensor_tensor(xT[:, m, :], xT[:, m, :], bank[4 + m % 4][:, :], ALU.add)\
                    .then_inc(sem("conv_x_ready"), 1)
                if m:
                    low_part("conv", "ffn_norm", m - 1)
            low_part("conv", "ffn_norm", KD - 1)

            dve.wait_ge(*nth("conv_in_rstd", 1))

            def conv_pair(i, first):
                for u in range(2):
                    p = 2 * i + u
                    for v in range(2):
                        dve.wait_ge(*nth("w_used", FIRST["conv_up"] + 4 * i + 2 * u + v + 1))
                        b, c = bank[2 * u + v], tmp[:, v, :]
                        if v == 1 and not (first and u == 0):
                            dve.wait_ge(*nth("conv_silu", p))
                        w = [prm[:, bass.ds(p + (COL[f"conv_{x}"] + KF * v), 1)] for x in ("w0", "w1", "w2", "b")]
                        if v == 1:
                            dve.wait_ge(*nth("conv_value", p + 1))
                        elif not (first and u == 0):
                            dve.wait_ge(*nth("conv_pair_read", p))
                        nc.vector.tensor_tensor(acc[:, :], b[:, :], rstd[:, :], ALU.mult)\
                            .then_inc(sem("conv_step"), 1)
                        dve.wait_ge(*nth("conv_step", 6 * p + 3 * v + 1))
                        nc.vector.tensor_scalar(c, acc[:, :], w[2], w[3], ALU.mult, ALU.add)\
                            .then_inc(sem("conv_step"), 1)
                        dve.wait_ge(*nth("conv_step", 6 * p + 3 * v + 2))
                        nc.vector.scalar_tensor_tensor(c[:, 1:], acc[:, 0:S - 1], w[1], c[:, 1:], ALU.mult, ALU.add)\
                            .then_inc(sem("conv_step"), 1)
                        dve.wait_ge(*nth("conv_step", 6 * p + 3 * v + 3))
                        last = nc.vector.scalar_tensor_tensor(c[:, 2:], acc[:, 0:S - 2], w[0], c[:, 2:], ALU.mult,
                                                              ALU.add)
                        last.then_inc(sem("conv_pair_read" if v else "conv_value"), 1)
                    hi, lo = (a[:, bass.ds(p, 1), :].rearrange("q a t -> q (a t)") for a in (a_hi, a_lo))
                    dve.wait_ge(*nth("conv_value", p + 1))
                    dve.wait_ge(*nth("conv_silu", p + 1))
                    nc.vector.tensor_tensor(hi, tmp[:, 0, :], sq[:, 0, :], ALU.mult).then_inc(sem("conv_a32"), 1)
                    nc.vector.tensor_tensor(sq[:, 1, :], tmp[:, 0, :], sq[:, 0, :], ALU.mult)\
                        .then_inc(sem("conv_a32"), 1)
                    dve.wait_ge(*nth("conv_a32", 2 * p + 2))
                    nc.vector.tensor_tensor(lo, sq[:, 1, :], hi.bitcast(F32), ALU.subtract)\
                        .then_inc(sem("conv_a_ready"), 1)
            conv_pair(0, True)
            with dve.Fori(1, KF // 2) as i:
                conv_pair(i, False)
            for m in range(KD):
                dve.wait_ge(*nth("w_used", FIRST["conv_down"] + 3 * (m + 1)))
                nc.vector.tensor_tensor(xT[:, m, :], xT[:, m, :], bank[4 + m % 4][:, :], ALU.add)\
                    .then_inc(sem("end_x_ready"), 1)
            for i in range(2 * NT):
                dve.wait_ge(*nth("out_turned", i + 1))
                nc.vector.tensor_copy(yT[:, i, :], bank[i][:, :]).then_inc(sem("out_copied"), 1)


def _layouts(inputs):
    import numpy as np
    f32 = np.float32

    def blocks(w):
        k, n = w.shape
        return w.reshape(k // P, P, n // P, P).transpose(2, 1, 0, 3).reshape(n // P, P, k)

    def pairs(w):
        b = blocks(w)
        return np.stack([b[:KF], b[KF:]], 1).reshape(2 * KF, P, D)

    def columns(v):
        return v.reshape(-1, P).T

    one = {name: (a[0] if a.shape[0] == 1 and name not in ("x", "positions") else a) for name, a in inputs.items()}
    cols = lambda name: columns(one[name].reshape(-1))
    conv_w = one["conv_w_2"]
    ch = np.arange(P)
    rope_of = ch % HD
    freq = 500000.0 ** (-(np.arange(0, 16, 2, dtype=f32)) / f32(16))
    values = {
        "ffn1_pre": cols("ffn1_pre"), "ffn1_post": cols("ffn1_post"), "mix_pre": cols("mix_pre"),
        "mix_post": cols("mix_post"), "ffn2_pre": cols("ffn2_pre"), "ffn2_post": cols("ffn2_post"),
        "attn_norm": cols("attn_norm_g_2"), "ffn_norm": cols("ffn_norm_g_2"), "pool_scale": cols("pool_scale"),
        "g_pool": cols("g_pool"), "g_attn": cols("g_attn"), "sinks": np.tile(one["sinks"], (P, 1)),
        "eps": np.full((P, 1), EPS), "half_pi": np.full((P, 1), math.pi / 2),
        "inv_freq": np.where(rope_of < 16, freq.astype(f32)[rope_of % 8], 0)[:, None],
        "rot_sign": np.where(rope_of < 8, -1, 1)[:, None],
        "q_norm": np.tile(one["q_norm_g_2"], 2)[:, None], "k_norm": np.tile(one["k_norm_g_2"], 2)[:, None],
        "sees_block": (P - 1 - ch >= 31)[:, None], "mu": cols("rwkv_mu_2"), "w0": cols("rwkv_w0_2"), "a0": cols("rwkv_a0_2"),
        "k_k": cols("rwkv_k_k_2"), "k_a": cols("rwkv_k_a_2"), "r_k": cols("rwkv_r_k_2"), "ln_g": cols("rwkv_ln_g_2"),
        "ln_b": cols("rwkv_ln_b_2"), "gn_eps": np.full((P, 1), 64e-5), "ln_256": np.full((P, 1), 8 * math.log(2)),
        "conv_b": cols("conv_b_2"), "conv_w0": columns(conv_w[0]), "conv_w1": columns(conv_w[1]),
        "conv_w2": columns(conv_w[2])}
    params = np.concatenate([values[name].astype(f32) for name, _ in PARAMS], 1)

    def takes(from_of):
        a = np.zeros((P, P), f32)
        a[from_of(ch), ch] = 1
        return a

    def rotated(c):
        d = c % HD
        return np.where(d < 8, c + 8, np.where(d < 16, c - 8, c))
    dup = [takes(lambda c, g=g: HD * g + c % HD) for g in range(2)]
    dup_rot = [takes(lambda c, g=g: HD * g + rotated(c % HD)) for g in range(2)]
    diff = ch[:, None] + P - np.arange(2 * P)[None]
    band = np.where((diff >= 0) & (diff < P), 0, 1e30).astype(f32)
    first = np.arange(16) + 1
    inv_count = np.stack([1 / np.minimum(first, w) for w in (2, 4, 8, 16)]).astype(f32).reshape(1, 64).repeat(P, 0)
    mix_const = np.concatenate([takes(rotated)] + dup + dup_rot + [band, inv_count], 1)

    dist = S - 1 - np.arange(5 * P)
    n = np.maximum(dist, 0)
    ratio = np.log(np.maximum(n, 1).astype(f32) / f32(16)) / f32(math.log(128 / 16))
    bucket = np.where(n < 16, n, np.minimum(16 + (ratio * f32(16)).astype(np.int32), 31))
    code = np.zeros((33, 5 * P), f32)
    code[bucket, np.arange(5 * P)] = -1
    code[:, dist < 0] = 0
    code[32, dist < 0] = 1e30
    head_ones = np.kron(np.eye(2), np.ones((HD, HD))).astype(f32)

    s, t = ch[:, None], ch[None]
    before, upto = (s // C == t // C) & (s < t), (s // C == t // C) & (s <= t)
    levels = [(s >> (k + 1) == t >> (k + 1)) & ((s >> k) % 2 == 0) & ((t >> k) % 2 == 1) for k in range(6)]
    reset = np.tile(np.arange(S) % C != 0, (P, 1))
    rwkv_const = np.concatenate([before, upto, before, upto, reset] + levels
                                + [head_ones, np.tile(np.eye(HD), (2, 1))], 1).astype(f32)

    w2 = one["w_in_2"]
    part = lambda a, b: blocks(w2[:, a:b])
    merge = np.concatenate([blocks(one["w_proj_a_2"]), blocks(one["w_proj_b_2"])], 2)
    pe = [one[n].reshape(16, P).T for n in ("cmp_pe_k_2", "cmp_pe_v_2")]
    return dict(
        x=inputs["x"], positions=inputs["positions"], params=params,
        const=np.concatenate([np.eye(P), np.ones((P, P))], 1).astype(f32), mix_const=mix_const,
        w_pool=one["w_pool"], w_ffn1_gu=pairs(one["ffn1_w_gu"]), w_ffn1_down=blocks(one["ffn1_w_down"]),
        w_in=blocks(one["w_in"])[[8, 9, 4, 5, 6, 7, 0, 1, 2, 3]], w_out=blocks(one["w_out"]),
        w_ffn2_gu=pairs(one["ffn2_w_gu"]), w_ffn2_down=blocks(one["ffn2_w_down"]),
        w_nsa=np.concatenate([part(768, 896), part(1024, 1152), part(896, 1024), part(1152, 1280), part(512, 640),
                              part(640, 768), part(0, 512), part(1280, 1408)]),
        nsa_const=np.concatenate(dup + [head_ones, np.eye(P)[::-1]], 1).astype(f32), rel_bias=inputs["rel_bias_2"], distance_code=code,
        cmp_pe=np.stack(pe), cmp_w1=np.stack([one["cmp_w1_k_2"], one["cmp_w1_v_2"]]),
        cmp_w2=np.stack([one["cmp_w2_k_2"], one["cmp_w2_v_2"]]), w_rwkv=part(1304, 3096)[list(RW_ORDER)], rwkv_const=rwkv_const,
        rwkv_w2a2=np.concatenate([one["rwkv_w2_2"], one["rwkv_a2_2"]]), rwkv_g2=one["rwkv_g2_2"],
        w_gates=part(3096, 5144),
        w_merge=merge, w_out_2=blocks(one["w_out_2"]), w_conv_up=pairs(one["w_up_2"]),
        w_conv_down=blocks(one["w_down_2"]))


def kernel(**inputs):
    import numpy as _np
    import concourse.bacc as _bacc
    from concourse import mybir as _mybir
    from concourse.bass_utils import run_bass_kernel_spmd as _run

    nc = _bacc.Bacc("TRN2", target_bir_lowering=False, num_devices=1)
    laid_out = _layouts({name: _np.asarray(a) for name, a in inputs.items()})
    arrays, args = {}, {}
    for name, a in laid_out.items():
        a = _np.ascontiguousarray(a)
        arrays[f"{name}_dram"] = a
        args[name] = nc.dram_tensor(f"{name}_dram", a.shape, _mybir.dt.from_np(a.dtype), kind="ExternalInput").ap()
    out = nc.dram_tensor("out_dram", (1, S, D), F32, kind="ExternalOutput").ap()
    build(nc, out=out, **args)
    r = _run(nc, [arrays], core_ids=[0])
    return r.results[0]["out_dram"]
```
